# Optimizing a Trainium2 kernel written in Bass

```python
import math
import jax
import jax.numpy as jnp
from jax import lax
import numpy as np
import jax, jax.numpy as jnp

D_MODEL = 1024
BATCH = 1
SEQ = 256
DEPTH = 2

CHUNK = 64
Q_BLOCK = 128
HEAD_DIM = 64
ROPE_DIM = HEAD_DIM // 4
ROPE_THETA = 500000.0
RMS_EPS = 1e-6
A_HEADS = D_MODEL // (2 * HEAD_DIM)
A_WIDTH = A_HEADS * HEAD_DIM
B_HEADS = D_MODEL // (4 * HEAD_DIM)
B_QK_WIDTH = B_HEADS * 2 * HEAD_DIM
B_VDIM = 2 * HEAD_DIM
B_WIDTH = B_HEADS * B_VDIM
C_WIDTH = D_MODEL // 2
CONV_W = 3
D_HEADS = D_MODEL // (2 * HEAD_DIM)
D_WIDTH = D_HEADS * HEAD_DIM
D_LEFT_CHUNKS = 8
D_BAND = (D_LEFT_CHUNKS + 1) * CHUNK
REL_CLIP = 128
X_HEADS = 4
X_HEAD_DIM = D_MODEL // X_HEADS
N_MEM = 256
D_FF = 2816
N_EVEN = (DEPTH + 1) // 2
N_ODD = DEPTH // 2
EVEN_SIZES = (A_WIDTH, A_WIDTH, A_WIDTH, A_HEADS, B_QK_WIDTH, B_QK_WIDTH, B_WIDTH)
ODD_SIZES = (C_WIDTH, C_WIDTH, C_WIDTH, D_WIDTH, D_WIDTH, D_WIDTH)
EVEN_IN = 3 * A_WIDTH + A_HEADS + 2 * B_QK_WIDTH + B_WIDTH
ODD_IN = 3 * C_WIDTH + 3 * D_WIDTH
EVEN_MIX = A_WIDTH + B_WIDTH
ODD_MIX = C_WIDTH + D_WIDTH
MAX_POS_OFFSET = 65536


def rms_norm(x, g):
    xf = x.astype(jnp.float32)
    y = xf * lax.rsqrt(jnp.mean(xf * xf, axis=-1, keepdims=True) + RMS_EPS)
    return (y * g.astype(jnp.float32)).astype(x.dtype)

def split_cols(y, sizes):
    out, start = [], 0
    for s in sizes:
        out.append(y[..., start:start + s])
        start += s
    return out

def rope_tables(positions):
    inv = ROPE_THETA ** (-jnp.arange(0, ROPE_DIM, 2, dtype=jnp.float32) / ROPE_DIM)
    ang = positions.astype(jnp.float32)[..., None] * inv
    return jnp.cos(ang), jnp.sin(ang)

def apply_partial_rope(x, cos, sin):
    half = ROPE_DIM // 2
    bshape = cos.shape[:2] + (1,) * (x.ndim - 3) + (half,)
    c, s = cos.reshape(bshape), sin.reshape(bshape)
    xr = x[..., :ROPE_DIM].astype(jnp.float32)
    x1, x2 = xr[..., :half], xr[..., half:]
    rot = jnp.concatenate([x1 * c - x2 * s, x2 * c + x1 * s], axis=-1).astype(x.dtype)
    return jnp.concatenate([rot, x[..., ROPE_DIM:]], axis=-1)

def swiglu(h, w_in, w_out):
    g, u = split_cols(h @ w_in, (D_FF, D_FF))
    return (jax.nn.silu(g) * u) @ w_out

def forgetting_attention(q, k, v, cum_logf):
    seq = q.shape[1]
    scale = q.shape[-1] ** -0.5
    outs = []
    for qs in range(0, seq, Q_BLOCK):
        qe = qs + Q_BLOCK
        s = jnp.einsum('bqhd,bkhd->bhqk', q[:, qs:qe], k[:, :qe],
                       preferred_element_type=jnp.float32) * scale
        s = s + cum_logf[:, :, qs:qe, None] - cum_logf[:, :, None, :qe]
        causal = jnp.arange(qs, qe)[:, None] >= jnp.arange(qe)[None, :]
        p = jax.nn.softmax(jnp.where(causal, s, -jnp.inf), axis=-1).astype(v.dtype)
        outs.append(jnp.einsum('bhqk,bkhd->bqhd', p, v[:, :qe]))
    return jnp.concatenate(outs, axis=1)

def differential_attention(q, k, v, lam):
    seq = q.shape[1]
    scale = q.shape[-1] ** -0.5
    outs = []
    for qs in range(0, seq, Q_BLOCK):
        qe = qs + Q_BLOCK
        s = jnp.einsum('bqhjd,bkhjd->bhjqk', q[:, qs:qe], k[:, :qe],
                       preferred_element_type=jnp.float32) * scale
        allowed = (jnp.arange(qs, qe)[:, None] // CHUNK) >= (jnp.arange(qe)[None, :] // CHUNK)
        p = jax.nn.softmax(jnp.where(allowed, s, -jnp.inf), axis=-1)
        p = (p[:, :, 0] - lam * p[:, :, 1]).astype(v.dtype)
        outs.append(jnp.einsum('bhqk,bkhe->bqhe', p, v[:, :qe]))
    return jnp.concatenate(outs, axis=1)

def short_conv_mixer(gate_b, gate_c, h, conv_w):
    u = gate_c * h
    y = lax.conv_general_dilated(u, conv_w[:, None, :], window_strides=(1,),
                                 padding=[(CONV_W - 1, 0)],
                                 dimension_numbers=('NWC', 'WIO', 'NWC'),
                                 feature_group_count=u.shape[-1])
    return gate_b * y

def chunk_band_attention(q, k, v, rel_table):
    bsz, seq, heads, hd = q.shape
    n_chunks = seq // CHUNK
    left = D_LEFT_CHUNKS * CHUNK
    pad = ((0, 0), (left, 0), (0, 0), (0, 0))
    kp, vp = jnp.pad(k, pad), jnp.pad(v, pad)
    rel = jnp.arange(CHUNK)[:, None] - jnp.arange(D_BAND)[None, :] + left
    rel_idx = jnp.clip(rel, -REL_CLIP, REL_CLIP) + REL_CLIP
    bias = rel_table[:, rel_idx].astype(jnp.float32)
    scale = hd ** -0.5

    def one_chunk(c):
        start = c * CHUNK
        qc = lax.dynamic_slice_in_dim(q, start, CHUNK, axis=1)
        kc = lax.dynamic_slice_in_dim(kp, start, D_BAND, axis=1)
        vc = lax.dynamic_slice_in_dim(vp, start, D_BAND, axis=1)
        s = jnp.einsum('bqhd,bkhd->bhqk', qc, kc, preferred_element_type=jnp.float32) * scale + bias
        valid = (start - left + jnp.arange(D_BAND)) >= 0
        p = jax.nn.softmax(jnp.where(valid, s, -jnp.inf), axis=-1).astype(v.dtype)
        return jnp.einsum('bhqk,bkhd->bqhd', p, vc)

    out = lax.map(one_chunk, jnp.arange(n_chunks))
    return out.transpose(1, 0, 2, 3, 4).reshape(bsz, seq, heads * hd)

def even_mixer(h, w_in, f_bias, qk_gains, lam_params, subln_gain, lambda_init, w_out, cos, sin):
    bsz, seq, _ = h.shape
    a_q, a_k, a_v, a_f, b_q, b_k, b_v = split_cols(h @ w_in, EVEN_SIZES)
    aq = rms_norm(a_q.reshape(bsz, seq, A_HEADS, HEAD_DIM), qk_gains[0])
    ak = rms_norm(a_k.reshape(bsz, seq, A_HEADS, HEAD_DIM), qk_gains[1])
    av = a_v.reshape(bsz, seq, A_HEADS, HEAD_DIM)
    logf = jax.nn.log_sigmoid((a_f + f_bias).astype(jnp.float32))
    cum_logf = jnp.cumsum(logf, axis=1).transpose(0, 2, 1)
    a_out = forgetting_attention(aq, ak, av, cum_logf).reshape(bsz, seq, A_WIDTH)
    bq = rms_norm(b_q.reshape(bsz, seq, B_HEADS, 2, HEAD_DIM), qk_gains[2])
    bk = rms_norm(b_k.reshape(bsz, seq, B_HEADS, 2, HEAD_DIM), qk_gains[3])
    bq, bk = apply_partial_rope(bq, cos, sin), apply_partial_rope(bk, cos, sin)
    bv = b_v.reshape(bsz, seq, B_HEADS, B_VDIM)
    lp = lam_params.astype(jnp.float32)
    lam = jnp.exp(jnp.sum(lp[0] * lp[1])) - jnp.exp(jnp.sum(lp[2] * lp[3])) + lambda_init
    b_out = differential_attention(bq, bk, bv, lam)
    b_out = (rms_norm(b_out, subln_gain) * (1.0 - lambda_init)).reshape(bsz, seq, B_WIDTH)
    return jnp.concatenate([a_out, b_out], axis=-1) @ w_out

def odd_mixer(h, w_in, conv_w, qk_gains, rel_table, w_out):
    bsz, seq, _ = h.shape
    c_b, c_c, c_h, d_q, d_k, d_v = split_cols(h @ w_in, ODD_SIZES)
    c_out = short_conv_mixer(c_b, c_c, c_h, conv_w)
    dq = rms_norm(d_q.reshape(bsz, seq, D_HEADS, HEAD_DIM), qk_gains[0])
    dk = rms_norm(d_k.reshape(bsz, seq, D_HEADS, HEAD_DIM), qk_gains[1])
    dv = d_v.reshape(bsz, seq, D_HEADS, HEAD_DIM)
    d_out = chunk_band_attention(dq, dk, dv, rel_table)
    return jnp.concatenate([c_out, d_out], axis=-1) @ w_out

def memory_cross_attention(h, mem_n, w_q, w_kv, qk_gains, w_o):
    bsz, seq, _ = h.shape
    q = rms_norm((h @ w_q).reshape(bsz, seq, X_HEADS, X_HEAD_DIM), qk_gains[0])
    k, v = split_cols(mem_n @ w_kv, (D_MODEL, D_MODEL))
    k = rms_norm(k.reshape(bsz, -1, X_HEADS, X_HEAD_DIM), qk_gains[1])
    v = v.reshape(bsz, -1, X_HEADS, X_HEAD_DIM)
    s = jnp.einsum('bqhd,bkhd->bhqk', q, k, preferred_element_type=jnp.float32) * X_HEAD_DIM ** -0.5
    p = jax.nn.softmax(s, axis=-1).astype(v.dtype)
    o = jnp.einsum('bhqk,bkhd->bqhd', p, v).reshape(bsz, seq, D_MODEL)
    return o @ w_o

def first_inputs(seed: int = 0) -> dict:
    key = jax.random.key(seed)
    ks = jax.random.split(key, 24)
    f32 = jnp.float32

    def dense(k, shape):
        return jax.random.normal(k, shape, f32) * shape[-2] ** -0.5

    def gain(k, shape):
        return 1.0 + 0.05 * jax.random.normal(k, shape, f32)

    x = jax.random.normal(ks[0], (BATCH, SEQ, D_MODEL), f32)
    mem = jax.random.normal(ks[1], (BATCH, N_MEM, D_MODEL), f32)
    offset = jax.random.randint(ks[2], (BATCH, 1), 0, MAX_POS_OFFSET, dtype=jnp.int32)
    positions = offset + jnp.arange(SEQ, dtype=jnp.int32)[None, :]
    return {
        'x': x,
        'mem': mem,
        'positions': positions,
        'ln_gains': gain(ks[3], (DEPTH, 5, D_MODEL)),
        'ffn1_w_in': dense(ks[4], (DEPTH, D_MODEL, 2 * D_FF)),
        'ffn1_w_out': dense(ks[5], (DEPTH, D_FF, D_MODEL)),
        'ffn2_w_in': dense(ks[6], (DEPTH, D_MODEL, 2 * D_FF)),
        'ffn2_w_out': dense(ks[7], (DEPTH, D_FF, D_MODEL)),
        'even_w_in': dense(ks[8], (N_EVEN, D_MODEL, EVEN_IN)),
        'even_f_bias': jax.random.uniform(ks[9], (N_EVEN, A_HEADS), f32, 1.0, 5.0),
        'even_qk_gains': gain(ks[10], (N_EVEN, 4, HEAD_DIM)),
        'even_lambda': 0.1 * jax.random.normal(ks[11], (N_EVEN, 4, HEAD_DIM), f32),
        'even_subln_gain': gain(ks[12], (N_EVEN, B_VDIM)),
        'even_w_out': dense(ks[13], (N_EVEN, EVEN_MIX, D_MODEL)),
        'odd_w_in': dense(ks[14], (N_ODD, D_MODEL, ODD_IN)),
        'odd_conv_w': jax.random.normal(ks[15], (N_ODD, CONV_W, C_WIDTH), f32) * CONV_W ** -0.5,
        'odd_qk_gains': gain(ks[16], (N_ODD, 2, HEAD_DIM)),
        'odd_rel_bias': 0.5 * jax.random.normal(ks[17], (N_ODD, D_HEADS, 2 * REL_CLIP + 1), f32),
        'odd_w_out': dense(ks[18], (N_ODD, ODD_MIX, D_MODEL)),
        'x_w_q': dense(ks[19], (DEPTH, D_MODEL, D_MODEL)),
        'x_w_kv': dense(ks[20], (DEPTH, D_MODEL, 2 * D_MODEL)),
        'x_qk_gains': gain(ks[21], (DEPTH, 2, X_HEAD_DIM)),
        'x_w_o': dense(ks[22], (DEPTH, D_MODEL, D_MODEL)),
    }

def first_block(x, mem, positions, ln_gains, ffn1_w_in, ffn1_w_out, ffn2_w_in, ffn2_w_out,
              even_w_in, even_f_bias, even_qk_gains, even_lambda, even_subln_gain, even_w_out,
              odd_w_in, odd_conv_w, odd_qk_gains, odd_rel_bias, odd_w_out,
              x_w_q, x_w_kv, x_qk_gains, x_w_o):
    cos, sin = rope_tables(positions)
    for layer in range(DEPTH):
        g = ln_gains[layer]
        x = x + 0.5 * swiglu(rms_norm(x, g[0]), ffn1_w_in[layer], ffn1_w_out[layer])
        h = rms_norm(x, g[1])
        if layer % 2 == 0:
            e = layer // 2
            lambda_init = 0.8 - 0.6 * math.exp(-0.3 * layer)
            mixed = even_mixer(h, even_w_in[e], even_f_bias[e], even_qk_gains[e], even_lambda[e],
                               even_subln_gain[e], lambda_init, even_w_out[e], cos, sin)
        else:
            o = layer // 2
            mixed = odd_mixer(h, odd_w_in[o], odd_conv_w[o], odd_qk_gains[o], odd_rel_bias[o],
                              odd_w_out[o])
        x = x + mixed
        x = x + memory_cross_attention(rms_norm(x, g[2]), rms_norm(mem, g[3]), x_w_q[layer],
                                       x_w_kv[layer], x_qk_gains[layer], x_w_o[layer])
        x = x + 0.5 * swiglu(rms_norm(x, g[4]), ffn2_w_in[layer], ffn2_w_out[layer])
    return x


DEPTH_2 = 1

ATTN_SCALE = HEAD_DIM ** -0.5
SWA_HEADS = 8
SWA_KV_HEADS = 2
SWA_WINDOW = 128
SWA_Q = SWA_HEADS * HEAD_DIM
SWA_KV = SWA_KV_HEADS * HEAD_DIM
SSM_WIDTH = 512
SSM_GROUP = 16
SSM_GROUPS = SSM_WIDTH // SSM_GROUP
SSM_STATE = 64
DT_MIN = 0.001
DT_MAX = 0.1
MOBA_HEADS = 8
MOBA_KV_HEADS = 2
MOBA_BLOCK = 256
MOBA_TOPK = 3
MOBA_Q_CHUNK = 64
MOBA_Q = MOBA_HEADS * HEAD_DIM
MOBA_KV = MOBA_KV_HEADS * HEAD_DIM
N_BRANCH = 3
D_FF_2 = 4 * D_MODEL
NORM_EPS = 1e-6
ALIBI_MAX_BIAS = 8.0
IN_SIZES = (SWA_Q, SWA_KV, SWA_KV, SSM_WIDTH, MOBA_Q, MOBA_KV, MOBA_KV, N_BRANCH * D_MODEL)
D_IN = sum(IN_SIZES)


def rms_norm_2(x, gain):
    xf = x.astype(jnp.float32)
    y = xf * lax.rsqrt(jnp.mean(xf * xf, axis=-1, keepdims=True) + NORM_EPS)
    return (y * gain.astype(jnp.float32)).astype(x.dtype)

def alibi_slopes():
    n = SWA_HEADS + MOBA_HEADS
    return jnp.asarray(2.0 ** (-ALIBI_MAX_BIAS * np.arange(1, n + 1) / n), jnp.float32)

def split_in(proj):
    outs, start = [], 0
    for size in IN_SIZES:
        outs.append(proj[..., start:start + size])
        start += size
    return outs

def swa_attention(q, k, v, sinks, slopes):
    B, S, Hq, d = q.shape
    Hkv = k.shape[2]
    G = Hq // Hkv
    W = SWA_WINDOW
    nb = S // W
    qb = q.reshape(B, nb, W, Hkv, G, d)
    kp = jnp.pad(k, ((0, 0), (W, 0), (0, 0), (0, 0))).reshape(B, nb + 1, W, Hkv, d)
    vp = jnp.pad(v, ((0, 0), (W, 0), (0, 0), (0, 0))).reshape(B, nb + 1, W, Hkv, d)
    kb = jnp.concatenate([kp[:, :-1], kp[:, 1:]], axis=2)
    vb = jnp.concatenate([vp[:, :-1], vp[:, 1:]], axis=2)
    s = jnp.einsum('bnqhgd,bnkhd->bnhgqk', qb, kb).astype(jnp.float32) * ATTN_SCALE
    t_rel = jnp.arange(W)[:, None]
    s_rel = jnp.arange(2 * W)[None, :] - W
    dist = t_rel - s_rel
    band = (dist >= 0) & (dist < W)
    mask = band[None] & ((jnp.arange(nb)[:, None, None] * W + s_rel[None]) >= 0)
    bias = -slopes.reshape(Hkv, G)[:, :, None, None] * dist.astype(jnp.float32)[None, None]
    s = jnp.where(mask[None, :, None, None], s + bias[None, None], -jnp.inf)
    sink = jnp.broadcast_to(sinks.astype(jnp.float32).reshape(Hkv, G)[None, None, :, :, None, None],
                            s.shape[:-1] + (1,))
    p = jax.nn.softmax(jnp.concatenate([s, sink], axis=-1), axis=-1)[..., :-1].astype(v.dtype)
    o = jnp.einsum('bnhgqk,bnkhd->bnqhgd', p, vb)
    return o.reshape(B, S, Hq * d)

def moba_attention(q, k, v, slopes):
    B, S, Hq, d = q.shape
    Hkv = k.shape[2]
    G = Hq // Hkv
    L = MOBA_BLOCK
    Qc = MOBA_Q_CHUNK
    Sp = -(-S // L) * L
    nblk = Sp // L
    topk = min(MOBA_TOPK, nblk)
    pad = ((0, 0), (0, Sp - S), (0, 0), (0, 0))
    q, k, v = jnp.pad(q, pad), jnp.pad(k, pad), jnp.pad(v, pad)
    k_blocks = jnp.repeat(k, G, axis=2).transpose(0, 2, 1, 3).reshape(B, Hq, nblk, L, d)
    v_blocks = jnp.repeat(v, G, axis=2).transpose(0, 2, 1, 3).reshape(B, Hq, nblk, L, d)
    k_mean = jnp.mean(k_blocks.astype(jnp.float32), axis=3)
    nq = Sp // Qc
    q_chunks = q.transpose(0, 2, 1, 3).reshape(B, Hq, nq, Qc, d).transpose(2, 0, 1, 3, 4)
    b_idx = jnp.arange(B)[:, None, None, None]
    h_idx = jnp.arange(Hq)[None, :, None, None]
    blk_ids = jnp.arange(nblk)
    rank_ids = jnp.arange(topk)
    offs = jnp.arange(L)

    def one_chunk(args):
        qi, ci = args
        t = ci * Qc + jnp.arange(Qc)
        j = (ci * Qc) // L
        gate = jnp.einsum('bhqd,bhnd->bhqn', qi.astype(jnp.float32), k_mean)
        gate = jnp.where(blk_ids < j, gate, -jnp.inf)
        _, sel = lax.top_k(gate, topk)
        valid = rank_ids < j
        k_sel = k_blocks[b_idx, h_idx, sel]
        v_sel = v_blocks[b_idx, h_idx, sel]
        s_sel = jnp.einsum('bhqd,bhqrkd->bhqrk', qi, k_sel).astype(jnp.float32) * ATTN_SCALE
        dist_sel = (t[None, None, :, None, None] - (sel[..., None] * L + offs)).astype(jnp.float32)
        s_sel = s_sel - slopes[None, :, None, None, None] * dist_sel
        s_sel = jnp.where(valid[None, None, None, :, None], s_sel, -jnp.inf)
        k_own = lax.dynamic_slice_in_dim(k_blocks, j, 1, axis=2)[:, :, 0]
        v_own = lax.dynamic_slice_in_dim(v_blocks, j, 1, axis=2)[:, :, 0]
        s_own = jnp.einsum('bhqd,bhkd->bhqk', qi, k_own).astype(jnp.float32) * ATTN_SCALE
        dist_own = t[:, None] - (j * L + offs)[None, :]
        s_own = s_own - slopes[None, :, None, None] * dist_own.astype(jnp.float32)[None, None]
        s_own = jnp.where((dist_own >= 0)[None, None], s_own, -jnp.inf)
        logits = jnp.concatenate([s_sel.reshape(B, Hq, Qc, topk * L), s_own], axis=-1)
        p = jax.nn.softmax(logits, axis=-1).astype(v_blocks.dtype)
        p_sel = p[..., :topk * L].reshape(B, Hq, Qc, topk, L)
        o = (jnp.einsum('bhqrk,bhqrkd->bhqd', p_sel, v_sel)
             + jnp.einsum('bhqk,bhkd->bhqd', p[..., topk * L:], v_own))
        return o

    o = lax.map(one_chunk, (q_chunks, jnp.arange(nq)))
    o = o.transpose(1, 0, 3, 2, 4).reshape(B, Sp, Hq * d)
    return o[:, :S]

def s5_ssm(u, lam_re, lam_im, log_step, b_re, b_im, c_re, c_im, d_skip):
    Bsz, S, _ = u.shape
    f32 = jnp.float32
    uf = u.astype(f32).reshape(Bsz, S, SSM_GROUPS, SSM_GROUP)
    lr, li = lam_re.astype(f32), lam_im.astype(f32)
    dt = jnp.exp(log_step.astype(f32))[:, None]
    mag = jnp.exp(lr * dt)
    ab_re, ab_im = mag * jnp.cos(li * dt), mag * jnp.sin(li * dt)
    den = lr * lr + li * li
    nr, ni = ab_re - 1.0, ab_im
    f_re, f_im = (nr * lr + ni * li) / den, (ni * lr - nr * li) / den
    br, bi = b_re.astype(f32), b_im.astype(f32)
    bb_re = f_re[..., None] * br - f_im[..., None] * bi
    bb_im = f_re[..., None] * bi + f_im[..., None] * br
    x_re = jnp.einsum('bsgh,gph->bsgp', uf, bb_re)
    x_im = jnp.einsum('bsgh,gph->bsgp', uf, bb_im)
    a_re = jnp.broadcast_to(ab_re, x_re.shape)
    a_im = jnp.broadcast_to(ab_im, x_im.shape)

    def combine(e1, e2):
        a1r, a1i, b1r, b1i = e1
        a2r, a2i, b2r, b2i = e2
        return (a2r * a1r - a2i * a1i, a2r * a1i + a2i * a1r,
                a2r * b1r - a2i * b1i + b2r, a2r * b1i + a2i * b1r + b2i)

    _, _, h_re, h_im = lax.associative_scan(combine, (a_re, a_im, x_re, x_im), axis=1)
    y = (jnp.einsum('bsgp,ghp->bsgh', h_re, c_re.astype(f32))
         - jnp.einsum('bsgp,ghp->bsgh', h_im, c_im.astype(f32))
         + d_skip.astype(f32).reshape(SSM_GROUPS, SSM_GROUP) * uf)
    return y.reshape(Bsz, S, SSM_WIDTH)

def second_inputs(seed: int = 0) -> dict:
    key = jax.random.key(seed)
    ks = jax.random.split(key, 24)
    f32 = jnp.float32
    nrm = lambda k, shape, scale: jax.random.normal(k, shape, f32) * scale
    x = jax.random.normal(ks[0], (BATCH, SEQ, D_MODEL), f32)
    norm_mix = 1.0 + nrm(ks[1], (DEPTH_2, D_MODEL), 0.02)
    w_in = nrm(ks[2], (DEPTH_2, D_MODEL, D_IN), D_MODEL ** -0.5)
    sinks = nrm(ks[3], (DEPTH_2, SWA_HEADS), 0.5)
    lam_re = -0.5 + nrm(ks[4], (DEPTH_2, SSM_GROUPS, SSM_STATE), 0.01)
    lam_im = (math.pi * jnp.arange(SSM_STATE, dtype=f32))[None, None, :] + nrm(ks[5], (DEPTH_2, SSM_GROUPS, SSM_STATE), 0.01)
    log_step = math.log(DT_MIN) + jax.random.uniform(ks[6], (DEPTH_2, SSM_GROUPS), f32) * (math.log(DT_MAX) - math.log(DT_MIN))
    b_re = nrm(ks[7], (DEPTH_2, SSM_GROUPS, SSM_STATE, SSM_GROUP), (2 * SSM_GROUP) ** -0.5)
    b_im = nrm(ks[8], (DEPTH_2, SSM_GROUPS, SSM_STATE, SSM_GROUP), (2 * SSM_GROUP) ** -0.5)
    c_re = nrm(ks[9], (DEPTH_2, SSM_GROUPS, SSM_GROUP, SSM_STATE), (2 * SSM_STATE) ** -0.5)
    c_im = nrm(ks[10], (DEPTH_2, SSM_GROUPS, SSM_GROUP, SSM_STATE), (2 * SSM_STATE) ** -0.5)
    d_skip = nrm(ks[11], (DEPTH_2, SSM_WIDTH), 1.0)
    w_glu = nrm(ks[12], (DEPTH_2, SSM_WIDTH, 2 * SSM_WIDTH), SSM_WIDTH ** -0.5)
    w_o_swa = nrm(ks[13], (DEPTH_2, SWA_Q, D_MODEL), SWA_Q ** -0.5)
    w_o_ssm = nrm(ks[14], (DEPTH_2, SSM_WIDTH, D_MODEL), SSM_WIDTH ** -0.5)
    w_o_moba = nrm(ks[15], (DEPTH_2, MOBA_Q, D_MODEL), MOBA_Q ** -0.5)
    w_out = nrm(ks[16], (DEPTH_2, D_MODEL, D_MODEL), D_MODEL ** -0.5)
    norm_ffn = 1.0 + nrm(ks[17], (DEPTH_2, D_MODEL), 0.02)
    w_ff1 = nrm(ks[18], (DEPTH_2, D_MODEL, D_FF_2), D_MODEL ** -0.5)
    w_ff2 = nrm(ks[19], (DEPTH_2, D_FF_2, D_MODEL), D_FF_2 ** -0.5)
    norm_final = 1.0 + nrm(ks[20], (D_MODEL,), 0.02)
    return {"x": x, "norm_mix": norm_mix, "w_in": w_in, "sinks": sinks,
            "lam_re": lam_re, "lam_im": lam_im, "log_step": log_step,
            "b_re": b_re, "b_im": b_im, "c_re": c_re, "c_im": c_im, "d_skip": d_skip,
            "w_glu": w_glu, "w_o_swa": w_o_swa, "w_o_ssm": w_o_ssm, "w_o_moba": w_o_moba,
            "w_out": w_out, "norm_ffn": norm_ffn, "w_ff1": w_ff1, "w_ff2": w_ff2,
            "norm_final": norm_final}

def second_block(x, norm_mix, w_in, sinks, lam_re, lam_im, log_step, b_re, b_im, c_re, c_im,
              d_skip, w_glu, w_o_swa, w_o_ssm, w_o_moba, w_out, norm_ffn, w_ff1, w_ff2,
              norm_final):
    B, S, _ = x.shape
    slopes = alibi_slopes()
    slopes_swa, slopes_moba = slopes[:SWA_HEADS], slopes[SWA_HEADS:]
    for l in range(DEPTH_2):
        h = rms_norm_2(x, norm_mix[l])
        qa, ka, va, u, qm, km, vm, gates = split_in(h @ w_in[l])
        oa = swa_attention(qa.reshape(B, S, SWA_HEADS, HEAD_DIM),
                           ka.reshape(B, S, SWA_KV_HEADS, HEAD_DIM),
                           va.reshape(B, S, SWA_KV_HEADS, HEAD_DIM), sinks[l], slopes_swa)
        ya = oa @ w_o_swa[l]
        ys = s5_ssm(u, lam_re[l], lam_im[l], log_step[l], b_re[l], b_im[l], c_re[l], c_im[l], d_skip[l])
        z = jax.nn.gelu(ys).astype(x.dtype) @ w_glu[l]
        yb = (z[..., :SSM_WIDTH] * jax.nn.sigmoid(z[..., SSM_WIDTH:])) @ w_o_ssm[l]
        om = moba_attention(qm.reshape(B, S, MOBA_HEADS, HEAD_DIM),
                            km.reshape(B, S, MOBA_KV_HEADS, HEAD_DIM),
                            vm.reshape(B, S, MOBA_KV_HEADS, HEAD_DIM), slopes_moba)
        yc = om @ w_o_moba[l]
        g = jax.nn.sigmoid(gates)
        mixed = (g[..., :D_MODEL] * ya + g[..., D_MODEL:2 * D_MODEL] * yb
                 + g[..., 2 * D_MODEL:] * yc)
        x = x + mixed @ w_out[l]
        h = rms_norm_2(x, norm_ffn[l])
        x = x + jnp.square(jax.nn.relu(h @ w_ff1[l])) @ w_ff2[l]
    return rms_norm_2(x, norm_final)


def setup_inputs(seed=0):
    out = dict(first_inputs(seed))
    for name, value in second_inputs(seed + 1).items():
        if name != "x":
            out[name + "_2"] = value
    return out


def reference(
    x, mem, positions, ln_gains, ffn1_w_in, ffn1_w_out, ffn2_w_in, ffn2_w_out, even_w_in,
    even_f_bias, even_qk_gains, even_lambda, even_subln_gain, even_w_out, odd_w_in, odd_conv_w,
    odd_qk_gains, odd_rel_bias, odd_w_out, x_w_q, x_w_kv, x_qk_gains, x_w_o, norm_mix_2, w_in_2,
    sinks_2, lam_re_2, lam_im_2, log_step_2, b_re_2, b_im_2, c_re_2, c_im_2, d_skip_2, w_glu_2,
    w_o_swa_2, w_o_ssm_2, w_o_moba_2, w_out_2, norm_ffn_2, w_ff1_2, w_ff2_2, norm_final_2,
):
    x = first_block(
        x, mem, positions, ln_gains, ffn1_w_in, ffn1_w_out, ffn2_w_in, ffn2_w_out, even_w_in,
        even_f_bias, even_qk_gains, even_lambda, even_subln_gain, even_w_out, odd_w_in,
        odd_conv_w, odd_qk_gains, odd_rel_bias, odd_w_out, x_w_q, x_w_kv, x_qk_gains, x_w_o,
    )
    return second_block(
        x, norm_mix_2, w_in_2, sinks_2, lam_re_2, lam_im_2, log_step_2, b_re_2, b_im_2, c_re_2,
        c_im_2, d_skip_2, w_glu_2, w_o_swa_2, w_o_ssm_2, w_o_moba_2, w_out_2, norm_ffn_2,
        w_ff1_2, w_ff2_2, norm_final_2,
    )


_drawn_inputs = setup_inputs


def setup_inputs(seed=0):
    import zlib

    import numpy as np

    out = dict(_drawn_inputs(seed))
    spreads = {}
    factors = {'odd_qk_gains': 8.0,
     'x_qk_gains': 5.368,
     'norm_mix_2': 8.0,
     'sinks_2': 40.457,
     'lam_re_2': 64.0,
     'lam_im_2': 52.568,
     'log_step_2': 60.296,
     'b_re_2': 64.0,
     'b_im_2': 64.0,
     'c_re_2': 64.0,
     'c_im_2': 64.0,
     'norm_ffn_2': 3.965,
     'norm_final_2': 7.986}
    for name, (base, spread) in spreads.items():
        noise = np.random.default_rng([zlib.crc32(name.encode()), seed]).standard_normal(out[name].shape)
        drawn = base * np.exp(spread * noise) if base else spread * noise
        out[name] = jnp.asarray(drawn.astype(out[name].dtype))
    for name, factor in factors.items():
        out[name] = (out[name] * factor).astype(out[name].dtype)
    return out
```

```python
import math
from contextlib import ExitStack

import numpy as np
import concourse.bass as bass
from concourse import mybir

F32 = mybir.dt.float32
I32 = mybir.dt.int32
ALU = mybir.AluOpType
ACT = mybir.ActivationFunctionType
AX = mybir.AxisListType.X
P = 128
NEG = -1.0e30
TWO_PI = 2.0 * math.pi
MAGIC = 12582912.0
ROPE_INV = [float.fromhex(v) for v in (
    "0x1.0000000000000p+0", "0x1.8d275e0000000p-3", "0x1.3411900000000p-5", "0x1.ddee9c0000000p-8",
    "0x1.72ba440000000p-10", "0x1.1f91f00000000p-12", "0x1.be21880000000p-15", "0x1.5a0f4e0000000p-17")]
NSLOT = 5
SLOTK = 4


def pieces_of_two_pi():
    out, rest = [], TWO_PI
    for k in range(4):
        if k == 3:
            out.append(float(np.float32(rest)))
            break
        m, e = math.frexp(rest)
        part = math.ldexp(math.floor(m * 4096.0), e - 12)
        out.append(part)
        rest -= part
    return out


CONST_N = 904 + 128


def build_consts():
    c = np.zeros((P, CONST_N), np.float32)
    i = np.arange(P)
    c[:, 0:128] = np.eye(P)
    c[:, 128:256] = (i[:, None] <= i[None, :])
    c[:, 256:384] = 1.0
    c[:, 512:640] = np.where(i[:, None] >= i[None, :], 0.0, NEG)
    c[:, 768:896] = np.where(i[:, None] // 64 >= i[None, :] // 64, 0.0, NEG)
    c[:, 896:904] = np.asarray(ROPE_INV, np.float32)
    c[:, 904:1032] = np.eye(P)[::-1]
    return c


def build_alibi():
    slopes = (2.0 ** (-8.0 * np.arange(1, 17) / 16)).astype(np.float32)
    dist = (128 + np.arange(P)[:, None] - np.arange(256)[None, :])
    df = dist.astype(np.float32)
    out = np.zeros((2, P, 8, 256), np.float32)
    for h in range(8):
        out[0, :, h] = np.where((dist >= 0) & (dist < 128), -slopes[h] * df, NEG)
        out[1, :, h] = np.where(dist >= 0, -slopes[8 + h] * df, NEG)
    return out


class Buf:

    def __init__(self, ap):
        self.ap = ap
        self.free = []

    def take(self):
        out, self.free = self.free, []
        return out

    def put(self, *toks):
        self.free += toks


class Rot:
    def __init__(self, aps):
        self.bufs = [Buf(a) for a in aps]
        self.n = 0

    def next(self):
        b = self.bufs[self.n % len(self.bufs)]
        self.n += 1
        return b


class Queue:

    def __init__(self, eng, sem):
        self.eng, self.sem, self.count, self.seen = eng, sem, 0, {}

    def wait(self, toks):
        for t in toks:
            if t is None:
                continue
            if isinstance(t, list):
                self.wait(t)
                continue
            sem, value = t
            if self.seen.get(id(sem), 0) < value:
                self.seen[id(sem)] = value
                self.eng.wait_ge(sem, value)

    def op(self, fn, after=(), inc=True):
        self.wait(after)
        ins = fn(self.eng)
        if not inc:
            return None
        self.count += 1
        ins.then_inc(self.sem, 1)
        return (self.sem, self.count)

    def last(self):
        return (self.sem, self.count) if self.count else None


def build(nc, D):
    ctx = ExitStack()
    with ctx:
        build_in(nc, D, ctx)


def build_in(nc, D, ctx):
    def sb(name, shape, dt=F32):
        return ctx.enter_context(nc.sbuf_tensor(name, shape, dt))

    def newsem(name):
        return ctx.enter_context(nc.semaphore(name))

    pe = Queue(nc.tensor, newsem("s_pe"))
    act = Queue(nc.scalar, newsem("s_act"))
    dve = Queue(nc.vector, newsem("s_dve"))
    pool = Queue(nc.gpsimd, newsem("s_pool"))
    sp = Queue(nc.sync, newsem("s_sp"))
    dsem = {}

    def dma(q, out, in_, name, after=()):
        if name not in dsem:
            dsem[name] = [newsem("d_" + name), 0]
        d = dsem[name]
        d[1] += 16
        q.wait(after)
        q.eng.dma_start(out, in_).then_inc(d[0], 16)
        return (d[0], d[1])

    def snapshot():
        return [q.last() for q in (pe, act, dve, pool)]

    ring = sb("ring", [P, NSLOT * SLOTK * 512])
    x = sb("x", [P, 2, 1024])
    hT = sb("hT", [P, 8, 256])
    R1 = sb("R1", [P, 8192])
    actT = R1[:, :].rearrange("p (k t) -> p k t", k=32)
    S_rot = Rot([R1[:, 512 * i:512 * i + 512] for i in range(4)])
    pT_rot = Rot([R1[:, 2048 + 512 * i:2560 + 512 * i] for i in range(4)])
    qT = R1[:, 4096:6144].rearrange("p (k t) -> p k t", k=8)
    kT = R1[:, 6144:8192].rearrange("p (k t) -> p k t", k=8)
    R2 = sb("R2", [P, 6144])
    mT = R2[:, 0:2048].rearrange("p (k t) -> p k t", k=8)
    xkT = R2[:, 2048:4096].rearrange("p (k t) -> p k t", k=8)
    xv = R2[:, 4096:6144].rearrange("p (t n) -> p t n", t=2)
    gates = R2[:, :].rearrange("p (t n) -> p t n", t=2)
    vsb = sb("vsb", [P, 2, 512])
    O = sb("O", [P, 2, 1024])
    oT = sb("oT", [P, 8, 256])
    M = sb("M", [P, 2, 1024])
    biasA = sb("biasA", [P, 8, 256])
    biasB = sb("biasB", [P, 8, 256])
    fs_rot = Rot([biasA[:, 2 * i:2 * i + 2, :].rearrange("p a b -> p (a b)") for i in range(4)])
    fa_rot = Rot([biasB[:, 2 * i:2 * i + 2, :].rearrange("p a b -> p (a b)") for i in range(4)])
    sqj_rot = Rot([sb(f"sqj{i}", [P, 512])[:, :] for i in range(2)])
    cst = sb("cst", [P, CONST_N])
    gcol = sb("gcol", [P, 112])
    rows = sb("rows", [112, P])
    st = sb("st", [P, 1700])
    evg = sb("evg", [P, 4, 64])
    odg = sb("odg", [P, 2, 64])
    xg = sb("xg", [P, 2, 256])
    sublng = sb("sublng", [P, 128])
    lamp = sb("lamp", [P, 4, 64])
    fbias = sb("fbias", [P, 8])
    sinkb = sb("sinkb", [P, 8])
    posr = sb("posr", [2, P], I32)
    posf = sb("posf", [2, P])
    ssr = sb("ssr", [16, 3, P])
    lsr = sb("lsr", [16, 2])
    rope = sb("rope", [P, 2, 2, 8])
    rtmp_rot = Rot([sb(f"rtmp{i}", [P, 4, 8, 8])[:, :, :, :] for i in range(2)])
    cumT = sb("cumT", [8, 2, 256])
    SM = sb("SM", [P, 8, 16])
    BT = sb("BT", [P, 2, 4, 128])
    CR = biasB[:, 0:4, :].rearrange("p (r a) n -> p r (a n)", r=2)
    BL = biasB[:, 0:4, :].rearrange("p a (b h) -> p (a b) h", h=32).rearrange("p (r j) h -> p r j h", r=2)
    CL = biasA[:, 0:4, :].rearrange("p a (b n) -> p (a b) n", n=128).rearrange("p (r j) n -> p r j n", r=2)
    pq = [sb(f"pq{i}", [P, 2, 4, 256]) for i in range(2)]
    ssm_t = R1[:, 0:1024].rearrange("p (a n) -> p a n", a=2)
    ssm_g = R1[:, 1024:2560].rearrange("p (a n) -> p a n", a=3)
    tabs = M[:, 0, :].rearrange("p (a j n) -> p a j n", a=2, j=4)
    uT = vsb[:, :, :].rearrange("p a n -> p (a n)").rearrange("p (k t) -> p k t", k=4)

    banks = [Buf(ctx.enter_context(nc.psum_tensor(f"b{i}", [P, 512], F32))) for i in range(8)]
    gpair = [(banks[0], banks[1]), (banks[2], banks[3])]
    gcount = [0]
    tb = [banks[4], banks[5], banks[6]]
    tcount = [0]
    ob = banks[7]

    def nextbank():
        tcount[0] += 1
        return tb[(tcount[0] - 1) % 3]

    stn = [0]

    def stat(n):
        stn[0] += n
        assert stn[0] <= 1700, stn
        return st[:, stn[0] - n:stn[0]]

    ident = cst[:, 0:128]
    tri = cst[:, 128:256]
    ones = cst[:, 256:384]
    maskc = cst[:, 384:640]
    maskb = cst[:, 640:896]
    inv8 = cst[:, 896:904]
    flip = cst[:, 904:1032]

    def sel(h, n):
        return cst[0:8, h:h + 1].to_broadcast([8, n])

    def v(d):
        return D[d]

    def bc_rows(ap1d, n):
        return bass.AP(ap1d.tensor, ap1d.offset, [[0, P], [1, n]])

    tx = [dma(sp, x[:, t, :], v("x").rearrange("b (t p) d -> t p (b d)", p=P)[t], f"x{t}") for t in range(2)]
    tcst = dma(sp, cst[:, :], v("consts"), "cst")
    trow = [dma(sp, rows[0:80, :], v("ln_gains").rearrange("l j (k p) -> (l j k) p", p=P), "rows"),
            dma(sp, rows[80:88, :], v("norm_mix_2").rearrange("l (k p) -> (l k) p", p=P), "rows"),
            dma(sp, rows[88:96, :], v("norm_ffn_2").rearrange("l (k p) -> (l k) p", p=P), "rows"),
            dma(sp, rows[96:108, :], v("odd_conv_w").rearrange("o w (k p) -> (o w k) p", p=P), "rows"),
            dma(sp, rows[108:112, :], v("d_skip_2").rearrange("l (k p) -> (l k) p", p=P), "rows")][-1]
    tsm = [dma(pool, evg[:, :, :].rearrange("p a b -> p (a b)"), bc_rows(v("even_qk_gains"), 256), "sm"),
           dma(pool, odg[:, :, :].rearrange("p a b -> p (a b)"), bc_rows(v("odd_qk_gains"), 128), "sm"),
           dma(pool, sublng[:, :], bc_rows(v("even_subln_gain"), 128), "sm"),
           dma(pool, lamp[:, :, :].rearrange("p a b -> p (a b)"), bc_rows(v("even_lambda"), 256), "sm"),
           dma(pool, fbias[:, :], bc_rows(v("even_f_bias"), 8), "sm"),
           dma(pool, sinkb[:, :], bc_rows(v("sinks_2"), 8), "sm"),
           dma(pool, posr[:, :], v("positions").rearrange("b (t p) -> (b t) p", p=P), "sm"),
           dma(pool, ssr[:, 0, :], v("lam_re_2").rearrange("l (j a) p -> (l j) (a p)", a=2), "sm"),
           dma(pool, ssr[:, 1, :], v("lam_im_2").rearrange("l (j a) p -> (l j) (a p)", a=2), "sm"),
           dma(pool, lsr[:, :], v("log_step_2").rearrange("l (j a) -> (l j) a", a=2), "sm")][-1]
    tz = pool.op(lambda e: e.memset(BL[:, :, :, :], 0.0))
    for ri, nm in enumerate(("b_re_2", "b_im_2")):
        src = v(nm).rearrange("l (j a) p h -> a p (l j) h", a=2)
        for a in range(2):
            tbl = dma(pool, BL[64 * a:64 * a + 64, ri, :, 16 * a:16 * a + 16], src[a], "bl", [tz])
    slots = [Buf(ring[:, i * SLOTK * 512:(i + 1) * SLOTK * 512].rearrange("p (k n) -> p k n", k=SLOTK))
             for i in range(NSLOT)]
    scount = [0]

    def load_chunk(W, kt0, nk, pieces):
        i = scount[0] % NSLOT
        scount[0] += 1
        s = slots[i]
        after = s.take()
        off = 0
        for c0, w in pieces:
            tok = dma(sp, s.ap[:, 0:nk, off:off + w],
                      W[kt0 * P:(kt0 + nk) * P, c0:c0 + w].rearrange("(k p) n -> p k n", p=P), f"w{i}", after)
            off += w
        return s, tok

    def gemm(lhs, KT, W, pieces, lhs_ready):
        pair = gpair[gcount[0] % 2]
        gcount[0] += 1
        width = sum(w for _, w in pieces)
        first = list(lhs_ready) + pair[0].take() + pair[1].take()
        done = [None, None]
        for k0 in range(0, KT, SLOTK):
            nk = min(SLOTK, KT - k0)
            s, tok = load_chunk(W, k0, nk, pieces)
            for kk in range(nk):
                kt = k0 + kk
                for t in range(2):
                    last = kt == KT - 1 or (kk == nk - 1 and t == 1)
                    r = pe.op(lambda e, kt=kt, t=t, kk=kk, s=s: e.matmul(
                        pair[t].ap[:, 0:width], lhs(kt, t), s.ap[:, kk, 0:width],
                        start=(kt == 0), stop=(kt == KT - 1)), [tok] + first, inc=last)
                    first = []
                    if kt == KT - 1:
                        done[t] = r
            s.put(r)
        return pair, done

    def gemm_T(rhs, KT, W, pieces, rhs_ready, mtiles):
        pair = gpair[gcount[0] % 2]
        gcount[0] += 1
        loads = []
        for k0 in range(0, KT, SLOTK):
            loads.append(load_chunk(W, k0, min(SLOTK, KT - k0), pieces))
        first = list(rhs_ready) + pair[0].take() + pair[1].take()
        done = [None, None]
        for m, cols in enumerate(mtiles):
            for kt in range(KT):
                s, tok = loads[kt // SLOTK]
                r = pe.op(lambda e, m=m, kt=kt, s=s, cols=cols: e.matmul(
                    pair[m // 2].ap[:, 256 * (m % 2):256 * (m % 2) + 256], cols(s.ap[:, kt % SLOTK, :]), rhs(kt),
                    start=(kt == 0), stop=(kt == KT - 1)), [tok] + first, inc=(kt == KT - 1))
                first = []
            done[m // 2] = r
        for s, _ in loads:
            s.put(r)
        return pair, done

    def rsqrt(src, n, after):
        y, t = stat(n), stat(n)
        yi, ti = y.bitcast(I32), t.bitcast(I32)
        r = dve.op(lambda e: e.tensor_scalar(ti, src.bitcast(I32), 1, None, ALU.logical_shift_right), after)
        r = dve.op(lambda e: e.tensor_scalar(yi, ti, -1.0, 1597463007.0, ALU.mult, ALU.add), [r])
        for _ in range(3):
            r = dve.op(lambda e: e.tensor_tensor(t, y, y, ALU.mult), [r])
            r = dve.op(lambda e: e.scalar_tensor_tensor(out=t, in0=t, scalar=-0.5, in1=src, op0=ALU.mult,
                                                        op1=ALU.mult), [r])
            r = dve.op(lambda e: e.scalar_tensor_tensor(out=y, in0=t, scalar=1.5, in1=y, op0=ALU.add,
                                                        op1=ALU.mult), [r])
        return y, r

    def rstd(ss, n, count, after):
        ms = stat(n)
        r = dve.op(lambda e: e.tensor_scalar(ms, ss, 1.0 / count, 1e-6, ALU.mult, ALU.add), after)
        return rsqrt(ms, n, [r])

    def row_rstd(src, ready):
        ss = stat(2)
        ra = []
        for t in range(2):
            r = act.op(lambda e, t=t: e.activation(O[:, t, :], src[:, t, :], ACT.Square, accum_out=ss[:, t:t + 1]),
                       [ready[t]] + xnb.take())
            ra.append(r)
        return rstd(ss, 2, 1024, ra)

    xnb = Buf(O)

    def norm_T(src, ready, g0, dst):
        r, tr = row_rstd(src, ready)
        fr = []
        tn = [dve.op(lambda e: e.tensor_scalar(O[:, 0, :], src[:, 0, :], r[:, 0:1], None, ALU.mult), [tr] + fr),
              act.op(lambda e: e.activation(O[:, 1, :], src[:, 1, :], ACT.Copy, scale=r[:, 1:2]), [tr] + fr)]
        fd = dst.take()
        out = []
        for t in range(2):
            for g in range(2):
                b = nextbank()
                fb = b.take()
                for i in range(4):
                    kt = 4 * g + i
                    r2 = pe.op(lambda e, b=b, i=i, kt=kt, t=t: e.transpose(
                        b.ap[:, i * P:(i + 1) * P], O[:, t, kt * P:(kt + 1) * P], ident), [tn[t], tgc] + fb,
                        inc=(i == 3))
                if t == 0:
                    r3 = dve.op(lambda e, b=b, g=g, t=t: e.tensor_tensor(
                        dst.ap[:, 4 * g:4 * g + 4, t * P:(t + 1) * P],
                        b.ap[:, :].rearrange("p (k n) -> p k n", k=4),
                        gcol[:, g0 + 4 * g:g0 + 4 * g + 4].unsqueeze(2).to_broadcast([P, 4, P]), ALU.mult),
                        [r2] + fd)
                else:
                    for i in range(4):
                        kt = 4 * g + i
                        r3 = act.op(lambda e, b=b, i=i, kt=kt, t=t: e.activation(
                            dst.ap[:, kt, t * P:(t + 1) * P], b.ap[:, i * P:(i + 1) * P], ACT.Copy,
                            scale=gcol[:, g0 + kt:g0 + kt + 1]), [r2] + fd)
                b.put(r3)
                out.append(r3)
        xnb.put(r2)
        return out

    evac_n = [0]

    def evac(dst, src, after, pick=None):
        evac_n[0] += 1
        if pick == "act" or (pick is None and evac_n[0] % 2):
            return act.op(lambda e: e.activation(dst, src, ACT.Copy), after)
        return dve.op(lambda e: e.tensor_copy(dst, src), after)

    def add_x(bank, t, n0, scale, tok):
        r = dve.op(lambda e: e.scalar_tensor_tensor(out=x[:, t, n0:n0 + 512], in0=bank.ap[:, :], scalar=scale,
                                                    in1=x[:, t, n0:n0 + 512], op0=ALU.mult, op1=ALU.add), [tok])
        bank.put(r)
        return r

    def project_x(lhs, KT, W, ready, scale):
        toks = [None, None]
        for c in range(2):
            pair, done = gemm(lhs, KT, W, [(512 * c, 512)], ready)
            for t in range(2):
                toks[t] = add_x(pair[t], t, 512 * c, scale, done[t])
        return toks, pe.last()

    hTb = Buf(hT)

    def ffn(xready, g0, W1, W2, F, gated, scale):
        hr = norm_T(x, xready, g0, hTb)
        snap = snapshot()
        nch = 11 if gated else 8
        per = 2 if gated else 4
        Fh = F
        pend = None
        ready = []

        def flush(p):
            c, toks, bufs = p
            for g in range(per // 2):
                b = nextbank()
                fb = b.take()
                for i in range(2):
                    for t in range(2):
                        jj = 2 * g + i
                        r = pe.op(lambda e, b=b, i=i, t=t, jj=jj, bufs=bufs: e.transpose(
                            b.ap[:, (2 * i + t) * P:(2 * i + t + 1) * P], bufs[t].ap[:, jj * P:(jj + 1) * P], ident),
                            [toks[t]] + fb, inc=(i == 1 and t == 1))
                k0 = per * c + 2 * g
                r2 = evac(actT[:, k0:k0 + 2, :].rearrange("p k t -> p (k t)"), b.ap[:, :], [r] + snap)
                b.put(r2)
                ready.append(r2)
            for t in range(2):
                bufs[t].put(r)

        for c in range(nch):
            pcs = [(256 * c, 256), (F + 256 * c, 256)] if gated else [(512 * c, 512)]
            pair, done = gemm(lambda kt, t: hT[:, kt, t * P:(t + 1) * P], 8, W1, pcs, hr)
            toks, bufs = [], []
            for t in range(2):
                s, a = fs_rot.next(), fa_rot.next()
                if gated:
                    r = act.op(lambda e, t=t, s=s, pair=pair: e.activation(s.ap[:, 0:256], pair[t].ap[:, 0:256], ACT.Silu),
                               [done[t]] + s.take() + snap)
                    r = dve.op(lambda e, t=t, s=s, a=a, pair=pair: e.tensor_tensor(
                        a.ap[:, 0:256], s.ap[:, 0:256], pair[t].ap[:, 256:512], ALU.mult), [r] + a.take() + snap)
                else:
                    r = act.op(lambda e, t=t, s=s, pair=pair: e.activation(s.ap, pair[t].ap[:, :], ACT.Relu),
                               [done[t]] + s.take() + snap)
                    r = dve.op(lambda e, s=s, a=a: e.tensor_tensor(a.ap, s.ap, s.ap, ALU.mult),
                               [r] + a.take() + snap)
                pair[t].put(r)
                s.put(r)
                toks.append(r)
                bufs.append(a)
            if pend:
                flush(pend)
            pend = (c, toks, bufs)
        hTb.put(pe.last())
        flush(pend)
        toks, pl = project_x(lambda kt, t: actT[:, kt, t * P:(t + 1) * P], Fh // P, W2, ready, scale)
        return toks, snapshot()

    fillers = []
    pending = []

    late = []

    def finish_late():
        while late:
            f, into = late.pop(0)
            into.append(f())

    def settle():
        finish_late()
        while pending:
            pending.pop(0)()

    def fill():
        settle()
        if fillers:
            pending.append(fillers.pop(0)())

    def drain_fill():
        while fillers or pending:
            fill()
        finish_late()

    def head_prep(bank, tok, nh, hd, gain, dst, k0, t, rope_on=False, dstfree=()):
        w = nh * hd
        sq = sqj_rot.next()
        r = act.op(lambda e: e.activation(sq.ap[:, 0:w], bank.ap[:, 0:w], ACT.Square), [tok] + sq.take())
        ss = stat(nh)
        r = dve.op(lambda e: e.tensor_reduce(ss, sq.ap[:, 0:w].rearrange("p (h d) -> p h d", h=nh), AX, ALU.add), [r])
        rs, r = rstd(ss, nh, hd, [r])
        n3 = sq.ap[:, 0:w].rearrange("p (h d) -> p h d", h=nh)
        r = dve.op(lambda e: e.tensor_tensor(n3, bank.ap[:, 0:w].rearrange("p (h d) -> p h d", h=nh),
                                             rs.unsqueeze(2).to_broadcast([P, nh, hd]), ALU.mult), [r])
        bank.put(r)
        r = pool.op(lambda e: e.tensor_tensor(n3, n3, gain.unsqueeze(1).to_broadcast([P, nh, hd]), ALU.mult),
                    [r, tsm])
        if rope_on:
            tmp = rtmp_rot.next()
            ft = tmp.take()
            q = tmp.ap
            x1, x2 = n3[:, :, 0:8], n3[:, :, 8:16]
            cb = rope[:, 0, t, :].unsqueeze(1).to_broadcast([P, nh, 8])
            sb_ = rope[:, 1, t, :].unsqueeze(1).to_broadcast([P, nh, 8])
            rr = [dve.op(lambda e, i=i, a=a, b=b: e.tensor_tensor(q[:, i, :, :], a, b, ALU.mult), [r, trope] + ft)
                  for i, (a, b) in enumerate(((x1, cb), (x2, sb_), (x2, cb), (x1, sb_)))][-1]
            dve.op(lambda e: e.tensor_tensor(x1, q[:, 0, :, :], q[:, 1, :, :], ALU.subtract), [rr])
            r = dve.op(lambda e: e.tensor_tensor(x2, q[:, 2, :, :], q[:, 3, :, :], ALU.add), [rr])
            tmp.put(r)
        nt = w // P

        def finish():
            b = nextbank()
            fb = b.take()
            for i in range(nt):
                r2 = pe.op(lambda e, i=i: e.transpose(b.ap[:, i * P:(i + 1) * P], sq.ap[:, i * P:(i + 1) * P], ident),
                           [r, tgc] + fb, inc=(i == nt - 1))
            r3 = evac(dst[:, k0:k0 + nt, t * P:(t + 1) * P], b.ap[:, 0:nt * P].rearrange("p (k n) -> p k n", k=nt),
                      [r2] + list(dstfree))
            b.put(r3)
            sq.put(r2)
            return r3
        return finish

    def softmax_group(s, nh, nk, tok, sink=None):
        s3 = s.ap[:, 0:nh * nk].rearrange("p (h k) -> p h k", h=nh)
        nm, sm = stat(nh), stat(nh)
        if sink is None:
            r = dve.op(lambda e: e.tensor_reduce(nm, s3, AX, ALU.max, negate=True), [tok])
        else:
            mx = stat(nh)
            r = dve.op(lambda e: e.tensor_reduce(mx, s3, AX, ALU.max), [tok])
            r = dve.op(lambda e: e.tensor_tensor(mx, mx, sink, ALU.max), [r, tsm])
            r = dve.op(lambda e: e.tensor_scalar(nm, mx, -1.0, None, ALU.mult), [r])
        for i in range(nh):
            r2 = act.op(lambda e, i=i: e.activation(s3[:, i, :], s3[:, i, :], ACT.Exp, bias=nm[:, i:i + 1],
                                                    accum_out=sm[:, i:i + 1]), [r])
        if sink is not None:
            es = stat(nh)
            r = dve.op(lambda e: e.tensor_tensor(es, sink, nm, ALU.add), [r])
            r = act.op(lambda e: e.activation(es, es, ACT.Exp), [r])
            r2 = dve.op(lambda e: e.tensor_tensor(sm, sm, es, ALU.add), [r, r2])
        return r2, sm

    def p_transposed(s, nh, nkt, tok):
        b = nextbank()
        fb = b.take()
        n = nh * nkt
        for i in range(n):
            r = pe.op(lambda e, i=i: e.transpose(b.ap[:, i * P:(i + 1) * P], s.ap[:, i * P:(i + 1) * P], ident),
                      [tok] + fb, inc=(i == n - 1))
        s.put(r)
        pt = pT_rot.next()
        r = evac(pt.ap[:, 0:n * P], b.ap[:, 0:n * P], [r] + pt.take())
        b.put(r)
        return pt, r

    def head_attention(q_at, k_at, v_at, ready_qk, ready_v, bias_at, snap, out_cols, sink=None, kfirst=None):
        work = []
        for t in range(2):
            per = 4 if t == 0 else 2
            for a in range(0, 4, per):
                for par in range(2):
                    work.append((t, [2 * (a + i) + par for i in range(per)]))
        state = {}
        otoks = [None, None]
        rsum = [stat(8), stat(8)]
        left = [8, 8]
        sumtok = [[], []]

        def score(t, heads):
            nk = P * (t + 1)
            nh = len(heads)
            b = nextbank()
            fb = b.take()
            for i, h in enumerate(heads):
                r = pe.op(lambda e, i=i, h=h: e.matmul(b.ap[:, i * nk:(i + 1) * nk], q_at(h, t), k_at(h, nk),
                                                       start=True, stop=True), list(ready_qk) + fb, inc=(i == nh - 1))
            s = S_rot.next()
            s3 = s.ap[:, 0:nh * nk].rearrange("p (h k) -> p h k", h=nh)
            bias, tbias = bias_at(heads, t)
            r = dve.op(lambda e: e.scalar_tensor_tensor(
                out=s3, in0=b.ap[:, 0:nh * nk].rearrange("p (h k) -> p h k", h=nh), scalar=0.125, in1=bias,
                op0=ALU.mult, op1=ALU.add), [r] + tbias + s.take() + snap)
            b.put(r)
            sk = None if sink is None else sink[:, heads[0]:heads[-1] + 1:2]
            r, sm = softmax_group(s, nh, nk, r, sk)
            r2 = dve.op(lambda e: e.reciprocal(rsum[t][:, heads[0]:heads[-1] + 1:2], sm), [r])
            sumtok[t].append(r2)
            return s, r

        def finish(t, heads, s, tok):
            nkt = t + 1
            pt, r = p_transposed(s, len(heads), nkt, tok)
            fo = ob.take()
            for i, h in enumerate(heads):
                for kt in range(nkt):
                    r2 = pe.op(lambda e, i=i, h=h, kt=kt: e.matmul(
                        ob.ap[:, 64 * h:64 * h + 64], pt.ap[:, (i * nkt + kt) * P:(i * nkt + kt + 1) * P],
                        v_at(h, kt), start=(kt == 0), stop=(kt == nkt - 1)), [r] + list(ready_v) + fo,
                        inc=(i == len(heads) - 1 and kt == nkt - 1))
            pt.put(r2)
            left[t] -= len(heads)
            if left[t] == 0:
                r3 = dve.op(lambda e: e.tensor_tensor(
                    O[:, t, out_cols:out_cols + 512].rearrange("p (h d) -> p h d", h=8),
                    ob.ap[:, :].rearrange("p (h d) -> p h d", h=8),
                    rsum[t].unsqueeze(2).to_broadcast([P, 8, 64]), ALU.mult), [r2] + sumtok[t] + ofree)
                ob.put(r3)
                otoks[t] = r3

        ofree = xnb.take()
        xnb.put(*ofree)
        prev = None
        for t, heads in work:
            s, r = score(t, heads)
            fill()
            if prev:
                finish(*prev)
            prev = (t, heads, s, r)
        finish(*prev)
        return otoks

    def transpose_out(src_cols, k0, toks, oT_free):
        out = []
        for g in range(2):
            b = nextbank()
            fb = b.take()
            for i in range(2):
                for t in range(2):
                    c = src_cols + (2 * g + i) * P
                    r = pe.op(lambda e, i=i, t=t, c=c, b=b: e.transpose(
                        b.ap[:, (2 * i + t) * P:(2 * i + t + 1) * P], O[:, t, c:c + P], ident),
                        [toks[t]] + fb, inc=(i == 1 and t == 1))
            r2 = evac(oT[:, k0 + 2 * g:k0 + 2 * g + 2, :].rearrange("p k t -> p (k t)"), b.ap[:, :], [r] + oT_free)
            b.put(r2)
            out.append(r2)
        xnb.put(r)
        return out

    tg = {}
    b0 = nextbank()
    r = pe.op(lambda e: e.transpose(b0.ap[:, 0:112], rows[:, :], cst[0:112, 0:112]), [tcst, trow])
    tgc = dve.op(lambda e: e.tensor_copy(gcol[:, :], b0.ap[:, 0:112]), [r])
    b0.put(tgc)

    def trig_prep():
        r = dve.op(lambda e: e.tensor_copy(posf[:, :], posr[:, :]), [tsm])
        r0 = dve.op(lambda e: e.tensor_copy(ssr[:, 2, :].rearrange("p (a n) -> p a n", a=2),
                                            lsr[:, :].unsqueeze(2).to_broadcast([16, 2, 64])), [tsm])
        b = nextbank()
        fb = b.take()
        pe.op(lambda e: e.transpose(b.ap[:, 0:2], posf[:, :], cst[0:2, 0:2]), [r, tcst] + fb, inc=False)
        for i in range(3):
            r = pe.op(lambda e, i=i: e.transpose(b.ap[:, 16 + 16 * i:32 + 16 * i], ssr[:, i, :], cst[0:16, 0:16]),
                      [r0], inc=(i == 2))
        ang = stat(32)
        raw = stat(64)
        r = dve.op(lambda e: e.tensor_copy(raw[:, :], b.ap[:, 0:64]), [r])
        b.put(r)
        rdt = act.op(lambda e: e.activation(SM[:, 0, :], raw[:, 48:64], ACT.Exp), [r])
        lr, li = raw[:, 16:32], raw[:, 32:48]
        for t in range(2):
            r = dve.op(lambda e, t=t: e.tensor_scalar(ang[:, 8 * t:8 * t + 8], inv8, raw[:, t:t + 1], None, ALU.mult),
                       [r])
        r = dve.op(lambda e: e.tensor_tensor(ang[:, 16:32], li, SM[:, 0, :], ALU.mult), [r, rdt])
        k, kh, kl, pk = stat(32), stat(32), stat(32), pieces_of_two_pi()
        r = dve.op(lambda e: e.tensor_scalar(k, ang, 1.0 / TWO_PI, MAGIC, ALU.mult, ALU.add), [r])
        r = dve.op(lambda e: e.tensor_scalar(k, k, MAGIC, None, ALU.subtract), [r])
        r = dve.op(lambda e: e.tensor_scalar(kh, k, 1.0 / 2048, MAGIC, ALU.mult, ALU.add), [r])
        r = dve.op(lambda e: e.tensor_scalar(kh, kh, MAGIC, 2048.0, ALU.subtract, ALU.mult), [r])
        r = dve.op(lambda e: e.tensor_tensor(kl, k, kh, ALU.subtract), [r])
        for kk, pp in ((kh, pk[0]), (kl, pk[0]), (kh, pk[1]), (kl, pk[1]), (kh, pk[2]), (kl, pk[2]), (k, pk[3])):
            r = dve.op(lambda e, kk=kk, pp=pp: e.scalar_tensor_tensor(out=ang, in0=kk, scalar=-pp, in1=ang,
                                                                      op0=ALU.mult, op1=ALU.add), [r])
        lim = 3.1415925
        r = dve.op(lambda e: e.tensor_scalar(ang, ang, lim, -lim, ALU.min, ALU.max), [r])
        na = stat(32)
        r2 = dve.op(lambda e: e.tensor_scalar(na, ang, -1.0, None, ALU.mult), [r])
        r2 = dve.op(lambda e: e.tensor_tensor(na, na, ang, ALU.min), [r2])
        r2 = dve.op(lambda e: e.tensor_scalar(na, na, math.pi / 2, None, ALU.add), [r2])
        sn, cs = stat(32), stat(32)
        r1 = act.op(lambda e: e.activation(sn, ang, ACT.Sin), [r])
        r2 = act.op(lambda e: e.activation(cs, na, ACT.Sin), [r2])
        r = dve.op(lambda e: e.tensor_copy(rope[:, 0, :, :].rearrange("p a b -> p (a b)"), cs[:, 0:16]), [r2])
        tro = dve.op(lambda e: e.tensor_copy(rope[:, 1, :, :].rearrange("p a b -> p (a b)"), sn[:, 0:16]), [r1])
        dve.op(lambda e: e.tensor_copy(SM[:, 2, :], cs[:, 16:32]))
        dve.op(lambda e: e.tensor_copy(SM[:, 3, :], sn[:, 16:32]))
        w = [stat(16) for _ in range(6)]
        r = dve.op(lambda e: e.tensor_tensor(w[0], lr, SM[:, 0, :], ALU.mult), [rdt])
        rm = act.op(lambda e: e.activation(SM[:, 1, :], w[0], ACT.Exp), [r])

        def tt(o, a, b_, op, after):
            return dve.op(lambda e: e.tensor_tensor(o, a, b_, op), after)
        r = tt(w[0], SM[:, 1, :], SM[:, 2, :], ALU.mult, [rm, dve.last()])
        r = dve.op(lambda e: e.tensor_scalar(w[0], w[0], -1.0, None, ALU.add), [r])
        tt(w[1], SM[:, 1, :], SM[:, 3, :], ALU.mult, [])
        tt(w[2], lr, lr, ALU.mult, [])
        r = tt(w[3], li, li, ALU.mult, [])
        r = tt(w[2], w[2], w[3], ALU.add, [r])
        rd = dve.op(lambda e: e.reciprocal(w[2], w[2]), [r])
        r = tt(w[3], w[0], lr, ALU.mult, [rd])
        r = tt(w[4], w[1], li, ALU.mult, [])
        r = tt(w[3], w[3], w[4], ALU.add, [r])
        r = tt(SM[:, 4, :], w[3], w[2], ALU.mult, [r])
        r = tt(w[4], w[1], lr, ALU.mult, [r])
        r = tt(w[5], w[0], li, ALU.mult, [])
        r = tt(w[4], w[4], w[5], ALU.subtract, [r])
        tf = tt(SM[:, 5, :], w[4], w[2], ALU.mult, [r])
        fre = SM[:, 4, :].unsqueeze(2).to_broadcast([P, 16, 32])
        fim = SM[:, 5, :].unsqueeze(2).to_broadcast([P, 16, 32])
        tA, tB, tC, tD = (biasA[:, 2 * i:2 * i + 2, :].rearrange("p a (b h) -> p (a b) h", h=32) for i in range(4))
        tt(tA, BL[:, 0, :, :], fre, ALU.mult, [tf, tbl])
        tt(tB, BL[:, 1, :, :], fim, ALU.mult, [])
        tt(tC, BL[:, 1, :, :], fre, ALU.mult, [])
        r = tt(tD, BL[:, 0, :, :], fim, ALU.mult, [])
        tt(BL[:, 0, :, :], tA, tB, ALU.subtract, [r])
        r = tt(BL[:, 1, :, :], tC, tD, ALU.add, [r])
        for ri in range(2):
            b = nextbank()
            fb = b.take()
            for J in range(4):
                r2 = pe.op(lambda e, b=b, ri=ri, J=J: e.transpose(
                    b.ap[:, J * P:(J + 1) * P], BL[:, ri, 4 * J:4 * J + 4, :].rearrange("p j h -> p (j h)"), ident),
                    [r] + fb, inc=(J == 3))
            tbt = dve.op(lambda e, b=b, ri=ri: e.tensor_copy(BT[:, ri, :, :].rearrange("p J c -> p (J c)"), b.ap[:, :]),
                         [r2])
            b.put(tbt)
        tg["bt"] = tbt
        tg["sm"] = tf
        return tro

    pqb = [Buf(p) for p in pq]
    ptab = {}

    def phase_table(J):
        buf = pqb[J % 2]
        t = buf.ap
        scr = tabs
        r = [pool.op(lambda e, ri=ri: e.tensor_copy(t[:, ri, :, 0:1], SM[:, 2 + ri, 4 * J:4 * J + 4].unsqueeze(2)),
                     [tg["sm"]] + buf.take()) for ri in range(2)]
        n = 1
        while n < 256:
            c, s = t[:, 0, :, 0:n], t[:, 1, :, 0:n]
            cw = t[:, 0, :, n - 1:n].to_broadcast([P, 4, n])
            sw = t[:, 1, :, n - 1:n].to_broadcast([P, 4, n])
            u1, u2 = scr[:, 0, :, 0:n], scr[:, 1, :, 0:n]
            for out, (a, b_), op in ((0, (cw, sw), ALU.subtract), (1, (sw, cw), ALU.add)):
                ra = pool.op(lambda e, a=a, u1=u1, c=c: e.tensor_tensor(u1, c, a, ALU.mult), r)
                rb = pool.op(lambda e, b_=b_, u2=u2, s=s: e.tensor_tensor(u2, s, b_, ALU.mult), r)
                ro = pool.op(lambda e, out=out, n=n, op=op, u1=u1, u2=u2: e.tensor_tensor(
                    t[:, out, :, n:2 * n], u1, u2, op), [ra, rb])
                r = [ro]
            n *= 2
        ptab[J] = ro

    def mem_load():
        fr = xnb.take()
        tm = [dma(pool, M[:, t, :], v("mem").rearrange("b (t p) d -> t p (b d)", p=P)[t], "mem", fr + mfree[:])
              for t in range(2)]
        xnb.put(*fr)
        return [tm[-1], tm[-1]]

    mfree = []
    mTb = Buf(mT)
    xkv = Buf(None)

    def cross_kv_fillers(l):
        W = v("x_w_kv")[l]
        xg_r = []
        out = {"k": [], "v": []}
        xkfree = xkv.take()
        txg = dma(pool, xg[:, :, :].rearrange("p a b -> p (a b)"), bc_rows(v("x_qk_gains")[l], 512), "xg", xgfree[:])

        def chunk(c):
            def start():
                pair, done = gemm(lambda kt, t: mT[:, kt, t * P:(t + 1) * P], 8, W, [(512 * c, 512)], mready[:])
                if c == 3:
                    mTb.put(pe.last())

                def consume():
                    for t in range(2):
                        if c < 2:
                            late.append((head_prep(pair[t], done[t], 2, 256, KG(1), xkT, 4 * c, t, dstfree=xkfree),
                                         out["k"]))
                        else:
                            r = evac(xv[:, t, 512 * (c - 2):512 * (c - 1)], pair[t].ap[:, :], [done[t]] + xkfree)
                            pair[t].put(r)
                            out["v"].append(r)
                return consume
            return start

        def KG(i):
            pool.wait([txg])
            return xg[:, i, :]
        fillers.extend([chunk(c) for c in range(4)])
        return out, KG

    xgfree = []

    def cross_attention(xready, l, kvout, KG):
        hr = norm_T(x, xready, (5 * l + 2) * 8, hTb)
        snap = snapshot()
        drain_fill()
        qr = []
        for c in range(2):
            pair, done = gemm(lambda kt, t: hT[:, kt, t * P:(t + 1) * P], 8, v("x_w_q")[l], [(512 * c, 512)], hr)
            finish_late()
            for t in range(2):
                late.append((head_prep(pair[t], done[t], 2, 256, KG(0), qT, 4 * c, t, dstfree=snap), qr))
        finish_late()
        hTb.put(pe.last())
        xgfree.append(pool.last())
        ready = qr + kvout["k"]
        prev = None
        rs = [stat(4), stat(4)]
        otok = {}
        stoks = {}
        ofree = xnb.take()
        xnb.put(*ofree)

        def score(t, hp):
            b = nextbank()
            fb = b.take()
            for i in range(2):
                h = 2 * hp + i
                for c in range(2):
                    r = pe.op(lambda e, i=i, h=h, c=c: e.matmul(
                        b.ap[:, 256 * i:256 * i + 256], qT[:, 2 * h + c, t * P:(t + 1) * P], xkT[:, 2 * h + c, :],
                        start=(c == 0), stop=(c == 1)), ready + fb, inc=(i == 1 and c == 1))
            s = S_rot.next()
            r = act.op(lambda e: e.activation(s.ap, b.ap[:, :], ACT.Copy, scale=0.0625), [r] + s.take() + snap)
            b.put(r)
            r, sm = softmax_group(s, 2, 256, r)
            stoks[(t, hp)] = dve.op(lambda e: e.reciprocal(rs[t][:, 2 * hp:2 * hp + 2], sm), [r])
            return s, r

        def finish(t, hp, s, tok):
            pt, r = p_transposed(s, 2, 2, tok)
            fo = ob.take()
            for i in range(2):
                h = 2 * hp + i
                for kt in range(2):
                    r2 = pe.op(lambda e, i=i, h=h, kt=kt: e.matmul(
                        ob.ap[:, 256 * i:256 * i + 256], pt.ap[:, (2 * i + kt) * P:(2 * i + kt + 1) * P],
                        xv[:, kt, 256 * h:256 * h + 256], start=(kt == 0), stop=(kt == 1)), [r] + kvout["v"] + fo,
                        inc=(i == 1 and kt == 1))
            pt.put(r2)
            r3 = dve.op(lambda e: e.tensor_tensor(
                O[:, t, 512 * hp:512 * hp + 512].rearrange("p (h d) -> p h d", h=2),
                ob.ap[:, :].rearrange("p (h d) -> p h d", h=2),
                rs[t][:, 2 * hp:2 * hp + 2].unsqueeze(2).to_broadcast([P, 2, 256]), ALU.mult),
                [r2, stoks[(t, hp)]] + ofree)
            ob.put(r3)
            otok[(t, hp)] = r3

        outr = []
        oTf = oTb.take()
        for hp in range(2):
            for t in range(2):
                s, r = score(t, hp)
                if prev:
                    finish(*prev)
                prev = (t, hp, s, r)
        finish(*prev)
        for hp in range(2):
            outr += transpose_out(512 * hp, 4 * hp, [otok[(0, hp)], otok[(1, hp)]], oTf)
        xkv.put(pe.last())
        toks, pl = project_x(lambda kt, t: oT[:, kt, t * P:(t + 1) * P], 8, v("x_w_o")[l], outr, 1.0)
        oTb.put(pl)
        return toks

    oTb = Buf(oT)

    def even_mixer(xready):
        hr = norm_T(x, xready, 8, hTb)
        snap = snapshot()
        W = v("even_w_in")[0]
        lhs = lambda kt, t: hT[:, kt, t * P:(t + 1) * P]
        qr, vr = [], []

        def chunk_qk(c0, gi, dst, rope_on, acc, dfree):
            pair, done = gemm(lhs, 8, W, [(c0, 512)], hr)

            def consume():
                return [head_prep(pair[t], done[t], 8, 64, evg[:, gi, :], dst, 0, t, rope_on, dfree) for t in range(2)]
            return consume
        pair, done = gemm(lhs, 8, W, [(1536, 8)], hr)
        fz, fn_, lf = [], [], []
        for t in range(2):
            z, na, mn = stat(8), stat(8), stat(8)
            r = dve.op(lambda e, t=t, z=z: e.tensor_tensor(z, pair[t].ap[:, 0:8], fbias[:, :], ALU.add), [done[t], tsm])
            pair[t].put(r)
            r = dve.op(lambda e, z=z, na=na: e.tensor_scalar(na, z, -1.0, None, ALU.mult), [r])
            r = dve.op(lambda e, z=z, na=na: e.tensor_tensor(na, na, z, ALU.min), [r])
            rm = dve.op(lambda e, z=z, mn=mn: e.tensor_scalar(mn, z, 0.0, None, ALU.min))
            r = act.op(lambda e, na=na: e.activation(na, na, ACT.Exp), [r])
            fz.append((na, mn, r, rm))
        for t in range(2):
            na, mn, r, rm = fz[t]
            r = act.op(lambda e, na=na: e.activation(na, na, ACT.Ln, bias=1.0), [r])
            lg = stat(8)
            r = dve.op(lambda e, na=na, mn=mn, lg=lg: e.tensor_tensor(lg, mn, na, ALU.subtract), [r, rm])
            lf.append((lg, r))

        def logf_sums():
            b = nextbank()
            fb = b.take()
            pe.op(lambda e: e.matmul(b.ap[0:8, 0:256], lf[0][0], cst[:, 128:384], start=True, stop=False),
                  [lf[0][1], lf[1][1]] + fb, inc=False)
            r = pe.op(lambda e: e.matmul(b.ap[0:8, 128:256], lf[1][0], tri, start=False, stop=True))
            r1 = dve.op(lambda e: e.tensor_copy(cumT[:, 0, :], b.ap[0:8, 0:256]), [r])
            r1 = dve.op(lambda e: e.tensor_scalar(cumT[:, 1, :], b.ap[0:8, 0:256], -1.0, None, ALU.mult), [r])
            b.put(r1)
            tb_ = []
            for t in range(2):
                nk = P * (t + 1)
                per = 512 // nk
                for h0 in range(0, 8, per):
                    b = nextbank()
                    fb = b.take()
                    for i in range(per):
                        h = h0 + i
                        pe.op(lambda e, b=b, i=i, h=h, nk=nk: e.matmul(
                            b.ap[:, i * nk:(i + 1) * nk], sel(h, P), cumT[:, 1, 0:nk], start=True, stop=False),
                            [r1] + fb, inc=False)
                        r = pe.op(lambda e, b=b, i=i, h=h, nk=nk, t=t: e.matmul(
                            b.ap[:, i * nk:(i + 1) * nk], cumT[:, 0, t * P:(t + 1) * P], sel(h, nk),
                            start=False, stop=True), inc=(i == per - 1))
                    dstb = biasA[:, h0:h0 + per, :] if t else biasB[:, h0:h0 + per, 0:P]
                    r = dve.op(lambda e, b=b, dstb=dstb, nk=nk, per=per: e.tensor_tensor(
                        dstb, b.ap[:, 0:per * nk].rearrange("p (h k) -> p h k", h=per),
                        maskc[:, 256 - nk:256].unsqueeze(1).to_broadcast([P, per, nk]), ALU.add), [r] + snap)
                    b.put(r)
                    tb_.append(r)
            return tb_
        c1 = chunk_qk(0, 0, qT, False, qr, snap)
        p1 = c1()
        c2 = chunk_qk(512, 1, kT, False, qr, snap)
        qr += [f() for f in p1]
        p2 = c2()
        pair, done = gemm(lhs, 8, W, [(1024, 512)], hr)
        qr += [f() for f in p2]
        for t in range(2):
            r = evac(vsb[:, t, :], pair[t].ap[:, :], [done[t]] + vfree.take())
            pair[t].put(r)
            vr.append(r)
        tbias = logf_sums()
        R = {}

        def f_qk(c0, gi, dst, name):
            def start():
                c = chunk_qk(c0, gi, dst, True, None, snap)

                def consume():
                    R[name] = []
                    late.extend((f, R[name]) for f in c())
                return consume
            return start

        def f_v():
            pair, done = gemm(lhs, 8, W, [(2568, 512)], hr)
            hTb.put(pe.last())

            def consume():
                R["v"] = [evac(M[:, t, 0:512], pair[t].ap[:, :], [done[t]] + mem_read) for t in range(2)]
                for t in range(2):
                    pair[t].put(R["v"][t])
            return consume
        bq = qT[:, 4:8, :]
        bk = kT[:, 4:8, :]
        fillers.extend([f_qk(1544, 2, bq, "q"), f_qk(2056, 3, bk, "k"), f_v])
        kvout, KG = cross_kv_fillers(0)
        q_at = lambda h, t: qT[64 * (h % 2):64 * (h % 2) + 64, h // 2, t * P:(t + 1) * P]
        k_at = lambda h, nk: kT[64 * (h % 2):64 * (h % 2) + 64, h // 2, 0:nk]

        def bias_at(heads, t):
            hs = slice(heads[0], heads[-1] + 1, 2)
            return (biasA[:, hs, :] if t else biasB[:, hs, 0:P]), tbias
        ot = head_attention(q_at, k_at, lambda h, kt: vsb[:, kt, 64 * h:64 * h + 64], qr, vr, bias_at, snap, 0)
        settle()
        finish_late()
        rb = R["q"] + R["k"]
        oTf = oTb.take()
        outr = transpose_out(0, 0, ot, oTf)
        lw = stat(128)
        l2 = stat(2)
        r = dve.op(lambda e: e.tensor_tensor(lw.rearrange("p (a n) -> p a n", a=2), lamp[:, 0:4:2, :], lamp[:, 1:4:2, :],
                                             ALU.mult), [tsm])
        r = dve.op(lambda e: e.tensor_reduce(l2, lw.rearrange("p (a n) -> p a n", a=2), AX, ALU.add), [r])
        r = act.op(lambda e: e.activation(l2, l2, ACT.Exp), [r])
        lam_init = 0.8 - 0.6 * math.exp(-0.3 * 0)
        nl = stat(1)
        r = dve.op(lambda e: e.tensor_tensor(nl, l2[:, 1:2], l2[:, 0:1], ALU.subtract), [r])
        tnl = dve.op(lambda e: e.tensor_scalar(nl, nl, -lam_init, None, ALU.add), [r])
        work = [(0, [0, 1, 2, 3]), (1, [0, 1]), (1, [2, 3])]
        fin = []

        def score(t, heads):
            nk, nh = P * (t + 1), len(heads)
            got = []
            for j in range(2):
                b = nextbank()
                fb = b.take()
                for i, h in enumerate(heads):
                    r = pe.op(lambda e, i=i, h=h, j=j, b=b: e.matmul(
                        b.ap[:, i * nk:(i + 1) * nk], bq[64 * j:64 * j + 64, h, t * P:(t + 1) * P],
                        bk[64 * j:64 * j + 64, h, 0:nk], start=True, stop=True), rb + fb, inc=(i == nh - 1))
                s = S_rot.next()
                s3 = s.ap[:, 0:nh * nk].rearrange("p (h k) -> p h k", h=nh)
                r = dve.op(lambda e, b=b, s3=s3: e.scalar_tensor_tensor(
                    out=s3, in0=b.ap[:, 0:nh * nk].rearrange("p (h k) -> p h k", h=nh), scalar=0.125,
                    in1=maskb[:, 256 - nk:256].unsqueeze(1).to_broadcast([P, nh, nk]), op0=ALU.mult, op1=ALU.add),
                    [r] + s.take())
                b.put(r)
                r, sm = softmax_group(s, nh, nk, r)
                got.append((s, s3, r, sm))
            rr = []
            for j in range(2):
                s, s3, r, sm = got[j]
                rc = stat(nh)
                r = dve.op(lambda e, rc=rc, sm=sm: e.reciprocal(rc, sm), [r])
                if j:
                    r = dve.op(lambda e, rc=rc: e.tensor_scalar(rc, rc, nl, None, ALU.mult), [r, tnl])
                r = dve.op(lambda e, s3=s3, rc=rc: e.tensor_tensor(
                    s3, s3, rc.unsqueeze(2).to_broadcast([P, nh, nk]), ALU.mult), [r])
                rr.append(r)
            s = got[0][0]
            r = pool.op(lambda e: e.tensor_tensor(s.ap, s.ap, got[1][0].ap, ALU.add), rr)
            got[1][0].put(r)
            return s, r

        def finish(t, heads, s, tok):
            nkt = t + 1
            pt, r = p_transposed(s, len(heads), nkt, tok)
            fo = ob.take()
            for i, h in enumerate(heads):
                for kt in range(nkt):
                    r2 = pe.op(lambda e, i=i, h=h, kt=kt: e.matmul(
                        ob.ap[:, P * h:P * h + P], pt.ap[:, (i * nkt + kt) * P:(i * nkt + kt + 1) * P],
                        M[:, kt, P * h:P * h + P], start=(kt == 0), stop=(kt == nkt - 1)), [r] + R["v"] + fo,
                        inc=(i == len(heads) - 1 and kt == nkt - 1))
            pt.put(r2)
            if heads[-1] != 3:
                return
            sq = sqj_rot.next()
            r = act.op(lambda e: e.activation(sq.ap[:, 0:512], ob.ap[:, :], ACT.Square), [r2] + sq.take())
            ss = stat(4)
            r = dve.op(lambda e: e.tensor_reduce(ss, sq.ap[:, 0:512].rearrange("p (h d) -> p h d", h=4), AX, ALU.add),
                       [r])
            sq.put(r)
            rs, r = rstd(ss, 4, 128, [r])
            o3 = O[:, t, 512:1024].rearrange("p (h d) -> p h d", h=4)
            r = dve.op(lambda e: e.tensor_tensor(o3, ob.ap[:, :].rearrange("p (h d) -> p h d", h=4),
                                                 rs.unsqueeze(2).to_broadcast([P, 4, P]), ALU.mult), [r])
            ob.put(r)
            r = dve.op(lambda e: e.tensor_tensor(o3, o3, sublng[:, :].unsqueeze(1).to_broadcast([P, 4, P]), ALU.mult),
                       [r, tsm])
            r = dve.op(lambda e: e.tensor_scalar(O[:, t, 512:1024], O[:, t, 512:1024], 1.0 - lam_init, None, ALU.mult),
                       [r])
            fin.append(r)
        prev = None
        for t, heads in work:
            s, r = score(t, heads)
            fill()
            if prev:
                finish(*prev)
            prev = (t, heads, s, r)
        finish(*prev)
        outr += transpose_out(512, 4, fin, oTf)
        vfree.put(pe.last())
        drain_fill()
        toks, pl = project_x(lambda kt, t: oT[:, kt, t * P:(t + 1) * P], 8, v("even_w_out")[0], outr, 1.0)
        oTb.put(pl)
        mfree.append(pl)
        return toks, kvout, KG

    vfree = Buf(None)
    mem_read = []

    def odd_mixer(xready):
        hr = norm_T(x, xready, (5 + 1) * 8, hTb)
        snap = snapshot()
        W = v("odd_w_in")[0]
        lhs = lambda kt, t: hT[:, kt, t * P:(t + 1) * P]
        rel = v("rel")
        tb0 = dma(pool, biasB[:, :, :], bass.AP(rel.tensor, rel.offset, [[1, P], [512, 8], [1, 256]]), "rel", snap)
        tbias = []

        def rel_bias():
            for g in range(4):
                b = nextbank()
                r = pe.op(lambda e, b=b, g=g: e.matmul(
                    b.ap[:, :], flip, biasB[:, 2 * g:2 * g + 2, :].rearrange("p h k -> p (h k)"), start=True, stop=True),
                    [tb0] + b.take())
                r = dve.op(lambda e, b=b, g=g: e.tensor_tensor(
                    biasA[:, 2 * g:2 * g + 2, :], b.ap[:, :].rearrange("p (h k) -> p h k", h=2),
                    maskb.unsqueeze(1).to_broadcast([P, 2, 256]), ALU.add), [r] + snap)
                b.put(r)
                tbias.append(r)
        qr, vr = [], []
        pre = []
        for n, (c0, dst) in enumerate(((1536, qT), (2048, kT))):
            pair, done = gemm(lhs, 8, W, [(c0, 512)], hr)
            qr += [f() for f in pre]
            pre = [head_prep(pair[t], done[t], 8, 64, odg[:, n, :], dst, 0, t, False, snap) for t in range(2)]
        pair, done = gemm(lhs, 8, W, [(2560, 512)], hr)
        qr += [f() for f in pre]
        fv = vfree.take()
        for t in range(2):
            r = evac(vsb[:, t, :], pair[t].ap[:, :], [done[t]] + fv)
            pair[t].put(r)
            vr.append(r)
        rel_bias()
        tflip = pe.last()
        R = {}
        uc = biasB

        def f_conv(which, c0):
            def start():
                mt = [lambda w, m=m: w[:, P * m:P * m + P] for m in range(4)]
                pair, done = gemm_T(lambda kt: hT[:, kt, :], 8, W, [(c0, 512)], hr, mt)
                if which == "b":
                    hTb.put(pe.last())

                def consume():
                    if which == "c":
                        R["c"] = [evac(uc[:, 2 * m:2 * m + 2, :].rearrange("p a b -> p (a b)"), pair[m].ap[:, :],
                                       [done[m], tflip] + snap) for m in range(2)]
                        for m in range(2):
                            pair[m].put(R["c"][m])
                    elif which == "h":
                        R["u"] = []
                        for m in range(2):
                            o = uc[:, 2 * m:2 * m + 2, :].rearrange("p a b -> p (a b)")
                            r = dve.op(lambda e, o=o, m=m: e.tensor_tensor(o, o, pair[m].ap[:, :], ALU.mult),
                                       [done[m], R["c"][m]])
                            pair[m].put(r)
                            R["u"].append(r)
                        R["y"] = []
                        for k in range(4):
                            u, y = uc[:, k, :], uc[:, 4 + k, :]
                            w = [gcol[:, 96 + 4 * i + k:97 + 4 * i + k] for i in range(3)]
                            r = dve.op(lambda e, u=u, y=y, w=w: e.tensor_scalar(y, u, w[2], None, ALU.mult),
                                       [R["u"][k // 2]] + snap)
                            r = dve.op(lambda e, u=u, y=y, w=w: e.scalar_tensor_tensor(
                                out=y[:, 1:256], in0=u[:, 0:255], scalar=w[1], in1=y[:, 1:256], op0=ALU.mult,
                                op1=ALU.add), [r])
                            r = dve.op(lambda e, u=u, y=y, w=w: e.scalar_tensor_tensor(
                                out=y[:, 2:256], in0=u[:, 0:254], scalar=w[0], in1=y[:, 2:256], op0=ALU.mult,
                                op1=ALU.add), [r])
                            R["y"].append(r)
                    else:
                        R["o"] = []
                        for m in range(2):
                            o = oT[:, 2 * m:2 * m + 2, :].rearrange("p a b -> p (a b)")
                            r = dve.op(lambda e, o=o, m=m: e.tensor_tensor(
                                o, uc[:, 4 + 2 * m:6 + 2 * m, :].rearrange("p a b -> p (a b)"), pair[m].ap[:, :], ALU.mult),
                                [done[m], R["y"][2 * m], R["y"][2 * m + 1]] + oTf)
                            pair[m].put(r)
                            R["o"].append(r)
                return consume
            return start
        oTf = oTb.take()
        fillers.extend([f_conv("c", 512), f_conv("h", 1024), f_conv("b", 0)])
        kvout, KG = cross_kv_fillers(1)
        q_at = lambda h, t: qT[64 * (h % 2):64 * (h % 2) + 64, h // 2, t * P:(t + 1) * P]
        k_at = lambda h, nk: kT[64 * (h % 2):64 * (h % 2) + 64, h // 2, 0:nk]

        def bias_at(heads, t):
            return biasA[:, heads[0]:heads[-1] + 1:2, 256 - P * (t + 1):256], tbias
        ot = head_attention(q_at, k_at, lambda h, kt: vsb[:, kt, 64 * h:64 * h + 64], qr, vr, bias_at, snap, 512)
        outr = transpose_out(512, 4, ot, oTf)
        vfree.put(pe.last())
        drain_fill()
        outr += R["o"]
        toks, pl = project_x(lambda kt, t: oT[:, kt, t * P:(t + 1) * P], 8, v("odd_w_out")[0], outr, 1.0)
        oTb.put(pl)
        return toks, kvout, KG

    def second_mixer(xready):
        hr = norm_T(x, xready, 80, hTb)
        snap = snapshot()
        W = v("w_in_2")[0]
        lhs = lambda kt, t: hT[:, kt, t * P:(t + 1) * P]
        rhs = lambda kt: hT[:, kt, :]
        tal = [dma(pool, (biasA, biasB)[i][:, :, :], v("alibi")[i], f"al{i}", snap) for i in range(2)]
        mt4 = [lambda w, m=m: w[:, P * m:P * m + P] for m in range(4)]
        kd = [lambda w, m=m: w[:, 64 * m:64 * m + 64].unsqueeze(1).to_broadcast([P, 2, 64]) for m in range(2)]

        def queries(c0, dst):
            pair, done = gemm_T(rhs, 8, W, [(c0, 512)], hr, mt4)
            out = []
            for m in range(2):
                r = evac(dst[:, 2 * m:2 * m + 2, :].rearrange("p a b -> p (a b)"), pair[m].ap[:, :], [done[m]] + snap)
                pair[m].put(r)
                out.append(r)
            return out

        def keys(c0, dst, vdst):
            pair = gpair[gcount[0] % 2]
            gcount[0] += 1
            loads = [load_chunk(W, k0, SLOTK, [(c0, 256)]) for k0 in (0, 4)]
            first = hr + pair[0].take() + pair[1].take()
            for m in range(2):
                for kt in range(8):
                    s, tok = loads[kt // SLOTK]
                    for a in range(2):
                        pass
                    r0 = pe.op(lambda e, m=m, kt=kt, s=s: e.matmul(
                        pair[0].ap[:, 256 * m:256 * m + 256], kdup[kt // SLOTK].ap[:, kt % SLOTK, m, :, :].rearrange(
                            "p a b -> p (a b)"), hT[:, kt, :],
                        start=(kt == 0), stop=(kt == 7)), [tok, dupt(loads, kt)] + first, inc=(kt == 7))
                    first = []
            for t in range(2):
                for kt in range(8):
                    s, tok = loads[kt // SLOTK]
                    r1 = pe.op(lambda e, t=t, kt=kt, s=s: e.matmul(
                        pair[1].ap[:, P * t:P * t + P], hT[:, kt, t * P:(t + 1) * P], s.ap[:, kt % SLOTK, 128:256],
                        start=(kt == 0), stop=(kt == 7)), inc=(kt == 7))
            for s, _ in loads:
                s.put(r1)
            for kb in kdup:
                kb.put(r0)
            ra = evac(dst[:, 0:2, :].rearrange("p a b -> p (a b)"), pair[0].ap[:, :], [r0] + snap)
            pair[0].put(ra)
            rb_ = evac(vdst, pair[1].ap[:, 0:256].rearrange("p (t n) -> p t n", t=2), [r1] + snap)
            pair[1].put(rb_)
            return ra, rb_
        kdup = [Buf(M[:, i, :].rearrange("p (k m a b) -> p k m a b", k=4, m=2, a=2)) for i in range(2)]
        duptok = {}

        def dupt(loads, kt):
            i = kt // SLOTK
            key = (id(loads), i)
            if key not in duptok:
                s, tok = loads[i]
                kb = kdup[i]
                fr = kb.take() + snap
                for a in range(2):
                    r = dve.op(lambda e, a=a, s=s, kb=kb: e.tensor_copy(
                        kb.ap[:, :, :, a, :], s.ap[:, :, 0:128].rearrange("p k (m b) -> p k m b", m=2)), [tok] + fr)
                duptok[key] = r
                s.put(r)
            return duptok[key]
        qa, qm = qT[:, 0:4, :], qT[:, 4:8, :]
        ka, km = kT[:, 0:2, :], kT[:, 2:4, :]
        va, vm = (kT[:, 4 + i, :].rearrange("p (t n) -> p t n", t=2) for i in range(2))
        rqa = queries(0, qa)
        rka, rva = keys(512, ka, va)
        rqm = queries(1280, qm)
        rkm, rvm = keys(1792, km, vm)
        pair, done = gemm_T(rhs, 8, W, [(768, 512)], hr, mt4)
        fv = vfree.take()
        ru = []
        for m in range(2):
            r = evac(uT[:, 2 * m:2 * m + 2, :].rearrange("p a b -> p (a b)"), pair[m].ap[:, :], [done[m]] + fv)
            pair[m].put(r)
            ru.append(r)
        gt = {}

        def f_gate(c):
            def start():
                pair, done = gemm(lhs, 8, W, [(2048 + 512 * c, 512)], hr)
                if c == 5:
                    hTb.put(pe.last())

                def consume():
                    for t in range(2):
                        gsl = gates[:, t, 512 * c:512 * c + 512]
                        r = act.op(lambda e, t=t, gsl=gsl: e.activation(gsl, pair[t].ap[:, :], ACT.Exp, scale=-1.0),
                                   [done[t]] + snap)
                        pair[t].put(r)
                        r = dve.op(lambda e, gsl=gsl: e.tensor_scalar(gsl, gsl, 1.0, None, ALU.add), [r])
                        gt[(c, t)] = dve.op(lambda e, gsl=gsl: e.reciprocal(gsl, gsl), [r])
                return consume
            return start
        fillers.extend([f_gate(c) for c in range(6)])
        mtok = {}

        def gated(lhs_, KT, Wo, ready, branch):
            for c in range(2):
                pair, done = gemm(lhs_, KT, Wo, [(512 * c, 512)], ready)
                for t in range(2):
                    gsl = gates[:, t, 1024 * branch + 512 * c:1024 * branch + 512 * c + 512]
                    dst = M[:, t, 512 * c:512 * c + 512]
                    tg_ = gt[(2 * branch + c, t)]
                    if branch == 0:
                        r = dve.op(lambda e, dst=dst, gsl=gsl, t=t, pair=pair: e.tensor_tensor(
                            dst, gsl, pair[t].ap[:, :], ALU.mult), [done[t], tg_] + kdup[0].free + kdup[1].free)
                        pair[t].put(r)
                    else:
                        r = dve.op(lambda e, gsl=gsl, t=t, pair=pair: e.tensor_tensor(
                            gsl, gsl, pair[t].ap[:, :], ALU.mult), [done[t], tg_])
                        pair[t].put(r)
                        r = pool.op(lambda e, dst=dst, gsl=gsl: e.tensor_tensor(dst, dst, gsl, ALU.add),
                                    [r, mtok[(c, t)]])
                    mtok[(c, t)] = r

        def attend(qd, kd_, vd, rq, rv, bias, tb_, sink):
            q_at = lambda h, t: qd[64 * (h % 2):64 * (h % 2) + 64, h // 2, t * P:(t + 1) * P]
            k_at = lambda h, nk: kd_[64 * (h % 2):64 * (h % 2) + 64, h // 4, 0:nk]
            return head_attention(q_at, k_at, lambda h, kt: vd[:, kt, 64 * (h // 4):64 * (h // 4) + 64], rq, [rv],
                                  lambda heads, t: (bias[:, heads[0]:heads[-1] + 1:2, 256 - P * (t + 1):256], [tb_]),
                                  snap, 0, sink)
        ot = attend(qa, ka, va, rqa + [rka], rva, biasA, tal[0], sinkb)
        oTf = oTb.take()
        outa = transpose_out(0, 0, ot, oTf)
        ot = attend(qm, km, vm, rqm + [rkm], rvm, biasB, tal[1], None)
        outm = transpose_out(0, 4, ot, oTf)
        rz = []
        zin = qT[:, 0:4, :]
        crf = Buf(None)
        snap2 = snapshot()
        tzc = pool.op(lambda e: e.memset(CL, 0.0), snap2)
        tz = pool.op(lambda e: e.memset(CR, 0.0), snap2)
        for ri, nm in enumerate(("c_re_2", "c_im_2")):
            src = v(nm).rearrange("l (J g) h p -> g h (l J) p", g=8)
            for g in range(8):
                tcl = dma(pool, CL[16 * g:16 * g + 16, ri, :, 64 * (g % 2):64 * (g % 2) + 64], src[g], "cl", [tzc])
        ybuf = Buf(ssm_g)
        tb1 = Buf(ssm_t)
        tb1.put(*snap2)
        ybuf.put(*snap2)
        for J in range(4):
            fc = crf.take()
            for ri in range(2):
                b = nextbank()
                r = pe.op(lambda e, b=b, ri=ri, J=J: e.transpose(b.ap[:, 0:P], CL[:, ri, J, :], ident),
                          [tcl, tz] + b.take())
                dst = bass.AP(CR.tensor, CR.offset + 512 * ri, [[2048, P], [160, 4], [1, 32]])
                tcr = dve.op(lambda e, b=b, dst=dst, ri=ri: e.tensor_scalar(
                    dst, b.ap[:, 0:P].rearrange("p (j c) -> p j c", j=4), -1.0 if ri else 1.0, None, ALU.mult),
                    [r, tz] + fc)
                b.put(tcr)
            fill()
            yb = ob
            fy = yb.take()
            tab = pqb[J % 2]
            for jj in range(4):
                b = nextbank()
                fb = b.take()
                for ri in range(2):
                    r = pe.op(lambda e, b=b, ri=ri, jj=jj, J=J: e.matmul(
                        b.ap[:, 256 * ri:256 * ri + 256], BT[32 * jj:32 * jj + 32, ri, J, :],
                        uT[32 * jj:32 * jj + 32, J, :], start=True, stop=True), ru + [tg["bt"]] + fb, inc=(ri == 1))
                c = tab.ap[:, 0, jj, :].unsqueeze(1).to_broadcast([P, 2, 256])
                s = tab.ap[:, 1, jj, :].unsqueeze(1).to_broadcast([P, 2, 256])
                b3 = b.ap[:, :].rearrange("p (a t) -> p a t", a=2)
                T1 = ssm_t[:, 0, :].rearrange("p (a t) -> p a t", a=2)
                T2 = ssm_t[:, 1, :].rearrange("p (a t) -> p a t", a=2)
                ft = tb1.take()
                dve.op(lambda e, T1=T1, b3=b3, c=c: e.tensor_tensor(T1, b3, c, ALU.mult), [r, ptab[J]] + ft)
                r = dve.op(lambda e, T2=T2, b3=b3, s=s: e.tensor_tensor(T2, b3, s, ALU.mult))
                b.put(r)
                X = ssm_g[:, 0, :].rearrange("p (a t) -> p a t", a=2)
                G = ssm_g[:, 1, :].rearrange("p (a t) -> p a t", a=2)
                H = ssm_g[:, 2, :].rearrange("p (a t) -> p a t", a=2)
                r1 = pool.op(lambda e: e.tensor_tensor(X[:, 0, :], T1[:, 0, :], T2[:, 1, :], ALU.add),
                             [r] + ybuf.take())
                r2 = pool.op(lambda e: e.tensor_tensor(X[:, 1, :], T1[:, 1, :], T2[:, 0, :], ALU.subtract), [r])
                mg = SM[:, 1, 4 * J + jj:4 * J + jj + 1].to_broadcast([P, 256])
                for a in range(2):
                    r = dve.op(lambda e, a=a, mg=mg: e.tensor_tensor_scan(G[:, a, :], mg, X[:, a, :], 0.0, ALU.mult,
                                                                          ALU.add), [(r1, r2)[a]])
                dve.op(lambda e, c=c: e.tensor_tensor(T1, G, c, ALU.mult), [r])
                r = dve.op(lambda e, s=s: e.tensor_tensor(T2, G, s, ALU.mult), [r])
                tab.put(r)
                r1 = pool.op(lambda e: e.tensor_tensor(H[:, 0, :], T1[:, 0, :], T2[:, 1, :], ALU.subtract), [r])
                r2 = pool.op(lambda e: e.tensor_tensor(H[:, 1, :], T1[:, 1, :], T2[:, 0, :], ALU.add), [r])
                tb1.put(r2)
                for ri in range(2):
                    r = pe.op(lambda e, ri=ri, jj=jj: e.matmul(
                        yb.ap[:, 0:256], CR[:, ri, P * jj:P * jj + P], H[:, ri, :],
                        start=(jj == 0 and ri == 0), stop=(jj == 3 and ri == 1)), [r1, r2, tcr] + fy, inc=(ri == 1))
                ybuf.put(r)
                if jj in (1,):
                    fill()
            crf.put(r)
            if J + 2 < 4:
                phase_table(J + 2)
            r = dve.op(lambda e, J=J: e.scalar_tensor_tensor(
                out=zin[:, J, :], in0=uT[:, J, :], scalar=gcol[:, 108 + J:109 + J], in1=yb.ap[:, 0:256], op0=ALU.mult,
                op1=ALU.add), [r] + snap2)
            yb.put(r)
            rz.append(r)
        rz2 = []
        for J in range(4):
            rz2.append(act.op(lambda e, J=J: e.activation(zin[:, J, :], zin[:, J, :], ACT.Gelu_apprx_tanh), [rz[J]]))
        drain_fill()
        gated(lambda kt, t: oT[:, kt, t * P:(t + 1) * P], 4, v("w_o_swa_2")[0], outa, 0)
        pairs = []
        for half in (1, 0):
            pairs.append(gemm_T(lambda kt: zin[:, kt, :], 4, v("w_glu_2")[0], [(512 * half, 512)], rz2, mt4))
        zg = kT[:, 0:4, :]
        yin = qT[:, 4:8, :]
        ry = []
        for m in range(2):
            zs = zg[:, 2 * m:2 * m + 2, :].rearrange("p a b -> p (a b)")
            ys = yin[:, 2 * m:2 * m + 2, :].rearrange("p a b -> p (a b)")
            (p2, d2), (p1, d1) = pairs
            r = act.op(lambda e, zs=zs, m=m, p2=p2: e.activation(zs, p2[m].ap[:, :], ACT.Exp, scale=-1.0), [d2[m]] + snap2)
            p2[m].put(r)
            r = dve.op(lambda e, zs=zs: e.tensor_scalar(zs, zs, 1.0, None, ALU.add), [r])
            r = dve.op(lambda e, zs=zs: e.reciprocal(zs, zs), [r])
            r = dve.op(lambda e, zs=zs, ys=ys, m=m, p1=p1: e.tensor_tensor(ys, zs, p1[m].ap[:, :], ALU.mult),
                       [r, d1[m]] + snap2)
            p1[m].put(r)
            ry.append(r)
        gated(lambda kt, t: oT[:, 4 + kt, t * P:(t + 1) * P], 4, v("w_o_moba_2")[0], outm, 2)
        gated(lambda kt, t: yin[:, kt, t * P:(t + 1) * P], 4, v("w_o_ssm_2")[0], ry, 1)
        oTb.put(pe.last())
        outr = []
        fo = oTb.take()
        for c in range(2):
            for g in range(2):
                b = nextbank()
                fb = b.take()
                for i in range(2):
                    for t in range(2):
                        col = 512 * c + (2 * g + i) * P
                        r = pe.op(lambda e, i=i, t=t, col=col, b=b: e.transpose(
                            b.ap[:, (2 * i + t) * P:(2 * i + t + 1) * P], M[:, t, col:col + P], ident),
                            [mtok[(c, t)]] + fb, inc=(i == 1 and t == 1))
                k0 = 4 * c + 2 * g
                r2 = evac(oT[:, k0:k0 + 2, :].rearrange("p k t -> p (k t)"), b.ap[:, :], [r] + fo)
                b.put(r2)
                outr.append(r2)
        toks, pl = project_x(lambda kt, t: oT[:, kt, t * P:(t + 1) * P], 8, v("w_out_2")[0], outr, 1.0)
        return toks

    mready = []
    tm = mem_load()
    mready[:] = norm_T(M, tm, 3 * 8, mTb)
    mfree.append(pe.last())
    trope = trig_prep()
    phase_table(0)
    phase_table(1)
    mem_read.append(pool.last())
    tok, fsnap = ffn(tx, 0, v("ffn1_w_in")[0], v("ffn1_w_out")[0], 2816, True, 0.5)
    tok, kvout, KG = even_mixer(tok)
    tok = cross_attention(tok, 0, kvout, KG)
    tm = mem_load()
    mready[:] = norm_T(M, tm, (5 + 3) * 8, mTb)
    tok, _ = ffn(tok, 4 * 8, v("ffn2_w_in")[0], v("ffn2_w_out")[0], 2816, True, 0.5)
    tok, _ = ffn(tok, 5 * 8, v("ffn1_w_in")[1], v("ffn1_w_out")[1], 2816, True, 0.5)
    tok, kvout, KG = odd_mixer(tok)
    tok = cross_attention(tok, 1, kvout, KG)
    tok, _ = ffn(tok, (5 + 4) * 8, v("ffn2_w_in")[1], v("ffn2_w_out")[1], 2816, True, 0.5)
    tok = second_mixer(tok)
    tok, _ = ffn(tok, 88, v("w_ff1_2")[0], v("w_ff2_2")[0], 4096, False, 1.0)
    fsn = snapshot()
    tgf = dma(pool, M[:, 0, :], bc_rows(v("norm_final_2"), 1024), "gf", fsn)
    r, tr = row_rstd(x, tok)
    ends = []
    for t in range(2):
        rr = dve.op(lambda e, t=t: e.scalar_tensor_tensor(out=O[:, t, :], in0=x[:, t, :], scalar=r[:, t:t + 1],
                                                          in1=M[:, 0, :], op0=ALU.mult, op1=ALU.mult),
                    [tr, tgf] + fsn)
        ends.append(dma(sp, v("out").rearrange("b (t p) d -> t p (b d)", p=P)[t], O[:, t, :], f"out{t}", [rr]))
    sp.wait(ends)


NAMES = ['x', 'mem', 'positions', 'ln_gains', 'ffn1_w_in', 'ffn1_w_out', 'ffn2_w_in', 'ffn2_w_out', 'even_w_in',
         'even_f_bias', 'even_qk_gains', 'even_lambda', 'even_subln_gain', 'even_w_out', 'odd_w_in', 'odd_conv_w',
         'odd_qk_gains', 'odd_rel_bias', 'odd_w_out', 'x_w_q', 'x_w_kv', 'x_qk_gains', 'x_w_o', 'norm_mix_2', 'w_in_2',
         'sinks_2', 'lam_re_2', 'lam_im_2', 'log_step_2', 'b_re_2', 'b_im_2', 'c_re_2', 'c_im_2', 'd_skip_2',
         'w_glu_2', 'w_o_swa_2', 'w_o_ssm_2', 'w_o_moba_2', 'w_out_2', 'norm_ffn_2', 'w_ff1_2', 'w_ff2_2',
         'norm_final_2']


def kernel(**inputs):
    import concourse.bacc as bacc
    from concourse.bass_utils import run_bass_kernel_spmd as run

    nc = bacc.Bacc("TRN2", target_bir_lowering=False, num_devices=1)
    arrays, D = {}, {}

    def give(name, a):
        a = np.ascontiguousarray(a)
        arrays["in_" + name] = a
        D[name] = nc.dram_tensor("in_" + name, a.shape, mybir.dt.from_np(a.dtype), kind="ExternalInput").ap()

    for name in NAMES:
        if name == 'odd_rel_bias':
            tab = np.asarray(inputs[name])[0]
            give("rel", np.concatenate([np.repeat(tab[:, 256:257], 127, 1), tab[:, ::-1],
                                        np.repeat(tab[:, 0:1], 128, 1)], 1))
        else:
            give(name, np.asarray(inputs[name]))
    give("consts", build_consts())
    give("alibi", build_alibi())
    D["out"] = nc.dram_tensor("out", (1, 256, 1024), F32, kind="ExternalOutput").ap()
    build(nc, D)
    r = run(nc, [arrays], core_ids=[0])
    return np.asarray(r.results[0]["out"])
```

```python
import math
from contextlib import ExitStack

import numpy as np
import concourse.bass as bass
from concourse import mybir

F32 = mybir.dt.float32
F32R = mybir.dt.float32r
I32 = mybir.dt.int32
ALU = mybir.AluOpType
ACT = mybir.ActivationFunctionType
AX = mybir.AxisListType.X
P = 128
NEG = -1.0e30
TWO_PI = 2.0 * math.pi
MAGIC = 12582912.0
ROPE_INV = [float.fromhex(v) for v in (
    "0x1.0000000000000p+0", "0x1.8d275e0000000p-3", "0x1.3411900000000p-5", "0x1.ddee9c0000000p-8",
    "0x1.72ba440000000p-10", "0x1.1f91f00000000p-12", "0x1.be21880000000p-15", "0x1.5a0f4e0000000p-17")]
SLOT = 1024
NRAW = 4
NSPLIT = 3


def pieces_of_two_pi():
    out, rest = [], TWO_PI
    for k in range(4):
        if k == 3:
            out.append(float(np.float32(rest)))
            break
        m, e = math.frexp(rest)
        part = math.ldexp(math.floor(m * 4096.0), e - 12)
        out.append(part)
        rest -= part
    return out


CONST_N = 904 + 128


def build_consts():
    c = np.zeros((P, CONST_N), np.float32)
    i = np.arange(P)
    c[:, 0:128] = np.eye(P)
    c[:, 128:256] = (i[:, None] <= i[None, :])
    c[:, 256:384] = 1.0
    c[:, 512:640] = np.where(i[:, None] >= i[None, :], 0.0, NEG)
    c[:, 768:896] = np.where(i[:, None] // 64 >= i[None, :] // 64, 0.0, NEG)
    c[:, 896:904] = np.asarray(ROPE_INV, np.float32)
    c[:, 904:1032] = np.eye(P)[::-1]
    return c


def build_alibi():
    slopes = (2.0 ** (-8.0 * np.arange(1, 17) / 16)).astype(np.float32)
    dist = (128 + np.arange(P)[:, None] - np.arange(256)[None, :])
    df = dist.astype(np.float32)
    out = np.zeros((2, P, 8, 256), np.float32)
    for h in range(8):
        out[0, :, h] = np.where((dist >= 0) & (dist < 128), -slopes[h] * df, NEG)
        out[1, :, h] = np.where(dist >= 0, -slopes[8 + h] * df, NEG)
    return out


class Buf:

    def __init__(self, ap):
        self.ap = ap
        self.free = []

    def take(self):
        out, self.free = self.free, []
        return out

    def put(self, *toks):
        self.free += toks


class Rot:
    def __init__(self, aps):
        self.bufs = [Buf(a) for a in aps]
        self.n = 0

    def next(self):
        b = self.bufs[self.n % len(self.bufs)]
        self.n += 1
        return b


class Queue:

    def __init__(self, eng, sem):
        self.eng, self.sem, self.count, self.seen = eng, sem, 0, {}

    def wait(self, toks):
        for t in toks:
            if t is None:
                continue
            if isinstance(t, list):
                self.wait(t)
                continue
            sem, value = t
            if self.seen.get(id(sem), 0) < value:
                self.seen[id(sem)] = value
                self.eng.wait_ge(sem, value)

    def op(self, fn, after=(), inc=True):
        self.wait(after)
        ins = fn(self.eng)
        if not inc:
            return None
        self.count += 1
        ins.then_inc(self.sem, 1)
        return (self.sem, self.count)

    def last(self):
        return (self.sem, self.count) if self.count else None


def build(nc, D, plan):
    with ExitStack() as ctx:
        return build_in(nc, D, ctx, plan)


def build_in(nc, D, ctx, plan):
    def sb(name, shape, dt=F32):
        return ctx.enter_context(nc.sbuf_tensor(name, shape, dt))

    def newsem(name):
        return ctx.enter_context(nc.semaphore(name))

    pe = Queue(nc.tensor, newsem("s_pe"))
    act = Queue(nc.scalar, newsem("s_act"))
    dve = Queue(nc.vector, newsem("s_dve"))
    pool = Queue(nc.gpsimd, newsem("s_pool"))
    sp = Queue(nc.sync, newsem("s_sp"))
    dsem = {}

    def dma(q, out, in_, name, after=()):
        if name not in dsem:
            dsem[name] = [newsem("d_" + name), 0]
        d = dsem[name]
        d[1] += 16
        q.wait(after)
        q.eng.dma_start(out, in_).then_inc(d[0], 16)
        return (d[0], d[1])

    def snapshot():
        return [q.last() for q in (pe, act, dve, pool)]

    raw = [sb(f"raw{i}", [P, SLOT]) for i in range(NRAW)]
    whi = [sb(f"whi{i}", [P, SLOT], F32R) for i in range(NSPLIT)]
    wlo = [sb(f"wlo{i}", [P, SLOT], F32R) for i in range(NSPLIT)]
    x = sb("x", [P, 2, 1024])
    hT = [sb(f"hT{i}", [P, 8, 256], F32R) for i in range(2)]
    oT = [sb(f"oT{i}", [P, 8, 256], F32R) for i in range(2)]
    mT = [sb(f"mT{i}", [P, 8, 256], F32R) for i in range(2)]
    R1 = sb("R1", [P, 8192])
    S_rot = Rot([R1[:, 512 * i:512 * i + 512] for i in range(4)])
    pT_rot = Rot([R1[:, 2048 + 512 * i:2560 + 512 * i] for i in range(4)])
    qT = R1[:, 4096:6144].rearrange("p (k t) -> p k t", k=8)
    kT = R1[:, 6144:8192].rearrange("p (k t) -> p k t", k=8)
    R2 = sb("R2", [P, 4096])
    xkT = R2[:, 0:2048].rearrange("p (k t) -> p k t", k=8)
    xv = R2[:, 2048:4096].rearrange("p (t n) -> p t n", t=2)
    vsb = sb("vsb", [P, 2, 512])
    O = sb("O", [P, 2, 1024])
    M = sb("M", [P, 2, 1024])
    cumT = M[0:8, 0, 512:1024].rearrange("p (a n) -> p a n", a=2)
    biasA = sb("biasA", [P, 8, 256])
    biasB = sb("biasB", [P, 8, 256])
    gates = [xkT.rearrange("p k t -> p (k t)").rearrange("p (t n) -> p t n", t=2), xv, O[:, :, :]]
    fs_rot = Rot([biasA[:, 2 * i:2 * i + 2, :].rearrange("p a b -> p (a b)") for i in range(4)])
    fa_rot = Rot([biasB[:, 2 * i:2 * i + 2, :].rearrange("p a b -> p (a b)") for i in range(4)])
    sqj_rot = Rot([sb(f"sqj{i}", [P, 512])[:, :] for i in range(2)])
    cst = sb("cst", [P, CONST_N])
    gcol = sb("gcol", [P, 112])
    rows = sb("rows", [112, P])
    st = sb("st", [P, 1700])
    evg = sb("evg", [P, 4, 64])
    odg = sb("odg", [P, 2, 64])
    xg = sb("xg", [P, 2, 256])
    sublng = sb("sublng", [P, 128])
    lamp = sb("lamp", [P, 4, 64])
    fbias = sb("fbias", [8, 1])
    sinkb = sb("sinkb", [P, 8])
    posr = R1[0:2, 2048:2176].bitcast(I32)
    posf = R1[0:2, 2176:2304]
    ssr = R1[0:16, 2304:2688].rearrange("p (a n) -> p a n", a=3)
    lsr = R1[0:16, 2688:2690]
    rope = sb("rope", [P, 2, 2, 8])
    rtmp_rot = Rot([sb(f"rtmp{i}", [P, 4, 8, 8])[:, :, :, :] for i in range(1)])
    SM = sb("SM", [P, 8, 16])
    BT = sb("BT", [P, 2, 4, 128])
    CR = biasA[:, :, :].rearrange("p (c r a) n -> p c r (a n)", c=2, r=2)
    BL = R2[:, 0:1024].rearrange("p (r j h) -> p r j h", r=2, h=32)
    CL = [b.ap.rearrange("p (j n) -> p j n", j=4) for b in sqj_rot.bufs]
    early = [qT, kT]
    pq0 = [a.rearrange("p (r j) n -> p r j n", r=2) for a in early]
    pq = [M[:, :, :].rearrange("p r (j n) -> p r j n", j=4), pq0[1]]
    spill = nc.dram_tensor("phases", (4, P, 2048), F32, kind="Internal").ap()
    tabs = vsb[:, :, :].rearrange("p a (j n) -> p a j n", j=4)
    uT = vsb[:, :, :].rearrange("p a n -> p (a n)").rearrange("p (k t) -> p k t", k=4)

    banks = [Buf(ctx.enter_context(nc.psum_tensor(f"b{i}", [P, 512], F32))) for i in range(8)]
    gpair = [(banks[0], banks[1]), (banks[2], banks[3])]
    gcount = [0]
    tb = [banks[4], banks[5], banks[6]]
    tcount = [0]
    ob = banks[7]

    def nextbank():
        tcount[0] += 1
        return tb[(tcount[0] - 1) % len(tb)]

    stn = [0]

    def stat(n):
        stn[0] += n
        assert stn[0] <= 1700, stn
        return st[:, stn[0] - n:stn[0]]

    ident = cst[:, 0:128]
    tri = cst[:, 128:256]
    ones = cst[:, 256:384]
    maskc = cst[:, 384:640]
    maskb = cst[:, 640:896]
    inv8 = cst[:, 896:904]
    flip = cst[:, 904:1032]

    def sel(h, n):
        return cst[0:8, h:h + 1].to_broadcast([8, n])

    def v(d):
        return D[d]

    def bc_rows(ap1d, n):
        return bass.AP(ap1d.tensor, ap1d.offset, [[0, P], [1, n]])

    tx = [[dma(sp, x[:, t, :], v("x").rearrange("b (t p) d -> t p (b d)", p=P)[t], f"x{t}")] * 2 for t in range(2)]
    tcst = dma(sp, cst[:, :], v("consts"), "cst")
    trow = [dma(sp, rows[0:80, :], v("ln_gains").rearrange("l j (k p) -> (l j k) p", p=P), "rows"),
            dma(sp, rows[80:88, :], v("norm_mix_2").rearrange("l (k p) -> (l k) p", p=P), "rows"),
            dma(sp, rows[88:96, :], v("norm_ffn_2").rearrange("l (k p) -> (l k) p", p=P), "rows"),
            dma(sp, rows[96:108, :], v("odd_conv_w").rearrange("o w (k p) -> (o w k) p", p=P), "rows"),
            dma(sp, rows[108:112, :], v("d_skip_2").rearrange("l (k p) -> (l k) p", p=P), "rows")][-1]
    tsm = [dma(pool, evg[:, :, :].rearrange("p a b -> p (a b)"), bc_rows(v("even_qk_gains"), 256), "sm"),
           dma(pool, odg[:, :, :].rearrange("p a b -> p (a b)"), bc_rows(v("odd_qk_gains"), 128), "sm"),
           dma(pool, sublng[:, :], bc_rows(v("even_subln_gain"), 128), "sm"),
           dma(pool, lamp[:, :, :].rearrange("p a b -> p (a b)"), bc_rows(v("even_lambda"), 256), "sm"),
           dma(pool, fbias[:, :], v("even_f_bias").rearrange("a b -> b a"), "sm"),
           dma(pool, sinkb[:, :], bc_rows(v("sinks_2"), 8), "sm"),
           dma(pool, posr[:, :], v("positions").rearrange("b (t p) -> (b t) p", p=P), "sm"),
           dma(pool, ssr[:, 0, :], v("lam_re_2").rearrange("l (j a) p -> (l j) (a p)", a=2), "sm"),
           dma(pool, ssr[:, 1, :], v("lam_im_2").rearrange("l (j a) p -> (l j) (a p)", a=2), "sm"),
           dma(pool, lsr[:, :], v("log_step_2").rearrange("l (j a) -> (l j) a", a=2), "sm")][-1]
    tz = pool.op(lambda e: e.memset(BL[:, :, :, :], 0.0))
    for ri, nm in enumerate(("b_re_2", "b_im_2")):
        src = v(nm).rearrange("l (j a) p h -> a p (l j) h", a=2)
        for a in range(2):
            tbl = dma(pool, BL[64 * a:64 * a + 64, ri, :, 16 * a:16 * a + 16], src[a], "bl", [tz])
    order = []
    stage = dict(loaded=0, split=0, used=0)
    rawfree = [None] * NRAW
    spfree = [None] * NSPLIT
    loadtok, splittok = {}, {}

    def advance(upto):
        if plan is None:
            return
        while stage["split"] < min(upto + 1, len(plan)):
            j = stage["split"]
            while stage["loaded"] < min(j + NRAW, len(plan)):
                i = stage["loaded"]
                stage["loaded"] += 1
                name, l, k0, nk, pieces = plan[i]
                width = sum(w for _, w in pieces)
                dst = raw[i % NRAW][:, 0:nk * width].rearrange("p (k n) -> p k n", k=nk)
                off = 0
                for c0, w in pieces:
                    loadtok[i] = dma(sp, dst[:, :, off:off + w],
                                     v(name)[l, k0 * P:(k0 + nk) * P, c0:c0 + w].rearrange("(k p) n -> p k n", p=P),
                                     f"w{i % NRAW}", [rawfree[i % NRAW]])
                    off += w
            name, l, k0, nk, pieces = plan[j]
            n = nk * sum(w for _, w in pieces)
            r_, h_, l_ = raw[j % NRAW], whi[j % NSPLIT], wlo[j % NSPLIT]
            fr = [loadtok[j], spfree[j % NSPLIT]]
            rh = act.op(lambda e: e.activation(h_[:, 0:n], r_[:, 0:n], ACT.Copy), fr)
            rl = dve.op(lambda e: e.tensor_tensor(l_[:, 0:n], r_[:, 0:n], h_[:, 0:n].bitcast(F32), ALU.subtract),
                        fr + [rh])
            rawfree[j % NRAW] = rl
            splittok[j] = [rh, rl]
            stage["split"] += 1

    def piece(name, l, k0, nk, pieces):
        j = stage["used"]
        stage["used"] += 1
        entry = (name, l, k0, nk, tuple(pieces))
        order.append(entry)
        if plan is not None:
            assert plan[j] == entry, (plan[j], entry)
        advance(j + NSPLIT - 1)
        n = nk * sum(w for _, w in pieces)
        hi, lo = (a[j % NSPLIT][:, 0:n].rearrange("p (k n) -> p k n", k=nk) for a in (whi, wlo))
        return hi, lo, splittok.get(j, []), j

    def release(j, tok):
        spfree[j % NSPLIT] = tok

    def per_piece(width):
        return SLOT // width

    def products(bank_ap, a, b, start, stop, after, inc, skip=False):
        (ah, al), (bh, bl) = a, b
        pe.op(lambda e: e.matmul(bank_ap, ah, bh, start=start, stop=False, skip_group_check=skip), after, inc=False)
        pe.op(lambda e: e.matmul(bank_ap, ah, bl, start=False, stop=False, skip_group_check=skip), inc=False)
        return pe.op(lambda e: e.matmul(bank_ap, al, bh, start=False, stop=stop, skip_group_check=skip), inc=inc)

    def nextpair():
        gcount[0] += 1
        return gpair[(gcount[0] - 1) % 2]

    def at(ready, kt, KT):
        return [ready[kt * len(ready) // KT]]

    def gemm(*args):
        for got in gemm_steps(*args):
            if got:
                return got

    def gemm_steps(lhs, KT, W, pieces, lhs_ready, pair=None, middle=None):
        pair = pair or nextpair()
        width = sum(w for _, w in pieces)
        first = pair[0].take() + pair[1].take()
        done = [None, None]
        for k0 in range(0, KT, per_piece(max(width, 256))):
            nk = min(per_piece(max(width, 256)), KT - k0)
            hi, lo, tok, j = piece(W[0], W[1], k0, nk, pieces)
            if k0 and middle:
                middle()
                middle = None
            for kk in range(nk):
                kt = k0 + kk
                for t in range(2):
                    last = kt == KT - 1 or (kk == nk - 1 and t == 1)
                    r = products(pair[t].ap[:, 0:width], lhs(kt, t), (hi[:, kk, :], lo[:, kk, :]), kt == 0,
                                 kt == KT - 1, tok + first + at(lhs_ready, kt, KT), last)
                    first = []
                    if kt == KT - 1:
                        done[t] = r
            release(j, r)
            yield (pair, done) if k0 + nk == KT else None

    def gemm_T(rhs, KT, W, pieces, rhs_ready, mtiles=4):
        pair = nextpair()
        first = pair[0].take() + pair[1].take()
        done = [None, None]
        width = sum(w for _, w in pieces)
        for k0 in range(0, KT, per_piece(width)):
            nk = min(per_piece(width), KT - k0)
            hi, lo, tok, j = piece(W[0], W[1], k0, nk, pieces)
            for kk in range(nk):
                kt = k0 + kk
                for m in range(mtiles):
                    cs = slice(P * m, P * m + P)
                    r = products(pair[m // 2].ap[:, 256 * (m % 2):256 * (m % 2) + 256], (hi[:, kk, cs], lo[:, kk, cs]),
                                 rhs(kt), kt == 0 and m % 2 == 0, kt == KT - 1, tok + first + at(rhs_ready, kt, KT),
                                 kt == KT - 1 or (kk == nk - 1 and m == mtiles - 1), True)
                    first = []
                    if kt == KT - 1:
                        done[m // 2] = r
            release(j, r)
        return pair, done

    def rsqrt(src, n, after):
        y, t = stat(n), stat(n)
        yi, ti = y.bitcast(I32), t.bitcast(I32)
        r = dve.op(lambda e: e.tensor_scalar(ti, src.bitcast(I32), 1, None, ALU.logical_shift_right), after)
        r = dve.op(lambda e: e.tensor_scalar(yi, ti, -1.0, 1597463007.0, ALU.mult, ALU.add), [r])
        for _ in range(3):
            r = dve.op(lambda e: e.tensor_tensor(t, y, y, ALU.mult), [r])
            r = dve.op(lambda e: e.scalar_tensor_tensor(out=t, in0=t, scalar=-0.5, in1=src, op0=ALU.mult,
                                                        op1=ALU.mult), [r])
            r = dve.op(lambda e: e.scalar_tensor_tensor(out=y, in0=t, scalar=1.5, in1=y, op0=ALU.add,
                                                        op1=ALU.mult), [r])
        return y, r

    def rstd(ss, n, count, after):
        ms = stat(n)
        r = dve.op(lambda e: e.tensor_scalar(ms, ss, 1.0 / count, 1e-6, ALU.mult, ALU.add), after)
        return rsqrt(ms, n, [r])

    def row_rstd(src, ready):
        ss = stat(4).rearrange("p (t n) -> p t n", t=2)
        ms = stat(2)
        fx = xnb.take()
        ra = []
        for t in range(2):
            for n in range(2):
                cs = slice(512 * n, 512 * n + 512)
                ra.append(act.op(lambda e: e.activation(O[:, t, cs], src[:, t, cs], ACT.Square,
                                                        accum_out=ss[:, t, n:n + 1]), [ready[t][n]] + fx))
        y, u, h = stat(2), stat(2), stat(2)
        yi, ui = y.bitcast(I32), u.bitcast(I32)
        r = dve.op(lambda e: e.tensor_tensor(ms, ss[:, :, 0], ss[:, :, 1], ALU.add), ra)
        r = dve.op(lambda e: e.tensor_scalar(ms, ms, 1.0 / 1024, 1e-6, ALU.mult, ALU.add), [r])
        rh = dve.op(lambda e: e.tensor_scalar(h, ms, -0.5, None, ALU.mult), [r])
        r = dve.op(lambda e: e.tensor_scalar(ui, ms.bitcast(I32), 1, None, ALU.logical_shift_right), [r])
        r = dve.op(lambda e: e.tensor_scalar(yi, ui, -1.0, 1597463007.0, ALU.mult, ALU.add), [r])
        r = [[r, rh]] * 2
        for _ in range(3):
            for t in range(2):
                yt, ut = y[:, t:t + 1], u[:, t:t + 1]
                r[t] = [dve.op(lambda e: e.scalar_tensor_tensor(out=ut, in0=yt, scalar=h[:, t:t + 1], in1=yt,
                                                                op0=ALU.mult, op1=ALU.mult), r[t])]
            for t in range(2):
                yt, ut = y[:, t:t + 1], u[:, t:t + 1]
                r[t] = [dve.op(lambda e: e.scalar_tensor_tensor(out=yt, in0=ut, scalar=1.5, in1=yt, op0=ALU.add,
                                                                op1=ALU.mult), r[t])]
        return y, r

    xnb = Buf(O)

    def halves(hi, lo, src, after, free=(), turn=0):
        if turn:
            r = dve.op(lambda e: e.tensor_copy(hi, src), list(after) + list(free))
        else:
            r = act.op(lambda e: e.activation(hi, src, ACT.Copy), list(after) + list(free))
        return dve.op(lambda e: e.tensor_tensor(lo, src, hi.bitcast(F32), ALU.subtract), [r] + list(free))

    def norm_rows(src, ready):
        y, r = row_rstd(src, ready)
        return [dve.op(lambda e: e.tensor_scalar(O[:, 0, :], src[:, 0, :], y[:, 0:1], None, ALU.mult), r[0]),
                act.op(lambda e: e.activation(O[:, 1, :], src[:, 1, :], ACT.Copy, scale=y[:, 1:2]), r[1])]

    def norm_turn(tn, g0, dst):
        fd = dst.take()
        out = []
        for g in range(4):
            b = nextbank()
            fb = b.take()
            for i in range(2):
                for t in range(2):
                    kt = 2 * g + i
                    r = pe.op(lambda e: e.transpose(b.ap[:, (2 * i + t) * P:(2 * i + t + 1) * P],
                                                    O[:, t, kt * P:(kt + 1) * P], ident), [tn[t], tgc] + fb,
                              inc=(i == 1 and t == 1))
            kts = [2 * g, 2 * g + 1]
            gain = [gcol[:, g0 + kt:g0 + kt + 1] for kt in kts]
            src = [b.ap[:, 256 * i:256 * i + 256] for i in range(2)]
            hi, lo = ([a[:, kt, :] for kt in kts] for a in dst.ap)
            for i in range(2):
                rh = act.op(lambda e: e.activation(hi[i], src[i], ACT.Copy, scale=gain[i]), [r] + fd)
            for i in range(2):
                out.append(dve.op(lambda e: e.scalar_tensor_tensor(out=lo[i], in0=src[i], scalar=gain[i],
                                                                   in1=hi[i].bitcast(F32), op0=ALU.mult,
                                                                   op1=ALU.subtract), [rh] + fd))
            b.put(out[-1])
        xnb.put(r)
        return out

    def norm_T(src, ready, g0, dst):
        return norm_turn(norm_rows(src, ready), g0, dst)

    evac_n = [0]

    def evac(dst, src, after, pick=None):
        evac_n[0] += 1
        if pick == "act" or (pick is None and evac_n[0] % 2):
            return act.op(lambda e: e.activation(dst, src, ACT.Copy), after)
        return dve.op(lambda e: e.tensor_copy(dst, src), after)

    def add_x(bank, t, n0, scale, tok):
        r = dve.op(lambda e: e.scalar_tensor_tensor(out=x[:, t, n0:n0 + 512], in0=bank.ap[:, :], scalar=scale,
                                                    in1=x[:, t, n0:n0 + 512], op0=ALU.mult, op1=ALU.add), [tok])
        bank.put(r)
        return r

    def both(T, k0=0):
        return lambda kt, t: tuple(a[:, k0 + kt, t * P:(t + 1) * P] for a in T)

    def flat(T, k0, n):
        return [a[:, k0:k0 + n, :].rearrange("p k t -> p (k t)") for a in T]

    def project_x(lhs, KT, W, ready, scale):
        toks = [[None] * 2 for _ in range(2)]
        for c in range(2):
            pair, done = gemm(lhs, KT, W, [(512 * c, 512)], ready)
            for t in range(2):
                toks[t][c] = add_x(pair[t], t, 512 * c, scale, done[t])
        return toks, pe.last()

    hTb = Buf(hT)
    oTb = Buf(oT)

    def ffn(xready, g0, l, names, F, gated, scale, between={}):
        hr = norm_T(x, xready, g0, hTb)
        snap = snapshot()
        per = 2 if gated else 4
        nch = F // (P * per)
        acc = banks[0:4]
        pair = (banks[4], banks[5])
        accfree = [b.take() for b in acc]
        aTfree = [oTb.take(), []]
        aTfree[1] = list(aTfree[0])
        tcnt = [0]
        made = {}

        def turn(c, toks, bufs):
            def go():
                out = []
                for g in range(per // 2):
                    b = banks[6 + tcnt[0] % 2]
                    tcnt[0] += 1
                    fb = b.take()
                    for i in range(2):
                        for t in range(2):
                            jj = 2 * g + i
                            r = pe.op(lambda e: e.transpose(
                                b.ap[:, (2 * i + t) * P:(2 * i + t + 1) * P], bufs[t].ap[:, jj * P:(jj + 1) * P], ident),
                                [toks[t]] + fb, inc=(i == 1 and t == 1))
                    hi, lo = flat(oT, 4 * (c % 2) + 2 * g, 2)
                    r2 = halves(hi, lo, b.ap[:, :], [r], aTfree[c % 2])
                    b.put(r2)
                    out.append(r2)
                for t in range(2):
                    bufs[t].put(r)
                made[c] = out
            return go

        def output(c):
            nk = SLOT // 1024
            for k0 in range(0, per, nk):
                hi, lo, tok, j = piece(names[1], l, per * c + k0, nk, [(0, 1024)])
                for kk in range(nk):
                    kt = k0 + kk
                    for t in range(2):
                        for n in range(2):
                            ends = c == nch - 1 and kt == per - 1
                            cs = slice(512 * n, 512 * n + 512)
                            r = products(acc[2 * t + n].ap[:, :], both(oT, 4 * (c % 2))(kt, t),
                                         (hi[:, kk, cs], lo[:, kk, cs]), c == 0 and kt == 0, ends,
                                         tok + made[c] + (accfree[2 * t + n] if c == 0 and kt == 0 else []),
                                         ends or (kk == nk - 1 and t == 1 and n == 1))
                            if ends:
                                fin[2 * t + n] = r
                release(j, r)
            aTfree[c % 2] = [r]
        fin = [None] * 4
        middle = None
        for c in range(nch):
            pcs = [(256 * c, 256), (F + 256 * c, 256)] if gated else [(512 * c, 512)]
            _, done = gemm(both(hT), 8, (names[0], l), pcs, hr, pair, middle)
            toks, bufs = [], []
            for t in range(2):
                s, a = fs_rot.next(), fa_rot.next()
                if gated:
                    r = act.op(lambda e: e.activation(s.ap[:, 0:256], pair[t].ap[:, 0:256], ACT.Silu),
                               [done[t]] + s.take() + snap)
                    r = dve.op(lambda e: e.tensor_tensor(a.ap[:, 0:256], s.ap[:, 0:256], pair[t].ap[:, 256:512], ALU.mult),
                               [r] + a.take() + snap)
                else:
                    r = act.op(lambda e: e.activation(s.ap, pair[t].ap[:, :], ACT.Relu), [done[t]] + s.take() + snap)
                    r = dve.op(lambda e: e.tensor_tensor(a.ap, s.ap, s.ap, ALU.mult), [r] + a.take() + snap)
                pair[t].put(r)
                s.put(r)
                toks.append(r)
                bufs.append(a)
            if c:
                output(c - 1)
            middle = turn(c, toks, bufs)
            if c in between:
                tb[:] = banks[6:8]
                between[c]()
                tb[:] = banks[4:7]
        hTb.put(pe.last())
        middle()
        output(nch - 1)
        oTb.put(pe.last())
        toks = [[None] * 2 for _ in range(2)]
        for t in range(2):
            for n in range(2):
                toks[t][n] = add_x(acc[2 * t + n], t, 512 * n, scale, fin[2 * t + n])
        return toks

    fillers = []
    slices = []
    pending = []
    late = []

    def finish_late():
        while late:
            f, into = late.pop(0)
            into.append(f())

    def settle():
        finish_late()
        while pending:
            pending.pop(0)()

    def fill():
        settle()
        if slices:
            f = next(slices[0])
            if f:
                slices.pop(0)
                pending.append(f)
        elif fillers:
            pending.append(fillers.pop(0)())

    def drain_fill():
        while fillers or slices or pending:
            fill()
        finish_late()

    def head_prep(bank, tok, nh, hd, gain, dst, k0, t, rope_on=False, dstfree=()):
        w = nh * hd
        sq = sqj_rot.next()
        r = act.op(lambda e: e.activation(sq.ap[:, 0:w], bank.ap[:, 0:w], ACT.Square), [tok] + sq.take())
        ss = stat(nh)
        r = dve.op(lambda e: e.tensor_reduce(ss, sq.ap[:, 0:w].rearrange("p (h d) -> p h d", h=nh), AX, ALU.add), [r])
        rs, r = rstd(ss, nh, hd, [r])
        n3 = sq.ap[:, 0:w].rearrange("p (h d) -> p h d", h=nh)
        r = dve.op(lambda e: e.tensor_tensor(n3, bank.ap[:, 0:w].rearrange("p (h d) -> p h d", h=nh),
                                             rs.unsqueeze(2).to_broadcast([P, nh, hd]), ALU.mult), [r])
        bank.put(r)
        r = pool.op(lambda e: e.tensor_tensor(n3, n3, gain.unsqueeze(1).to_broadcast([P, nh, hd]), ALU.mult),
                    [r, tsm])
        if rope_on:
            tmp = rtmp_rot.next()
            ft = tmp.take()
            q = tmp.ap
            x1, x2 = n3[:, :, 0:8], n3[:, :, 8:16]
            cb = rope[:, 0, t, :].unsqueeze(1).to_broadcast([P, nh, 8])
            sb_ = rope[:, 1, t, :].unsqueeze(1).to_broadcast([P, nh, 8])
            rr = [dve.op(lambda e, i=i, a=a, b=b: e.tensor_tensor(q[:, i, :, :], a, b, ALU.mult), [r, tg["rope"]] + ft)
                  for i, (a, b) in enumerate(((x1, cb), (x2, sb_), (x2, cb), (x1, sb_)))][-1]
            dve.op(lambda e: e.tensor_tensor(x1, q[:, 0, :, :], q[:, 1, :, :], ALU.subtract), [rr])
            r = dve.op(lambda e: e.tensor_tensor(x2, q[:, 2, :, :], q[:, 3, :, :], ALU.add), [rr])
            tmp.put(r)
        nt = w // P

        def finish():
            b = nextbank()
            fb = b.take()
            for i in range(nt):
                r2 = pe.op(lambda e, i=i: e.transpose(b.ap[:, i * P:(i + 1) * P], sq.ap[:, i * P:(i + 1) * P], ident),
                           [r, tgc] + fb, inc=(i == nt - 1))
            r3 = evac(dst[:, k0:k0 + nt, t * P:(t + 1) * P], b.ap[:, 0:nt * P].rearrange("p (k n) -> p k n", k=nt),
                      [r2] + list(dstfree))
            b.put(r3)
            sq.put(r2)
            return r3
        return finish

    def softmax_group(s, nh, nk, tok, sink=None):
        s3 = s.ap[:, 0:nh * nk].rearrange("p (h k) -> p h k", h=nh)
        nm, sm = stat(nh), stat(nh)
        if sink is None:
            r = dve.op(lambda e: e.tensor_reduce(nm, s3, AX, ALU.max, negate=True), [tok])
        else:
            mx = stat(nh)
            r = dve.op(lambda e: e.tensor_reduce(mx, s3, AX, ALU.max), [tok])
            r = dve.op(lambda e: e.tensor_tensor(mx, mx, sink, ALU.max), [r, tsm])
            r = dve.op(lambda e: e.tensor_scalar(nm, mx, -1.0, None, ALU.mult), [r])
        for i in range(nh):
            r2 = act.op(lambda e, i=i: e.activation(s3[:, i, :], s3[:, i, :], ACT.Exp, bias=nm[:, i:i + 1],
                                                    accum_out=sm[:, i:i + 1]), [r])
        if sink is not None:
            es = stat(nh)
            r = dve.op(lambda e: e.tensor_tensor(es, sink, nm, ALU.add), [r])
            r = act.op(lambda e: e.activation(es, es, ACT.Exp), [r])
            r2 = dve.op(lambda e: e.tensor_tensor(sm, sm, es, ALU.add), [r, r2])
        return r2, sm

    def p_transposed(s, nh, nkt, tok):
        b = nextbank()
        fb = b.take()
        n = nh * nkt
        for i in range(n):
            r = pe.op(lambda e, i=i: e.transpose(b.ap[:, i * P:(i + 1) * P], s.ap[:, i * P:(i + 1) * P], ident),
                      [tok] + fb, inc=(i == n - 1))
        s.put(r)
        pt = pT_rot.next()
        r = evac(pt.ap[:, 0:n * P], b.ap[:, 0:n * P], [r] + pt.take())
        b.put(r)
        return pt, r

    def staged(work, score, finish, heads_at=None):
        scored, turned = [], []

        def turn():
            item, (s, r) = scored.pop(0)
            nh = 2 if heads_at is None else len(item[heads_at])
            turned.append((item, p_transposed(s, nh, 2 if heads_at is None else item[0] + 1, r)))

        def close():
            item, (pt, r) = turned.pop(0)
            finish(*item, pt, r)
        for item in work:
            scored.append((item, score(*item)))
            fill()
            if len(scored) == 2:
                turn()
            if len(turned) == 2:
                close()
        turn()
        close()
        fill()
        close()

    def head_attention(q_at, k_at, v_at, ready_qk, ready_v, bias_at, snap, out_cols, sink=None, kfirst=None):
        work = []
        for t in range(2):
            per = 4 if t == 0 else 2
            for a in range(0, 4, per):
                for par in range(2):
                    work.append((t, [2 * (a + i) + par for i in range(per)]))
        state = {}
        otoks = [None, None]
        rsum = [stat(8), stat(8)]
        left = [8, 8]
        sumtok = [[], []]

        def score(t, heads):
            nk = P * (t + 1)
            nh = len(heads)
            b = nextbank()
            fb = b.take()
            for i, h in enumerate(heads):
                r = pe.op(lambda e, i=i, h=h: e.matmul(b.ap[:, i * nk:(i + 1) * nk], q_at(h, t), k_at(h, nk),
                                                       start=True, stop=True), list(ready_qk) + fb, inc=(i == nh - 1))
            s = S_rot.next()
            s3 = s.ap[:, 0:nh * nk].rearrange("p (h k) -> p h k", h=nh)
            bias, tbias = bias_at(heads, t)
            r = dve.op(lambda e: e.scalar_tensor_tensor(
                out=s3, in0=b.ap[:, 0:nh * nk].rearrange("p (h k) -> p h k", h=nh), scalar=0.125, in1=bias,
                op0=ALU.mult, op1=ALU.add), [r] + tbias + s.take() + snap)
            b.put(r)
            sk = None if sink is None else sink[:, heads[0]:heads[-1] + 1:2]
            r, sm = softmax_group(s, nh, nk, r, sk)
            r2 = dve.op(lambda e: e.reciprocal(rsum[t][:, heads[0]:heads[-1] + 1:2], sm), [r])
            sumtok[t].append(r2)
            return s, r

        def finish(t, heads, pt, r):
            nkt = t + 1
            fo = ob.take()
            for i, h in enumerate(heads):
                for kt in range(nkt):
                    r2 = pe.op(lambda e, i=i, h=h, kt=kt: e.matmul(
                        ob.ap[:, 64 * h:64 * h + 64], pt.ap[:, (i * nkt + kt) * P:(i * nkt + kt + 1) * P],
                        v_at(h, kt), start=(kt == 0), stop=(kt == nkt - 1)), [r] + list(ready_v) + fo,
                        inc=(i == len(heads) - 1 and kt == nkt - 1))
            pt.put(r2)
            left[t] -= len(heads)
            if left[t] == 0:
                r3 = dve.op(lambda e: e.tensor_tensor(
                    O[:, t, out_cols:out_cols + 512].rearrange("p (h d) -> p h d", h=8),
                    ob.ap[:, :].rearrange("p (h d) -> p h d", h=8),
                    rsum[t].unsqueeze(2).to_broadcast([P, 8, 64]), ALU.mult), [r2] + sumtok[t] + ofree)
                ob.put(r3)
                otoks[t] = r3

        ofree = xnb.take()
        xnb.put(*ofree)
        staged(work, score, finish, 1)
        return otoks

    def transpose_out(src_cols, k0, toks, oT_free):
        out = []
        for g in range(2):
            b = nextbank()
            fb = b.take()
            for i in range(2):
                for t in range(2):
                    c = src_cols + (2 * g + i) * P
                    r = pe.op(lambda e, i=i, t=t, c=c, b=b: e.transpose(
                        b.ap[:, (2 * i + t) * P:(2 * i + t + 1) * P], O[:, t, c:c + P], ident),
                        [toks[t]] + fb, inc=(i == 1 and t == 1))
            hi, lo = flat(oT, k0 + 2 * g, 2)
            r2 = halves(hi, lo, b.ap[:, :], [r], oT_free)
            b.put(r2)
            out.append(r2)
        xnb.put(r)
        return out

    tg = {}
    b0 = nextbank()
    r = pe.op(lambda e: e.transpose(b0.ap[:, 0:112], rows[:, :], cst[0:112, 0:112]), [tcst, trow])
    tgc = dve.op(lambda e: e.tensor_copy(gcol[:, :], b0.ap[:, 0:112]), [r])
    b0.put(tgc)

    def trig_prep():
        r = dve.op(lambda e: e.tensor_copy(posf[:, :], posr[:, :]), [tsm])
        r0 = dve.op(lambda e: e.tensor_copy(ssr[:, 2, :].rearrange("p (a n) -> p a n", a=2),
                                            lsr[:, :].unsqueeze(2).to_broadcast([16, 2, 64])), [tsm])
        b = nextbank()
        fb = b.take()
        pe.op(lambda e: e.transpose(b.ap[:, 0:2], posf[:, :], cst[0:2, 0:2]), [r, tcst] + fb, inc=False)
        for i in range(3):
            r = pe.op(lambda e, i=i: e.transpose(b.ap[:, 16 + 16 * i:32 + 16 * i], ssr[:, i, :], cst[0:16, 0:16]),
                      [r0], inc=(i == 2))
        ang = stat(32)
        raw = stat(64)
        dve.op(lambda e: e.tensor_copy(raw[:, 0:2], b.ap[:, 0:2]), [r])
        r = dve.op(lambda e: e.tensor_copy(raw[:, 16:64], b.ap[:, 16:64]), [r])
        b.put(r)
        rdt = act.op(lambda e: e.activation(SM[:, 0, :], raw[:, 48:64], ACT.Exp), [r])
        lr, li = raw[:, 16:32], raw[:, 32:48]
        for t in range(2):
            r = dve.op(lambda e, t=t: e.tensor_scalar(ang[:, 8 * t:8 * t + 8], inv8, raw[:, t:t + 1], None, ALU.mult),
                       [r])
        r = dve.op(lambda e: e.tensor_tensor(ang[:, 16:32], li, SM[:, 0, :], ALU.mult), [r, rdt])
        k, kh, kl, pk = stat(32), stat(32), stat(32), pieces_of_two_pi()
        r = dve.op(lambda e: e.tensor_scalar(k, ang, 1.0 / TWO_PI, MAGIC, ALU.mult, ALU.add), [r])
        r = dve.op(lambda e: e.tensor_scalar(k, k, MAGIC, None, ALU.subtract), [r])
        r = dve.op(lambda e: e.tensor_scalar(kh, k, 1.0 / 2048, MAGIC, ALU.mult, ALU.add), [r])
        r = dve.op(lambda e: e.tensor_scalar(kh, kh, MAGIC, 2048.0, ALU.subtract, ALU.mult), [r])
        r = dve.op(lambda e: e.tensor_tensor(kl, k, kh, ALU.subtract), [r])
        for kk, pp in ((kh, pk[0]), (kl, pk[0]), (kh, pk[1]), (kl, pk[1]), (kh, pk[2]), (kl, pk[2]), (k, pk[3])):
            r = dve.op(lambda e, kk=kk, pp=pp: e.scalar_tensor_tensor(out=ang, in0=kk, scalar=-pp, in1=ang,
                                                                      op0=ALU.mult, op1=ALU.add), [r])
        lim = 3.1415925
        r = dve.op(lambda e: e.tensor_scalar(ang, ang, lim, -lim, ALU.min, ALU.max), [r])
        na = stat(32)
        r2 = dve.op(lambda e: e.tensor_scalar(na, ang, -1.0, None, ALU.mult), [r])
        r2 = dve.op(lambda e: e.tensor_tensor(na, na, ang, ALU.min), [r2])
        r2 = dve.op(lambda e: e.tensor_scalar(na, na, math.pi / 2, None, ALU.add), [r2])
        sn, cs = stat(32), stat(32)
        r1 = act.op(lambda e: e.activation(sn, ang, ACT.Sin), [r])
        r2 = act.op(lambda e: e.activation(cs, na, ACT.Sin), [r2])
        r = dve.op(lambda e: e.tensor_copy(rope[:, 0, :, :].rearrange("p a b -> p (a b)"), cs[:, 0:16]), [r2])
        tro = dve.op(lambda e: e.tensor_copy(rope[:, 1, :, :].rearrange("p a b -> p (a b)"), sn[:, 0:16]), [r1])
        dve.op(lambda e: e.tensor_copy(SM[:, 2, :], cs[:, 16:32]))
        dve.op(lambda e: e.tensor_copy(SM[:, 3, :], sn[:, 16:32]))
        w = [stat(16) for _ in range(6)]
        r = dve.op(lambda e: e.tensor_tensor(w[0], lr, SM[:, 0, :], ALU.mult), [rdt])
        rm = act.op(lambda e: e.activation(SM[:, 1, :], w[0], ACT.Exp), [r])

        def tt(o, a, b_, op, after):
            return dve.op(lambda e: e.tensor_tensor(o, a, b_, op), after)
        r = tt(w[0], SM[:, 1, :], SM[:, 2, :], ALU.mult, [rm, dve.last()])
        r = dve.op(lambda e: e.tensor_scalar(w[0], w[0], -1.0, None, ALU.add), [r])
        tt(w[1], SM[:, 1, :], SM[:, 3, :], ALU.mult, [])
        tt(w[2], lr, lr, ALU.mult, [])
        r = tt(w[3], li, li, ALU.mult, [])
        r = tt(w[2], w[2], w[3], ALU.add, [r])
        rd = dve.op(lambda e: e.reciprocal(w[2], w[2]), [r])
        r = tt(w[3], w[0], lr, ALU.mult, [rd])
        r = tt(w[4], w[1], li, ALU.mult, [])
        r = tt(w[3], w[3], w[4], ALU.add, [r])
        r = tt(SM[:, 4, :], w[3], w[2], ALU.mult, [r])
        r = tt(w[4], w[1], lr, ALU.mult, [r])
        r = tt(w[5], w[0], li, ALU.mult, [])
        r = tt(w[4], w[4], w[5], ALU.subtract, [r])
        tf = tt(SM[:, 5, :], w[4], w[2], ALU.mult, [r])
        tg["sm"] = tf
        return tro

    def input_matrices():
        tf = tg["sm"]

        def tt(o, a, b_, op, after):
            return dve.op(lambda e: e.tensor_tensor(o, a, b_, op), after)
        fre = SM[:, 4, :].unsqueeze(2).to_broadcast([P, 16, 32])
        fim = SM[:, 5, :].unsqueeze(2).to_broadcast([P, 16, 32])
        tA, tB, tC, tD = (R2[:, 1024 + 512 * i:1536 + 512 * i].rearrange("p (j h) -> p j h", h=32) for i in range(4))
        tt(tA, BL[:, 0, :, :], fre, ALU.mult, [tf, tbl])
        tt(tB, BL[:, 1, :, :], fim, ALU.mult, [])
        tt(tC, BL[:, 1, :, :], fre, ALU.mult, [])
        r = tt(tD, BL[:, 0, :, :], fim, ALU.mult, [])
        tt(BL[:, 0, :, :], tA, tB, ALU.subtract, [r])
        return tt(BL[:, 1, :, :], tC, tD, ALU.add, [r])

    def input_turn(r):
        for ri in range(2):
            b = nextbank()
            fb = b.take()
            for J in range(4):
                r2 = pe.op(lambda e, b=b, ri=ri, J=J: e.transpose(
                    b.ap[:, J * P:(J + 1) * P], BL[:, ri, 4 * J:4 * J + 4, :].rearrange("p j h -> p (j h)"), ident),
                    [r] + fb, inc=(J == 3))
            tbt = dve.op(lambda e, b=b, ri=ri: e.tensor_copy(BT[:, ri, :, :].rearrange("p J c -> p (J c)"), b.ap[:, :]),
                         [r2])
            b.put(tbt)
        tg["bt"] = tbt
        xkv.put(tbt)

    pqb = [Buf(p) for p in pq]
    ptab = {}
    spilled = {}

    def phase_table(J):
        t = pq0[J % 2]
        r = [pool.op(lambda e: e.tensor_copy(t[:, ri, :, 0:1], SM[:, 2 + ri, 4 * J:4 * J + 4].unsqueeze(2)),
                     [tg["sm"], spilled.get(J - 2)]) for ri in range(2)]
        n = 1
        while n < 256:
            c, s = t[:, 0, :, 0:n], t[:, 1, :, 0:n]
            cw = t[:, 0, :, n - 1:n].to_broadcast([P, 4, n])
            sw = t[:, 1, :, n - 1:n].to_broadcast([P, 4, n])
            u1, u2 = tabs[:, 0, :, 0:n], tabs[:, 1, :, 0:n]
            for out, (a, b_), op in ((0, (cw, sw), ALU.subtract), (1, (sw, cw), ALU.add)):
                ra = pool.op(lambda e: e.tensor_tensor(u1, c, a, ALU.mult), r)
                rb = pool.op(lambda e: e.tensor_tensor(u2, s, b_, ALU.mult), r)
                ro = pool.op(lambda e: e.tensor_tensor(t[:, out, :, n:2 * n], u1, u2, op), [ra, rb])
                r = [ro]
            n *= 2
        spilled[J] = dma(pool, spill[J], early[J % 2].rearrange("p k t -> p (k t)"), f"spill{J}", [ro])

    def load_table(J):
        src = spill[J].rearrange("p (r n) -> p r n", r=2)
        dst = M[:, :, :] if J % 2 == 0 else kT.rearrange("p (r j) n -> p r (j n)", r=2)
        ptab[J] = dma(pool, dst, src, f"tab{J % 2}", pqb[J % 2].take() + [spilled[J]])

    def mem_load():
        fr = xnb.take()
        tm = [dma(pool, M[:, t, :], v("mem").rearrange("b (t p) d -> t p (b d)", p=P)[t], "mem", fr + mfree[:])
              for t in range(2)]
        xnb.put(*fr)
        return [[tm[-1]] * 2] * 2

    mfree = []
    mTb = Buf(mT)
    xkv = Buf(None)

    def cross_kv_fillers(l):
        W = ("x_w_kv", l)
        xg_r = []
        out = {"k": [], "v": []}
        xkfree = xkv.take()
        txg = dma(pool, xg[:, :, :].rearrange("p a b -> p (a b)"), bc_rows(v("x_qk_gains")[l], 512), "xg", xgfree[:])

        def chunk(c):
            def start():
                pair, done = gemm(both(mT), 8, W, [(512 * c, 512)], mready[:])
                if c == 3:
                    mTb.put(pe.last())

                def consume():
                    for t in range(2):
                        if c < 2:
                            late.append((head_prep(pair[t], done[t], 2, 256, KG(1), xkT, 4 * c, t, dstfree=xkfree),
                                         out["k"]))
                        else:
                            r = evac(xv[:, t, 512 * (c - 2):512 * (c - 1)], pair[t].ap[:, :], [done[t]] + xkfree)
                            pair[t].put(r)
                            out["v"].append(r)
                return consume
            return start

        def KG(i):
            pool.wait([txg])
            return xg[:, i, :]
        fillers.extend([chunk(c) for c in range(4)])
        return out, KG

    xgfree = []

    def cross_attention(xready, l, kvout, KG):
        hr = norm_T(x, xready, (5 * l + 2) * 8, hTb)
        snap = snapshot()
        drain_fill()
        qr = []
        for c in range(2):
            pair, done = gemm(both(hT), 8, ("x_w_q", l), [(512 * c, 512)], hr)
            finish_late()
            for t in range(2):
                late.append((head_prep(pair[t], done[t], 2, 256, KG(0), qT, 4 * c, t, dstfree=snap), qr))
        finish_late()
        hTb.put(pe.last())
        xgfree.append(pool.last())
        ready = qr + kvout["k"]
        rs = [stat(4), stat(4)]
        otok = {}
        stoks = {}
        ofree = xnb.take()
        xnb.put(*ofree)

        def score(t, hp):
            b = nextbank()
            fb = b.take()
            for i in range(2):
                h = 2 * hp + i
                for c in range(2):
                    r = pe.op(lambda e, i=i, h=h, c=c: e.matmul(
                        b.ap[:, 256 * i:256 * i + 256], qT[:, 2 * h + c, t * P:(t + 1) * P], xkT[:, 2 * h + c, :],
                        start=(c == 0), stop=(c == 1)), ready + fb, inc=(i == 1 and c == 1))
            s = S_rot.next()
            r = act.op(lambda e: e.activation(s.ap, b.ap[:, :], ACT.Copy, scale=0.0625), [r] + s.take() + snap)
            b.put(r)
            r, sm = softmax_group(s, 2, 256, r)
            stoks[(t, hp)] = dve.op(lambda e: e.reciprocal(rs[t][:, 2 * hp:2 * hp + 2], sm), [r])
            return s, r

        def finish(t, hp, pt, r):
            fo = ob.take()
            for i in range(2):
                h = 2 * hp + i
                for kt in range(2):
                    r2 = pe.op(lambda e, i=i, h=h, kt=kt: e.matmul(
                        ob.ap[:, 256 * i:256 * i + 256], pt.ap[:, (2 * i + kt) * P:(2 * i + kt + 1) * P],
                        xv[:, kt, 256 * h:256 * h + 256], start=(kt == 0), stop=(kt == 1)), [r] + kvout["v"] + fo,
                        inc=(i == 1 and kt == 1))
            pt.put(r2)
            r3 = dve.op(lambda e: e.tensor_tensor(
                O[:, t, 512 * hp:512 * hp + 512].rearrange("p (h d) -> p h d", h=2),
                ob.ap[:, :].rearrange("p (h d) -> p h d", h=2),
                rs[t][:, 2 * hp:2 * hp + 2].unsqueeze(2).to_broadcast([P, 2, 256]), ALU.mult),
                [r2, stoks[(t, hp)]] + ofree)
            ob.put(r3)
            otok[(t, hp)] = r3

        outr = []
        oTf = oTb.take()
        staged([(t, hp) for hp in range(2) for t in range(2)], score, finish)
        for hp in range(2):
            outr += transpose_out(512 * hp, 4 * hp, [otok[(0, hp)], otok[(1, hp)]], oTf)
        xkv.put(pe.last())
        toks, pl = project_x(both(oT), 8, ("x_w_o", l), outr, 1.0)
        oTb.put(pl)
        return toks

    def even_mixer(xready):
        hr = norm_T(x, xready, 8, hTb)
        snap = snapshot() + R1free
        W = ("even_w_in", 0)
        lhs = both(hT)
        qr, vr = [], []

        def chunk_qk(c0, gi, dst, rope_on, acc, dfree):
            pair, done = gemm(lhs, 8, W, [(c0, 512)], hr)

            def consume():
                return [head_prep(pair[t], done[t], 8, 64, evg[:, gi, :], dst, 0, t, rope_on, dfree) for t in range(2)]
            return consume
        b = nextbank()
        fb = b.take()
        for k0 in range(0, 8, 4):
            hi, lo, tok, j = piece(W[0], W[1], k0, 4, [(1536, 8)])
            for kk in range(4):
                r = products(b.ap[0:8, 0:256], (hi[:, kk, :], lo[:, kk, :]), tuple(a[:, k0 + kk, :] for a in hT),
                             k0 + kk == 0, k0 + kk == 7, tok + fb + [hr[k0 + kk]], kk == 3)
            release(j, r)
        z, na = (M[0:8, 1, 512 + 256 * i:768 + 256 * i] for i in range(2))
        r = dve.op(lambda e: e.tensor_scalar(z, b.ap[0:8, 0:256], fbias[:, :], None, ALU.add), [r, tsm] + mem_read)
        b.put(r)
        r = dve.op(lambda e: e.scalar_tensor_tensor(out=na, in0=z, scalar=-1.0, in1=z, op0=ALU.mult, op1=ALU.min), [r])
        rm = dve.op(lambda e: e.tensor_scalar(z, z, 0.0, None, ALU.min), [r])
        r = act.op(lambda e: e.activation(na, na, ACT.Exp), [r])
        r = act.op(lambda e: e.activation(na, na, ACT.Ln, bias=1.0), [r])
        r = dve.op(lambda e: e.tensor_tensor(z, z, na, ALU.subtract), [r, rm])
        r = dve.op(lambda e: e.tensor_tensor_scan(cumT[:, 0, :], cst[0:8, 256:257].to_broadcast([8, 256]), z, 0.0,
                                                  ALU.mult, ALU.add), [r])
        r1 = dve.op(lambda e: e.tensor_scalar(cumT[:, 1, :], cumT[:, 0, :], -1.0, None, ALU.mult), [r])

        def logf_sums():
            tb_ = []
            for t in range(2):
                nk = P * (t + 1)
                per = 512 // nk
                for h0 in range(0, 8, per):
                    b = nextbank()
                    fb = b.take()
                    for i in range(per):
                        h = h0 + i
                        pe.op(lambda e, b=b, i=i, h=h, nk=nk: e.matmul(
                            b.ap[:, i * nk:(i + 1) * nk], sel(h, P), cumT[:, 1, 0:nk], start=True, stop=False),
                            [r1] + fb, inc=False)
                        r = pe.op(lambda e, b=b, i=i, h=h, nk=nk, t=t: e.matmul(
                            b.ap[:, i * nk:(i + 1) * nk], cumT[:, 0, t * P:(t + 1) * P], sel(h, nk),
                            start=False, stop=True), inc=(i == per - 1))
                    dstb = biasA[:, h0:h0 + per, :] if t else biasB[:, h0:h0 + per, 0:P]
                    r = dve.op(lambda e, b=b, dstb=dstb, nk=nk, per=per: e.tensor_tensor(
                        dstb, b.ap[:, 0:per * nk].rearrange("p (h k) -> p h k", h=per),
                        maskc[:, 256 - nk:256].unsqueeze(1).to_broadcast([P, per, nk]), ALU.add), [r] + snap)
                    b.put(r)
                    tb_.append(r)
            return tb_
        c1 = chunk_qk(0, 0, qT, False, qr, snap)
        p1 = c1()
        c2 = chunk_qk(512, 1, kT, False, qr, snap)
        qr += [f() for f in p1]
        p2 = c2()
        pair, done = gemm(lhs, 8, W, [(1024, 512)], hr)
        qr += [f() for f in p2]
        for t in range(2):
            r = evac(vsb[:, t, :], pair[t].ap[:, :], [done[t]] + vfree.take())
            pair[t].put(r)
            vr.append(r)
        tbias = logf_sums()
        R = {}

        def f_qk(c0, gi, dst, name):
            def start():
                c = chunk_qk(c0, gi, dst, True, None, snap)

                def consume():
                    R[name] = []
                    late.extend((f, R[name]) for f in c())
                return consume
            return start

        def f_v():
            pair, done = gemm(lhs, 8, W, [(2568, 512)], hr)
            hTb.put(pe.last())

            def consume():
                R["v"] = [evac(M[:, t, 0:512], pair[t].ap[:, :], [done[t]] + mem_read) for t in range(2)]
                for t in range(2):
                    pair[t].put(R["v"][t])
            return consume
        bq = qT[:, 4:8, :]
        bk = kT[:, 4:8, :]
        fillers.extend([f_qk(1544, 2, bq, "q"), f_qk(2056, 3, bk, "k"), f_v])
        kvout, KG = cross_kv_fillers(0)
        q_at = lambda h, t: qT[64 * (h % 2):64 * (h % 2) + 64, h // 2, t * P:(t + 1) * P]
        k_at = lambda h, nk: kT[64 * (h % 2):64 * (h % 2) + 64, h // 2, 0:nk]

        def bias_at(heads, t):
            hs = slice(heads[0], heads[-1] + 1, 2)
            return (biasA[:, hs, :] if t else biasB[:, hs, 0:P]), tbias
        ot = head_attention(q_at, k_at, lambda h, kt: vsb[:, kt, 64 * h:64 * h + 64], qr, vr, bias_at, snap, 0)
        settle()
        finish_late()
        rb = R["q"] + R["k"]
        oTf = oTb.take()
        outr = transpose_out(0, 0, ot, oTf)
        lw = stat(128)
        l2 = stat(2)
        r = dve.op(lambda e: e.tensor_tensor(lw.rearrange("p (a n) -> p a n", a=2), lamp[:, 0:4:2, :], lamp[:, 1:4:2, :],
                                             ALU.mult), [tsm])
        r = dve.op(lambda e: e.tensor_reduce(l2, lw.rearrange("p (a n) -> p a n", a=2), AX, ALU.add), [r])
        r = act.op(lambda e: e.activation(l2, l2, ACT.Exp), [r])
        lam_init = 0.8 - 0.6 * math.exp(-0.3 * 0)
        nl = stat(1)
        r = dve.op(lambda e: e.tensor_tensor(nl, l2[:, 1:2], l2[:, 0:1], ALU.subtract), [r])
        tnl = dve.op(lambda e: e.tensor_scalar(nl, nl, -lam_init, None, ALU.add), [r])
        work = [(0, [0, 1, 2, 3]), (1, [0, 1]), (1, [2, 3])]
        fin = []

        def score(t, heads):
            nk, nh = P * (t + 1), len(heads)
            got = []
            for j in range(2):
                b = nextbank()
                fb = b.take()
                for i, h in enumerate(heads):
                    r = pe.op(lambda e, i=i, h=h, j=j, b=b: e.matmul(
                        b.ap[:, i * nk:(i + 1) * nk], bq[64 * j:64 * j + 64, h, t * P:(t + 1) * P],
                        bk[64 * j:64 * j + 64, h, 0:nk], start=True, stop=True), rb + fb, inc=(i == nh - 1))
                s = S_rot.next()
                s3 = s.ap[:, 0:nh * nk].rearrange("p (h k) -> p h k", h=nh)
                r = dve.op(lambda e, b=b, s3=s3: e.scalar_tensor_tensor(
                    out=s3, in0=b.ap[:, 0:nh * nk].rearrange("p (h k) -> p h k", h=nh), scalar=0.125,
                    in1=maskb[:, 256 - nk:256].unsqueeze(1).to_broadcast([P, nh, nk]), op0=ALU.mult, op1=ALU.add),
                    [r] + s.take())
                b.put(r)
                r, sm = softmax_group(s, nh, nk, r)
                got.append((s, s3, r, sm))
            rr = []
            for j in range(2):
                s, s3, r, sm = got[j]
                rc = stat(nh)
                r = dve.op(lambda e, rc=rc, sm=sm: e.reciprocal(rc, sm), [r])
                if j:
                    r = dve.op(lambda e, rc=rc: e.tensor_scalar(rc, rc, nl, None, ALU.mult), [r, tnl])
                r = dve.op(lambda e, s3=s3, rc=rc: e.tensor_tensor(
                    s3, s3, rc.unsqueeze(2).to_broadcast([P, nh, nk]), ALU.mult), [r])
                rr.append(r)
            s = got[0][0]
            r = pool.op(lambda e: e.tensor_tensor(s.ap, s.ap, got[1][0].ap, ALU.add), rr)
            got[1][0].put(r)
            return s, r

        def finish(t, heads, pt, r):
            nkt = t + 1
            fo = ob.take()
            for i, h in enumerate(heads):
                for kt in range(nkt):
                    r2 = pe.op(lambda e, i=i, h=h, kt=kt: e.matmul(
                        ob.ap[:, P * h:P * h + P], pt.ap[:, (i * nkt + kt) * P:(i * nkt + kt + 1) * P],
                        M[:, kt, P * h:P * h + P], start=(kt == 0), stop=(kt == nkt - 1)), [r] + R["v"] + fo,
                        inc=(i == len(heads) - 1 and kt == nkt - 1))
            pt.put(r2)
            if heads[-1] != 3:
                return
            sq = sqj_rot.next()
            r = act.op(lambda e: e.activation(sq.ap[:, 0:512], ob.ap[:, :], ACT.Square), [r2] + sq.take())
            ss = stat(4)
            r = dve.op(lambda e: e.tensor_reduce(ss, sq.ap[:, 0:512].rearrange("p (h d) -> p h d", h=4), AX, ALU.add),
                       [r])
            sq.put(r)
            rs, r = rstd(ss, 4, 128, [r])
            o3 = O[:, t, 512:1024].rearrange("p (h d) -> p h d", h=4)
            r = dve.op(lambda e: e.tensor_tensor(o3, ob.ap[:, :].rearrange("p (h d) -> p h d", h=4),
                                                 rs.unsqueeze(2).to_broadcast([P, 4, P]), ALU.mult), [r])
            ob.put(r)
            r = dve.op(lambda e: e.tensor_tensor(o3, o3, sublng[:, :].unsqueeze(1).to_broadcast([P, 4, P]), ALU.mult),
                       [r, tsm])
            r = dve.op(lambda e: e.tensor_scalar(O[:, t, 512:1024], O[:, t, 512:1024], 1.0 - lam_init, None, ALU.mult),
                       [r])
            fin.append(r)
        staged(work, score, finish, 1)
        outr += transpose_out(512, 4, fin, oTf)
        vfree.put(pe.last())
        drain_fill()
        toks, pl = project_x(both(oT), 8, ("even_w_out", 0), outr, 1.0)
        oTb.put(pl)
        mfree.append(pl)
        return toks, kvout, KG

    vfree = Buf(None)
    mem_read = []

    def odd_mixer(xready):
        hr = norm_T(x, xready, (5 + 1) * 8, hTb)
        snap = snapshot()
        W = ("odd_w_in", 0)
        lhs = both(hT)
        rel = v("rel")
        tb0 = dma(pool, biasB[:, :, :], bass.AP(rel.tensor, rel.offset, [[1, P], [512, 8], [1, 256]]), "rel", snap)
        tbias = []

        def rel_bias():
            for g in range(4):
                b = nextbank()
                r = pe.op(lambda e, b=b, g=g: e.matmul(
                    b.ap[:, :], flip, biasB[:, 2 * g:2 * g + 2, :].rearrange("p h k -> p (h k)"), start=True, stop=True),
                    [tb0] + b.take())
                r = dve.op(lambda e, b=b, g=g: e.tensor_tensor(
                    biasA[:, 2 * g:2 * g + 2, :], b.ap[:, :].rearrange("p (h k) -> p h k", h=2),
                    maskb.unsqueeze(1).to_broadcast([P, 2, 256]), ALU.add), [r] + snap)
                b.put(r)
                tbias.append(r)
        qr, vr = [], []
        pre = []
        for n, (c0, dst) in enumerate(((1536, qT), (2048, kT))):
            pair, done = gemm(lhs, 8, W, [(c0, 512)], hr)
            qr += [f() for f in pre]
            pre = [head_prep(pair[t], done[t], 8, 64, odg[:, n, :], dst, 0, t, False, snap) for t in range(2)]
        pair, done = gemm(lhs, 8, W, [(2560, 512)], hr)
        qr += [f() for f in pre]
        fv = vfree.take()
        for t in range(2):
            r = evac(vsb[:, t, :], pair[t].ap[:, :], [done[t]] + fv)
            pair[t].put(r)
            vr.append(r)
        rel_bias()
        tflip = pe.last()
        R = {}
        uc = biasB

        def f_conv(which, c0):
            def start():
                pair, done = gemm_T(lambda kt: tuple(a[:, kt, :] for a in hT), 8, W, [(c0, 512)], hr)
                if which == "b":
                    hTb.put(pe.last())

                def consume():
                    if which == "c":
                        R["c"] = [evac(uc[:, 2 * m:2 * m + 2, :].rearrange("p a b -> p (a b)"), pair[m].ap[:, :],
                                       [done[m], tflip] + snap) for m in range(2)]
                        for m in range(2):
                            pair[m].put(R["c"][m])
                    elif which == "h":
                        R["u"] = []
                        for m in range(2):
                            o = uc[:, 2 * m:2 * m + 2, :].rearrange("p a b -> p (a b)")
                            r = dve.op(lambda e, o=o, m=m: e.tensor_tensor(o, o, pair[m].ap[:, :], ALU.mult),
                                       [done[m], R["c"][m]])
                            pair[m].put(r)
                            R["u"].append(r)
                        R["y"] = []
                        for k in range(4):
                            u, y = uc[:, k, :], uc[:, 4 + k, :]
                            w = [gcol[:, 96 + 4 * i + k:97 + 4 * i + k] for i in range(3)]
                            r = dve.op(lambda e, u=u, y=y, w=w: e.tensor_scalar(y, u, w[2], None, ALU.mult),
                                       [R["u"][k // 2]] + snap)
                            r = dve.op(lambda e, u=u, y=y, w=w: e.scalar_tensor_tensor(
                                out=y[:, 1:256], in0=u[:, 0:255], scalar=w[1], in1=y[:, 1:256], op0=ALU.mult,
                                op1=ALU.add), [r])
                            r = dve.op(lambda e, u=u, y=y, w=w: e.scalar_tensor_tensor(
                                out=y[:, 2:256], in0=u[:, 0:254], scalar=w[0], in1=y[:, 2:256], op0=ALU.mult,
                                op1=ALU.add), [r])
                            R["y"].append(r)
                    else:
                        R["o"] = []
                        for m in range(2):
                            o = uc[:, 4 + 2 * m:6 + 2 * m, :].rearrange("p a b -> p (a b)")
                            r = dve.op(lambda e: e.tensor_tensor(o, o, pair[m].ap[:, :], ALU.mult),
                                       [done[m], R["y"][2 * m], R["y"][2 * m + 1]])
                            pair[m].put(r)
                            hi, lo = flat(oT, 2 * m, 2)
                            R["o"].append(halves(hi, lo, o, [r], oTf))
                return consume
            return start
        oTf = oTb.take()
        fillers.extend([f_conv("c", 512), f_conv("h", 1024), f_conv("b", 0)])
        kvout, KG = cross_kv_fillers(1)
        q_at = lambda h, t: qT[64 * (h % 2):64 * (h % 2) + 64, h // 2, t * P:(t + 1) * P]
        k_at = lambda h, nk: kT[64 * (h % 2):64 * (h % 2) + 64, h // 2, 0:nk]

        def bias_at(heads, t):
            return biasA[:, heads[0]:heads[-1] + 1:2, 256 - P * (t + 1):256], tbias
        ot = head_attention(q_at, k_at, lambda h, kt: vsb[:, kt, 64 * h:64 * h + 64], qr, vr, bias_at, snap, 512)
        outr = transpose_out(512, 4, ot, oTf)
        vfree.put(pe.last())
        drain_fill()
        outr = R["o"] + outr
        toks, pl = project_x(both(oT), 8, ("odd_w_out", 0), outr, 1.0)
        oTb.put(pl)
        return toks, kvout, KG

    def second_mixer(xready):
        hr = norm_T(x, xready, 80, hTb)
        snap = snapshot()
        W = ("w_in_2", 0)
        lhs = both(hT)
        rhs = lambda kt: tuple(a[:, kt, :] for a in hT)
        tal = [dma(pool, (biasA, biasB)[i][:, :, :], v("alibi")[i], f"al{i}", snap) for i in range(2)]
        tzc = [pool.op(lambda e: e.memset(CL[ri], 0.0), snap) for ri in range(2)][-1]
        for ri, nm in enumerate(("c_re_2", "c_im_2")):
            src = v(nm).rearrange("l (J g) h p -> g h (l J) p", g=8)
            for g in range(8):
                tcl = dma(pool, CL[ri][16 * g:16 * g + 16, :, 64 * (g % 2):64 * (g % 2) + 64], src[g], "cl", [tzc])
        pqb[0].put(*snap)
        load_table(0)

        def queries(c0, dst):
            pair, done = gemm_T(rhs, 8, W, [(c0, 512)], hr)
            out = []
            for m in range(2):
                r = evac(dst[:, 2 * m:2 * m + 2, :].rearrange("p a b -> p (a b)"), pair[m].ap[:, :], [done[m]] + snap)
                pair[m].put(r)
                out.append(r)
            return out

        def keys(c0, dst, vdst, name):
            pair = nextpair()
            first = hr + pair[0].take() + pair[1].take()
            for k0 in range(0, 8, per_piece(256)):
                hi, lo, tok, j = piece(W[0], W[1], k0, per_piece(256), [(c0, 256)])
                for kk in range(per_piece(256)):
                    kt = k0 + kk
                    r0 = products(pair[0].ap[:, 0:256], (hi[:, kk, 0:P], lo[:, kk, 0:P]), rhs(kt), kt == 0, kt == 7,
                                  tok + first, kt == 7)
                    first = []
                    for t in range(2):
                        r1 = products(pair[1].ap[:, P * t:P * t + P], lhs(kt, t), (hi[:, kk, P:256], lo[:, kk, P:256]),
                                      kt == 0 and t == 0, kt == 7, [], t == 1 and (kt == 7 or kk == per_piece(256) - 1),
                                      True)
                release(j, r1)
            ra = evac(dst[:, 0, :], pair[0].ap[:, 0:256], [r0] + snap)
            pair[0].put(ra)
            rb_ = evac(vdst, pair[1].ap[:, 0:256].rearrange("p (t n) -> p t n", t=2), [r1] + snap)
            pair[1].put(rb_)
            rs = [dma(pool, dst[64 * (1 - a):64 * (1 - a) + 64, 1, :], dst[64 * a:64 * a + 64, 0, :], name, [ra] + snap)
                  for a in range(2)]
            return [ra, rs[-1]], rb_
        qa, qm = qT[:, 0:4, :], qT[:, 4:8, :]
        ka, km = kT[:, 0:2, :], kT[:, 2:4, :]
        va, vm = (kT[:, 4 + i, :].rearrange("p (t n) -> p t n", t=2) for i in range(2))
        rqa = queries(0, qa)
        rka, rva = keys(512, ka, va, "ka")
        rqm = queries(1280, qm)
        rkm, rvm = keys(1792, km, vm, "km")
        pair, done = gemm_T(rhs, 8, W, [(768, 512)], hr)
        fv = vfree.take()
        ru = []
        for m in range(2):
            r = evac(uT[:, 2 * m:2 * m + 2, :].rearrange("p a b -> p (a b)"), pair[m].ap[:, :], [done[m]] + fv)
            pair[m].put(r)
            ru.append(r)
        gt = {}

        def f_gate(c):
            for got in gemm_steps(lhs, 8, W, [(2048 + 512 * c, 512)], hr):
                if got:
                    break
                yield None
            pair, done = got
            if c == 5:
                hTb.put(pe.last())

            def consume():
                for t in range(2):
                    gsl = gates[c // 2][:, t, 512 * (c % 2):512 * (c % 2) + 512]
                    r = act.op(lambda e: e.activation(gsl, pair[t].ap[:, :], ACT.Exp, scale=-1.0),
                               [done[t]] + snap + (xnb.free if c >= 4 else []))
                    pair[t].put(r)
                    r = dve.op(lambda e, gsl=gsl: e.tensor_scalar(gsl, gsl, 1.0, None, ALU.add), [r])
                    gt[(c, t)] = dve.op(lambda e, gsl=gsl: e.reciprocal(gsl, gsl), [r])
            yield consume
        slices.extend(f_gate(c) for c in range(4))
        mtok = {}

        def gated(lhs_, KT, Wo, ready, branch):
            for c in range(2):
                pair, done = gemm(lhs_, KT, Wo, [(512 * c, 512)], ready)
                for t in range(2):
                    gsl = gates[branch][:, t, 512 * c:512 * c + 512]
                    dst = M[:, t, 512 * c:512 * c + 512]
                    tg_ = gt[(2 * branch + c, t)]
                    if branch == 0:
                        r = dve.op(lambda e, dst=dst, gsl=gsl, t=t, pair=pair: e.tensor_tensor(
                            dst, gsl, pair[t].ap[:, :], ALU.mult), [done[t], tg_] + pqb[0].free)
                        pair[t].put(r)
                    else:
                        r = dve.op(lambda e, gsl=gsl, t=t, pair=pair: e.tensor_tensor(
                            gsl, gsl, pair[t].ap[:, :], ALU.mult), [done[t], tg_])
                        pair[t].put(r)
                        r = pool.op(lambda e, dst=dst, gsl=gsl: e.tensor_tensor(dst, dst, gsl, ALU.add),
                                    [r, mtok[(c, t)]])
                    mtok[(c, t)] = r

        def attend(qd, kd_, vd, rq, rv, bias, tb_, sink):
            q_at = lambda h, t: qd[64 * (h % 2):64 * (h % 2) + 64, h // 2, t * P:(t + 1) * P]
            k_at = lambda h, nk: kd_[64 * (h % 2):64 * (h % 2) + 64, int(h // 4 != h % 2), 0:nk]
            return head_attention(q_at, k_at, lambda h, kt: vd[:, kt, 64 * (h // 4):64 * (h // 4) + 64], rq, [rv],
                                  lambda heads, t: (bias[:, heads[0]:heads[-1] + 1:2, 256 - P * (t + 1):256], [tb_]),
                                  snap, 0, sink)
        ot = attend(qa, ka, va, rqa + rka, rva, biasA, tal[0], sinkb)
        oTf = oTb.take()
        outa = transpose_out(0, 0, ot, oTf)
        tzr = pool.op(lambda e: e.memset(CR, 0.0), [ot, pe.last()])
        ot = attend(qm, km, vm, rqm + rkm, rvm, biasB, tal[1], None)
        outm = transpose_out(0, 4, ot, oTf)
        slices.extend(f_gate(c) for c in (4, 5))
        rz = []
        zin = qT[:, 0:4, :]
        snap2 = snapshot()
        pqb[1].put(*snap2)
        load_table(1)
        T_rot = Rot([R1[:, 1024 * i:1024 * i + 1024].rearrange("p (n a t) -> p n a t", n=2, a=2) for i in range(2)])
        H_rot = Rot([R1[:, 2560 + 512 * i:3072 + 512 * i].rearrange("p (a t) -> p a t", a=2) for i in range(3)])
        G = R1[:, 2048:2560].rearrange("p (a t) -> p a t", a=2)
        gb = Buf(G)
        gb.put(*snap2)
        for rot in (T_rot, H_rot):
            for b in rot.bufs:
                b.put(*snap2)
        crbuf = [Buf(CR[:, i]) for i in range(2)]
        tcr = {}

        def project_of(J):
            buf = crbuf[J % 2]
            fc = buf.take()
            for ri in range(2):
                b = banks[6]
                r = pe.op(lambda e: e.transpose(b.ap[:, 0:P], CL[ri][:, J, :], ident), [tcl] + b.take())
                dst = bass.AP(buf.ap.tensor, buf.ap.offset + 512 * ri, [[2048, P], [160, 4], [1, 32]])
                r = dve.op(lambda e: e.tensor_scalar(dst, b.ap[:, 0:P].rearrange("p (j c) -> p j c", j=4),
                                                     -1.0 if ri else 1.0, None, ALU.mult), [r, tzr] + fc)
                b.put(r)
            tcr[J] = r

        def phases(J, jj):
            tab = pqb[J % 2].ap
            return [tab[:, n, jj, :].unsqueeze(1).to_broadcast([P, 2, 256]) for n in range(2)]

        def drive(J, jj):
            b = banks[4 + jj % 2]
            fb = b.take()
            for ri in range(2):
                r = pe.op(lambda e: e.matmul(
                    b.ap[:, 256 * ri:256 * ri + 256], BT[32 * jj:32 * jj + 32, ri, J, :],
                    uT[32 * jj:32 * jj + 32, J, :], start=True, stop=True), ru + [tg["bt"]] + fb, inc=(ri == 1))
            return b, r

        def turn_back(J, jj, b, r):
            c, s = phases(J, jj)
            b3 = b.ap[:, :].rearrange("p (a t) -> p a t", a=2)
            T, X = T_rot.next(), H_rot.next()
            T1, T2 = T.ap[:, 0], T.ap[:, 1]
            dve.op(lambda e: e.tensor_tensor(T1, b3, c, ALU.mult), [r, ptab[J]] + T.take())
            r = dve.op(lambda e: e.tensor_tensor(T2, b3, s, ALU.mult))
            b.put(r)
            r1 = pool.op(lambda e: e.tensor_tensor(X.ap[:, 0, :], T1[:, 0, :], T2[:, 1, :], ALU.add), [r] + X.take())
            r2 = pool.op(lambda e: e.tensor_tensor(X.ap[:, 1, :], T1[:, 1, :], T2[:, 0, :], ALU.subtract), [r])
            return T, X, (r1, r2)

        def turn_forth(J, jj, T, X, rx):
            mg = SM[:, 1, 4 * J + jj:4 * J + jj + 1].to_broadcast([P, 256])
            fg = gb.take()
            for a in range(2):
                r = dve.op(lambda e: e.tensor_tensor_scan(G[:, a, :], mg, X.ap[:, a, :], 0.0, ALU.mult, ALU.add),
                           [rx[a]] + fg)
            c, s = phases(J, jj)
            T1, T2 = T.ap[:, 0], T.ap[:, 1]
            dve.op(lambda e: e.tensor_tensor(T1, G, c, ALU.mult), [r, rx[1]])
            r = dve.op(lambda e: e.tensor_tensor(T2, G, s, ALU.mult), [r])
            pqb[J % 2].put(r)
            gb.put(r)
            if jj == 3 and J + 2 < 4:
                load_table(J + 2)
            r1 = pool.op(lambda e: e.tensor_tensor(X.ap[:, 0, :], T1[:, 0, :], T2[:, 1, :], ALU.subtract), [r])
            r2 = pool.op(lambda e: e.tensor_tensor(X.ap[:, 1, :], T1[:, 1, :], T2[:, 0, :], ALU.add), [r])
            T.put(r2)
            return X, [r1, r2]

        def project(J, jj, X, rh):
            fy = ob.take() if jj == 0 else []
            for ri in range(2):
                r = pe.op(lambda e: e.matmul(
                    ob.ap[:, 0:256], crbuf[J % 2].ap[:, ri, P * jj:P * jj + P], X.ap[:, ri, :],
                    start=(jj == 0 and ri == 0), stop=(jj == 3 and ri == 1)), rh + [tcr[J]] + fy, inc=(ri == 1))
            X.put(r)
            if jj < 3:
                return
            crbuf[J % 2].put(r)
            r = dve.op(lambda e: e.scalar_tensor_tensor(
                out=zin[:, J, :], in0=uT[:, J, :], scalar=gcol[:, 108 + J:109 + J], in1=ob.ap[:, 0:256], op0=ALU.mult,
                op1=ALU.add), [r] + snap2)
            ob.put(r)
            rz.append(r)
            if J + 2 < 4:
                project_of(J + 2)
        project_of(0)
        project_of(1)
        driven, back, forth = {0: drive(0, 0)}, {}, {}
        for k in range(18):
            if k + 1 < 16:
                driven[k + 1] = drive(*divmod(k + 1, 4))
            if k < 16:
                back[k] = turn_back(*divmod(k, 4), *driven.pop(k))
            fill()
            if 1 <= k < 17:
                forth[k - 1] = turn_forth(*divmod(k - 1, 4), *back.pop(k - 1))
            if k >= 2:
                project(*divmod(k - 2, 4), *forth.pop(k - 2))
        rz2 = []
        for J in range(4):
            rz2.append(act.op(lambda e, J=J: e.activation(zin[:, J, :], zin[:, J, :], ACT.Gelu_apprx_tanh), [rz[J]]))
        drain_fill()
        fh = hTb.take()
        for J in range(4):
            rz2[J] = halves(hT[0][:, J, :], hT[1][:, J, :], zin[:, J, :], [rz2[J]], fh)
        gated(both(oT), 4, ("w_o_swa_2", 0), outa, 0)
        pairs = []
        for half in (1, 0):
            pairs.append(gemm_T(rhs, 4, ("w_glu_2", 0), [(512 * half, 512)], rz2))
        zg = kT[:, 0:4, :]
        yin = qT[:, 4:8, :]
        ry = []
        for m in range(2):
            zs = zg[:, 2 * m:2 * m + 2, :].rearrange("p a b -> p (a b)")
            ys = yin[:, 2 * m:2 * m + 2, :].rearrange("p a b -> p (a b)")
            (p2, d2), (p1, d1) = pairs
            r = act.op(lambda e, zs=zs, m=m, p2=p2: e.activation(zs, p2[m].ap[:, :], ACT.Exp, scale=-1.0), [d2[m]] + snap2)
            p2[m].put(r)
            r = dve.op(lambda e, zs=zs: e.tensor_scalar(zs, zs, 1.0, None, ALU.add), [r])
            r = dve.op(lambda e, zs=zs: e.reciprocal(zs, zs), [r])
            r = dve.op(lambda e, zs=zs, ys=ys, m=m, p1=p1: e.tensor_tensor(ys, zs, p1[m].ap[:, :], ALU.mult),
                       [r, d1[m]] + snap2)
            p1[m].put(r)
            hi, lo = flat(hT, 4 + 2 * m, 2)
            ry.append(halves(hi, lo, ys, [r], fh))
        gated(both(oT, 4), 4, ("w_o_moba_2", 0), outm, 2)
        gated(both(hT, 4), 4, ("w_o_ssm_2", 0), ry, 1)
        oTb.put(pe.last())
        hTb.put(pe.last())
        xnb.put(mtok[(0, 0)], mtok[(0, 1)], mtok[(1, 0)], mtok[(1, 1)])
        outr = []
        fo = oTb.take()
        for c in range(2):
            for g in range(2):
                b = nextbank()
                fb = b.take()
                for i in range(2):
                    for t in range(2):
                        col = 512 * c + (2 * g + i) * P
                        r = pe.op(lambda e, i=i, t=t, col=col, b=b: e.transpose(
                            b.ap[:, (2 * i + t) * P:(2 * i + t + 1) * P], M[:, t, col:col + P], ident),
                            [mtok[(c, t)]] + fb, inc=(i == 1 and t == 1))
                k0 = 4 * c + 2 * g
                hi, lo = flat(oT, k0, 2)
                r2 = halves(hi, lo, b.ap[:, :], [r], fo)
                b.put(r2)
                outr.append(r2)
        toks, pl = project_x(both(oT), 8, ("w_out_2", 0), outr, 1.0)
        oTb.put(pl)
        return toks

    mready = []
    made = {}

    def mem_rows():
        made["rows"] = norm_rows(M, made["mem"])

    def mem_turn(l):
        mready[:] = norm_turn(made["rows"], (5 * l + 3) * 8, mTb)
        mfree.append(pe.last())

    def angles():
        tg["rope"] = trig_prep()
        made["in"] = input_matrices()
    made["mem"] = mem_load()
    tok = ffn(tx, 0, 0, ("ffn1_w_in", "ffn1_w_out"), 2816, True, 0.5,
              {1: angles, 2: lambda: input_turn(made["in"]), 3: mem_rows, 4: lambda: mem_turn(0)})
    for J in range(4):
        phase_table(J)
    mem_read.extend(made["rows"])
    vfree.put(pool.last())
    R1free = [spilled[2], spilled[3]]
    tok, kvout, KG = even_mixer(tok)
    tok = cross_attention(tok, 0, kvout, KG)
    made["mem"] = mem_load()
    tok = ffn(tok, 4 * 8, 0, ("ffn2_w_in", "ffn2_w_out"), 2816, True, 0.5, {2: mem_rows, 3: lambda: mem_turn(1)})
    tok = ffn(tok, 5 * 8, 1, ("ffn1_w_in", "ffn1_w_out"), 2816, True, 0.5)
    tok, kvout, KG = odd_mixer(tok)
    tok = cross_attention(tok, 1, kvout, KG)
    tok = ffn(tok, (5 + 4) * 8, 1, ("ffn2_w_in", "ffn2_w_out"), 2816, True, 0.5)
    tok = second_mixer(tok)
    tok = ffn(tok, 88, 0, ("w_ff1_2", "w_ff2_2"), 4096, False, 1.0)
    fsn = snapshot()
    tgf = dma(pool, M[:, 0, :], bc_rows(v("norm_final_2"), 1024), "gf", fsn)
    r, tr = row_rstd(x, tok)
    ends = []
    for t in range(2):
        rr = dve.op(lambda e, t=t: e.scalar_tensor_tensor(out=O[:, t, :], in0=x[:, t, :], scalar=r[:, t:t + 1],
                                                          in1=M[:, 0, :], op0=ALU.mult, op1=ALU.mult),
                    [tr[t], tgf] + fsn)
        ends.append(dma(sp, v("out").rearrange("b (t p) d -> t p (b d)", p=P)[t], O[:, t, :], f"out{t}", [rr]))
    sp.wait(ends)
    sp.wait(list(spilled.values()))
    return order


NAMES = ['x', 'mem', 'positions', 'ln_gains', 'ffn1_w_in', 'ffn1_w_out', 'ffn2_w_in', 'ffn2_w_out', 'even_w_in',
         'even_f_bias', 'even_qk_gains', 'even_lambda', 'even_subln_gain', 'even_w_out', 'odd_w_in', 'odd_conv_w',
         'odd_qk_gains', 'odd_rel_bias', 'odd_w_out', 'x_w_q', 'x_w_kv', 'x_qk_gains', 'x_w_o', 'norm_mix_2', 'w_in_2',
         'sinks_2', 'lam_re_2', 'lam_im_2', 'log_step_2', 'b_re_2', 'b_im_2', 'c_re_2', 'c_im_2', 'd_skip_2',
         'w_glu_2', 'w_o_swa_2', 'w_o_ssm_2', 'w_o_moba_2', 'w_out_2', 'norm_ffn_2', 'w_ff1_2', 'w_ff2_2',
         'norm_final_2']


def kernel(**inputs):
    import concourse.bacc as bacc
    from concourse.bass_utils import run_bass_kernel_spmd as run

    arrays = {}

    def give(name, a):
        arrays["in_" + name] = np.ascontiguousarray(a)

    for name in NAMES:
        if name == 'odd_rel_bias':
            tab = np.asarray(inputs[name])[0]
            give("rel", np.concatenate([np.repeat(tab[:, 256:257], 127, 1), tab[:, ::-1],
                                        np.repeat(tab[:, 0:1], 128, 1)], 1))
        else:
            give(name, np.asarray(inputs[name]))
    give("consts", build_consts())
    give("alibi", build_alibi())
    def program(plan):
        nc = bacc.Bacc("TRN2", target_bir_lowering=False, num_devices=1)
        D = {n[3:]: nc.dram_tensor(n, a.shape, mybir.dt.from_np(a.dtype), kind="ExternalInput").ap()
             for n, a in arrays.items()}
        D["out"] = nc.dram_tensor("out", (1, 256, 1024), F32, kind="ExternalOutput").ap()
        return nc, build(nc, D, plan)

    _, plan = program(None)
    nc, _ = program(plan)
    r = run(nc, [arrays], core_ids=[0])
    return np.asarray(r.results[0]["out"])
```

```python
import math
from contextlib import ExitStack

import numpy as np
import concourse.bass as bass
from concourse import mybir

F32 = mybir.dt.float32
F32R = mybir.dt.float32r
I32 = mybir.dt.int32
ALU = mybir.AluOpType
ACT = mybir.ActivationFunctionType
AX = mybir.AxisListType.X
P = 128
NEG = -1.0e30
TWO_PI = 2.0 * math.pi
MAGIC = 12582912.0
ROPE_INV = [float.fromhex(v) for v in (
    "0x1.0000000000000p+0", "0x1.8d275e0000000p-3", "0x1.3411900000000p-5", "0x1.ddee9c0000000p-8",
    "0x1.72ba440000000p-10", "0x1.1f91f00000000p-12", "0x1.be21880000000p-15", "0x1.5a0f4e0000000p-17")]
SLOT = 1024
NRAW = 5
NSPLIT = 3


def pieces_of_two_pi():
    out, rest = [], TWO_PI
    for k in range(4):
        if k == 3:
            out.append(float(np.float32(rest)))
            break
        m, e = math.frexp(rest)
        part = math.ldexp(math.floor(m * 4096.0), e - 12)
        out.append(part)
        rest -= part
    return out


CONST_N = 904 + 128


def build_consts():
    c = np.zeros((P, CONST_N), np.float32)
    i = np.arange(P)
    c[:, 0:128] = np.eye(P)
    c[:, 128:256] = (i[:, None] <= i[None, :])
    c[:, 256:384] = 1.0
    c[:, 512:640] = np.where(i[:, None] >= i[None, :], 0.0, NEG)
    c[:, 768:896] = np.where(i[:, None] // 64 >= i[None, :] // 64, 0.0, NEG)
    c[:, 896:904] = np.asarray(ROPE_INV, np.float32)
    c[:, 904:1032] = np.eye(P)[::-1]
    return c


def build_alibi():
    slopes = (2.0 ** (-8.0 * np.arange(1, 17) / 16)).astype(np.float32)
    dist = (128 + np.arange(P)[:, None] - np.arange(256)[None, :])
    df = dist.astype(np.float32)
    out = np.zeros((2, P, 8, 256), np.float32)
    for h in range(8):
        out[0, :, h] = np.where((dist >= 0) & (dist < 128), -slopes[h] * df, NEG)
        out[1, :, h] = np.where(dist >= 0, -slopes[8 + h] * df, NEG)
    return out


class Buf:

    def __init__(self, ap):
        self.ap = ap
        self.free = []

    def take(self):
        out, self.free = self.free, []
        return out

    def put(self, *toks):
        self.free += toks


class Rot:
    def __init__(self, aps):
        self.bufs = [Buf(a) for a in aps]
        self.n = 0

    def next(self):
        b = self.bufs[self.n % len(self.bufs)]
        self.n += 1
        return b


class Queue:

    def __init__(self, eng, sem):
        self.eng, self.sem, self.count, self.seen = eng, sem, 0, {}

    def wait(self, toks):
        for t in toks:
            if t is None:
                continue
            if isinstance(t, list):
                self.wait(t)
                continue
            sem, value = t
            if self.seen.get(id(sem), 0) < value:
                self.seen[id(sem)] = value
                self.eng.wait_ge(sem, value)

    def op(self, fn, after=(), inc=True):
        self.wait(after)
        ins = fn(self.eng)
        if not inc:
            return None
        self.count += 1
        ins.then_inc(self.sem, 1)
        return (self.sem, self.count)

    def last(self):
        return (self.sem, self.count) if self.count else None


def build(nc, D, plan):
    with ExitStack() as ctx:
        return build_in(nc, D, ctx, plan)


def build_in(nc, D, ctx, plan):
    def sb(name, shape, dt=F32):
        return ctx.enter_context(nc.sbuf_tensor(name, shape, dt))

    def newsem(name):
        return ctx.enter_context(nc.semaphore(name))

    pe = Queue(nc.tensor, newsem("s_pe"))
    act = Queue(nc.scalar, newsem("s_act"))
    dve = Queue(nc.vector, newsem("s_dve"))
    pool = Queue(nc.gpsimd, newsem("s_pool"))
    sp = Queue(nc.sync, newsem("s_sp"))
    dsem = {}

    def dma(q, out, in_, name, after=()):
        if name not in dsem:
            dsem[name] = [newsem("d_" + name), 0]
        d = dsem[name]
        d[1] += 16
        q.wait(after)
        q.eng.dma_start(out, in_).then_inc(d[0], 16)
        return (d[0], d[1])

    def snapshot():
        return [q.last() for q in (pe, act, dve, pool)]

    raw = [sb(f"raw{i}", [P, SLOT]) for i in range(NRAW)]
    whi = [sb(f"whi{i}", [P, SLOT], F32R) for i in range(NSPLIT)]
    wlo = [sb(f"wlo{i}", [P, SLOT], F32R) for i in range(NSPLIT)]
    x = sb("x", [P, 2, 1024])
    hT = [sb(f"hT{i}", [P, 8, 256], F32R) for i in range(2)]
    oT = [sb(f"oT{i}", [P, 8, 256], F32R) for i in range(2)]
    mT = [sb(f"mT{i}", [P, 8, 256], F32R) for i in range(2)]
    R1 = sb("R1", [P, 8192])
    S_rot = Rot([R1[:, 512 * i:512 * i + 512] for i in range(4)])
    pT_rot = Rot([R1[:, 2048 + 512 * i:2560 + 512 * i] for i in range(4)])
    qT = R1[:, 4096:6144].rearrange("p (k t) -> p k t", k=8)
    kT = R1[:, 6144:8192].rearrange("p (k t) -> p k t", k=8)
    R2 = sb("R2", [P, 4096])
    xkT = R2[:, 0:2048].rearrange("p (k t) -> p k t", k=8)
    xv = R2[:, 2048:4096].rearrange("p (t n) -> p t n", t=2)
    vsb = sb("vsb", [P, 2, 512])
    O = sb("O", [P, 2, 1024])
    M = sb("M", [P, 2, 1024])
    cumT = M[0:8, 0, 512:1024].rearrange("p (a n) -> p a n", a=2)
    biasA = sb("biasA", [P, 8, 256])
    biasB = sb("biasB", [P, 8, 256])
    gates = [xkT.rearrange("p k t -> p (k t)").rearrange("p (t n) -> p t n", t=2), xv, O[:, :, :]]
    fs_rot = Rot([biasA[:, 2 * i:2 * i + 2, :].rearrange("p a b -> p (a b)") for i in range(4)])
    fa_rot = Rot([biasB[:, 2 * i:2 * i + 2, :].rearrange("p a b -> p (a b)") for i in range(4)])
    sqj_rot = Rot([sb(f"sqj{i}", [P, 512])[:, :] for i in range(2)])
    cst = sb("cst", [P, CONST_N])
    gcol = sb("gcol", [P, 124])
    rows = sb("rows", [124, P])
    st = sb("st", [P, 1600])
    evg = sb("evg", [P, 4, 64])
    sublng = sb("sublng", [P, 128])
    lamp = sb("lamp", [P, 4, 64])
    fbias = sb("fbias", [8, 1])
    sinkb = sb("sinkb", [P, 8])
    posr = R1[0:2, 2048:2176].bitcast(I32)
    posf = R1[0:2, 2176:2304]
    ssr = R1[0:16, 2304:2688].rearrange("p (a n) -> p a n", a=3)
    lsr = R1[0:16, 2688:2690]
    rope = sb("rope", [P, 2, 2, 8])
    rtmp_rot = Rot([sb(f"rtmp{i}", [P, 4, 8, 8])[:, :, :, :] for i in range(1)])
    SM = sb("SM", [P, 8, 16])
    BT = sb("BT", [P, 2, 4, 128])
    CR = biasA[:, :, :].rearrange("p (c r a) n -> p c r (a n)", c=2, r=2)
    BL = R2[:, 0:1024].rearrange("p (r j h) -> p r j h", r=2, h=32)
    CL = [b.ap.rearrange("p (j n) -> p j n", j=4) for b in sqj_rot.bufs]
    early = [qT, kT]
    pq0 = [a.rearrange("p (r j) n -> p r j n", r=2) for a in early]
    pq = [M[:, :, :].rearrange("p r (j n) -> p r j n", j=4), pq0[1]]
    spill = nc.dram_tensor("phases", (4, P, 2048), F32, kind="Internal").ap()
    tabs = vsb[:, :, :].rearrange("p a (j n) -> p a j n", j=4)
    uT = vsb[:, :, :].rearrange("p a n -> p (a n)").rearrange("p (k t) -> p k t", k=4)

    banks = [Buf(ctx.enter_context(nc.psum_tensor(f"b{i}", [P, 512], F32))) for i in range(8)]
    gpair = [(banks[0], banks[1]), (banks[2], banks[3])]
    gcount = [0]
    tb = [banks[4], banks[5], banks[6]]
    tcount = [0]
    ob = banks[7]

    def nextbank():
        tcount[0] += 1
        return tb[(tcount[0] - 1) % len(tb)]

    stn = [0]

    def stat(n):
        stn[0] += n
        assert stn[0] <= 1600, stn
        return st[:, stn[0] - n:stn[0]]

    ident = cst[:, 0:128]
    tri = cst[:, 128:256]
    ones = cst[:, 256:384]
    maskc = cst[:, 384:640]
    maskb = cst[:, 640:896]
    inv8 = cst[:, 896:904]
    flip = cst[:, 904:1032]

    def sel(h, n):
        return cst[0:8, h:h + 1].to_broadcast([8, n])

    def v(d):
        return D[d]

    def bc_rows(ap1d, n):
        return bass.AP(ap1d.tensor, ap1d.offset, [[0, P], [1, n]])

    tx = [[dma(sp, x[:, t, :], v("x").rearrange("b (t p) d -> t p (b d)", p=P)[t], f"x{t}")] * 2 for t in range(2)]
    tcst = dma(sp, cst[:, :], v("consts"), "cst")
    trow = [dma(sp, rows[0:80, :], v("ln_gains").rearrange("l j (k p) -> (l j k) p", p=P), "rows"),
            dma(sp, rows[80:88, :], v("norm_mix_2").rearrange("l (k p) -> (l k) p", p=P), "rows"),
            dma(sp, rows[88:96, :], v("norm_ffn_2").rearrange("l (k p) -> (l k) p", p=P), "rows"),
            dma(sp, rows[96:108, :], v("odd_conv_w").rearrange("o w (k p) -> (o w k) p", p=P), "rows"),
            dma(sp, rows[108:112, :], v("d_skip_2").rearrange("l (k p) -> (l k) p", p=P), "rows"),
            dma(sp, rows[112:120, :], v("x_qk_gains").rearrange("l i (k p) -> (l i k) p", p=P), "rows")]
    for a in range(2):
        trow += [dma(sp, rows[120:122, 64 * a:64 * a + 64], v("even_qk_gains")[0, 0:2], "rows"),
                 dma(sp, rows[122:124, 64 * a:64 * a + 64], v("odd_qk_gains")[0], "rows")]
    trow = trow[-1]
    tsm = [dma(pool, evg[:, :, :].rearrange("p a b -> p (a b)"), bc_rows(v("even_qk_gains"), 256), "sm"),
           dma(pool, sublng[:, :], bc_rows(v("even_subln_gain"), 128), "sm"),
           dma(pool, lamp[:, :, :].rearrange("p a b -> p (a b)"), bc_rows(v("even_lambda"), 256), "sm"),
           dma(pool, fbias[:, :], v("even_f_bias").rearrange("a b -> b a"), "sm"),
           dma(pool, sinkb[:, :], bc_rows(v("sinks_2"), 8), "sm"),
           dma(pool, posr[:, :], v("positions").rearrange("b (t p) -> (b t) p", p=P), "sm"),
           dma(pool, ssr[:, 0, :], v("lam_re_2").rearrange("l (j a) p -> (l j) (a p)", a=2), "sm"),
           dma(pool, ssr[:, 1, :], v("lam_im_2").rearrange("l (j a) p -> (l j) (a p)", a=2), "sm"),
           dma(pool, lsr[:, :], v("log_step_2").rearrange("l (j a) -> (l j) a", a=2), "sm")][-1]
    tz = pool.op(lambda e: e.memset(BL[:, :, :, :], 0.0))
    for ri, nm in enumerate(("b_re_2", "b_im_2")):
        src = v(nm).rearrange("l (j a) p h -> a p (l j) h", a=2)
        for a in range(2):
            tbl = dma(pool, BL[64 * a:64 * a + 64, ri, :, 16 * a:16 * a + 16], src[a], "bl", [tz])
    order = []
    stage = dict(loaded=0, split=0, used=0)
    rawfree = [None] * NRAW
    spfree = [None] * NSPLIT
    loadtok, splittok = {}, {}

    def advance(upto):
        if plan is None:
            return
        while stage["split"] < min(upto + 1, len(plan)):
            j = stage["split"]
            while stage["loaded"] < min(j + NRAW, len(plan)):
                i = stage["loaded"]
                stage["loaded"] += 1
                name, l, k0, nk, pieces = plan[i]
                width = sum(w for _, w in pieces)
                dst = raw[i % NRAW][:, 0:nk * width].rearrange("p (k n) -> p k n", k=nk)
                off = 0
                for c0, w in pieces:
                    loadtok[i] = dma(sp, dst[:, :, off:off + w],
                                     v(name)[l, k0 * P:(k0 + nk) * P, c0:c0 + w].rearrange("(k p) n -> p k n", p=P),
                                     f"w{i % NRAW}", [rawfree[i % NRAW]])
                    off += w
            name, l, k0, nk, pieces = plan[j]
            n = nk * sum(w for _, w in pieces)
            r_, h_, l_ = raw[j % NRAW], whi[j % NSPLIT], wlo[j % NSPLIT]
            fr = [loadtok[j], spfree[j % NSPLIT]]
            rh = act.op(lambda e: e.activation(h_[:, 0:n], r_[:, 0:n], ACT.Copy), fr)
            rl = dve.op(lambda e: e.tensor_tensor(l_[:, 0:n], r_[:, 0:n], h_[:, 0:n].bitcast(F32), ALU.subtract),
                        fr + [rh])
            rawfree[j % NRAW] = rl
            splittok[j] = [rh, rl]
            stage["split"] += 1

    def piece(name, l, k0, nk, pieces):
        j = stage["used"]
        stage["used"] += 1
        entry = (name, l, k0, nk, tuple(pieces))
        order.append(entry)
        if plan is not None:
            assert plan[j] == entry, (plan[j], entry)
        advance(j + NSPLIT - 1)
        n = nk * sum(w for _, w in pieces)
        hi, lo = (a[j % NSPLIT][:, 0:n].rearrange("p (k n) -> p k n", k=nk) for a in (whi, wlo))
        return hi, lo, splittok.get(j, []), j

    def release(j, tok):
        spfree[j % NSPLIT] = tok

    def per_piece(width):
        return SLOT // width

    def products(bank_ap, a, b, start, stop, after, inc, skip=False):
        (ah, al), (bh, bl) = a, b
        pe.op(lambda e: e.matmul(bank_ap, ah, bh, start=start, stop=False, skip_group_check=skip), after, inc=False)
        pe.op(lambda e: e.matmul(bank_ap, ah, bl, start=False, stop=False, skip_group_check=skip), inc=False)
        return pe.op(lambda e: e.matmul(bank_ap, al, bh, start=False, stop=stop, skip_group_check=skip), inc=inc)

    def nextpair():
        gcount[0] += 1
        return gpair[(gcount[0] - 1) % 2]

    chains = []

    def step_chains():
        for c in list(chains):
            if next(c, True):
                chains.remove(c)

    def at(ready, kt, KT):
        return [ready[kt * len(ready) // KT]]

    def gemm(*args):
        for got in gemm_steps(*args):
            if got:
                return got

    def gemm_steps(lhs, KT, W, pieces, lhs_ready, pair=None, middle=None):
        pair = pair or nextpair()
        width = sum(w for _, w in pieces)
        first = pair[0].take() + pair[1].take()
        done = [None, None]
        for k0 in range(0, KT, per_piece(max(width, 256))):
            nk = min(per_piece(max(width, 256)), KT - k0)
            hi, lo, tok, j = piece(W[0], W[1], k0, nk, pieces)
            if k0 and middle:
                middle()
                middle = None
            for kk in range(nk):
                kt = k0 + kk
                for t in range(2):
                    last = kt == KT - 1 or (kk == nk - 1 and t == 1)
                    r = products(pair[t].ap[:, 0:width], lhs(kt, t), (hi[:, kk, :], lo[:, kk, :]), kt == 0,
                                 kt == KT - 1, tok + first + at(lhs_ready, kt, KT), last)
                    first = []
                    if kt == KT - 1:
                        done[t] = r
            release(j, r)
            step_chains()
            yield (pair, done) if k0 + nk == KT else None

    def gemm_T(rhs, KT, W, pieces, rhs_ready, mtiles=4):
        pair = nextpair()
        first = pair[0].take() + pair[1].take()
        done = [None, None]
        width = sum(w for _, w in pieces)
        for k0 in range(0, KT, per_piece(width)):
            nk = min(per_piece(width), KT - k0)
            hi, lo, tok, j = piece(W[0], W[1], k0, nk, pieces)
            for kk in range(nk):
                kt = k0 + kk
                for m in range(mtiles):
                    cs = slice(P * m, P * m + P)
                    r = products(pair[m // 2].ap[:, 256 * (m % 2):256 * (m % 2) + 256], (hi[:, kk, cs], lo[:, kk, cs]),
                                 rhs(kt), kt == 0 and m % 2 == 0, kt == KT - 1, tok + first + at(rhs_ready, kt, KT),
                                 kt == KT - 1 or (kk == nk - 1 and m == mtiles - 1), True)
                    first = []
                    if kt == KT - 1:
                        done[m // 2] = r
            release(j, r)
            step_chains()
        return pair, done

    def rsqrt(src, n, after):
        y, t = stat(n), stat(n)
        yi, ti = y.bitcast(I32), t.bitcast(I32)
        r = dve.op(lambda e: e.tensor_scalar(ti, src.bitcast(I32), 1, None, ALU.logical_shift_right), after)
        r = dve.op(lambda e: e.tensor_scalar(yi, ti, -1.0, 1597463007.0, ALU.mult, ALU.add), [r])
        for _ in range(3):
            r = dve.op(lambda e: e.tensor_tensor(t, y, y, ALU.mult), [r])
            r = dve.op(lambda e: e.scalar_tensor_tensor(out=t, in0=t, scalar=-0.5, in1=src, op0=ALU.mult,
                                                        op1=ALU.mult), [r])
            r = dve.op(lambda e: e.scalar_tensor_tensor(out=y, in0=t, scalar=1.5, in1=y, op0=ALU.add,
                                                        op1=ALU.mult), [r])
        return y, r

    def rstd(ss, n, count, after):
        ms = stat(n)
        r = dve.op(lambda e: e.tensor_scalar(ms, ss, 1.0 / count, 1e-6, ALU.mult, ALU.add), after)
        return rsqrt(ms, n, [r])

    def row_rstd(src, ready):
        ss = stat(4).rearrange("p (t n) -> p t n", t=2)
        ms = stat(2)
        fx = xnb.take()
        ra = []
        for t in range(2):
            for n in range(2):
                cs = slice(512 * n, 512 * n + 512)
                ra.append(act.op(lambda e: e.activation(O[:, t, cs], src[:, t, cs], ACT.Square,
                                                        accum_out=ss[:, t, n:n + 1]), [ready[t][n]] + fx))
        y, u, h = stat(2), stat(2), stat(2)
        yi, ui = y.bitcast(I32), u.bitcast(I32)
        r = dve.op(lambda e: e.tensor_tensor(ms, ss[:, :, 0], ss[:, :, 1], ALU.add), ra)
        r = dve.op(lambda e: e.tensor_scalar(ms, ms, 1.0 / 1024, 1e-6, ALU.mult, ALU.add), [r])
        rh = dve.op(lambda e: e.tensor_scalar(h, ms, -0.5, None, ALU.mult), [r])
        r = dve.op(lambda e: e.tensor_scalar(ui, ms.bitcast(I32), 1, None, ALU.logical_shift_right), [r])
        r = dve.op(lambda e: e.tensor_scalar(yi, ui, -1.0, 1597463007.0, ALU.mult, ALU.add), [r])
        r = [[r, rh]] * 2
        for _ in range(3):
            for t in range(2):
                yt, ut = y[:, t:t + 1], u[:, t:t + 1]
                r[t] = [dve.op(lambda e: e.scalar_tensor_tensor(out=ut, in0=yt, scalar=h[:, t:t + 1], in1=yt,
                                                                op0=ALU.mult, op1=ALU.mult), r[t])]
            for t in range(2):
                yt, ut = y[:, t:t + 1], u[:, t:t + 1]
                r[t] = [dve.op(lambda e: e.scalar_tensor_tensor(out=yt, in0=ut, scalar=1.5, in1=yt, op0=ALU.add,
                                                                op1=ALU.mult), r[t])]
        return y, r

    xnb = Buf(O)

    def halves(hi, lo, src, after, free=(), turn=0):
        if turn:
            r = dve.op(lambda e: e.tensor_copy(hi, src), list(after) + list(free))
        else:
            r = act.op(lambda e: e.activation(hi, src, ACT.Copy), list(after) + list(free))
        return dve.op(lambda e: e.tensor_tensor(lo, src, hi.bitcast(F32), ALU.subtract), [r] + list(free))

    def norm_rows(src, ready):
        y, r = row_rstd(src, ready)
        return [dve.op(lambda e: e.tensor_scalar(O[:, 0, :], src[:, 0, :], y[:, 0:1], None, ALU.mult), r[0]),
                act.op(lambda e: e.activation(O[:, 1, :], src[:, 1, :], ACT.Copy, scale=y[:, 1:2]), r[1])]

    def norm_later(ready, g0, dst):
        out = norm_turn(ready, g0, dst, x)
        advance(stage["used"] + NSPLIT - 1)
        return (out, *row_rstd(x, ready))

    def norm_turn(tn, g0, dst, src_x=None):
        rows_of = O if src_x is None else src_x
        fd = dst.take()
        out = []
        for g in range(4):
            b = nextbank()
            fb = b.take()
            for i in range(2):
                for t in range(2):
                    kt = 2 * g + i
                    r = pe.op(lambda e: e.transpose(b.ap[:, (2 * i + t) * P:(2 * i + t + 1) * P],
                                                    rows_of[:, t, kt * P:(kt + 1) * P], ident),
                              [tn[t] if src_x is None else tn[t][kt // 4], tgc] + fb, inc=(i == 1 and t == 1))
            kts = [2 * g, 2 * g + 1]
            gain = [gcol[:, g0 + kt:g0 + kt + 1] for kt in kts]
            src = [b.ap[:, 256 * i:256 * i + 256] for i in range(2)]
            hi, lo = ([a[:, kt, :] for kt in kts] for a in dst.ap)
            for i in range(2):
                rh = act.op(lambda e: e.activation(hi[i], src[i], ACT.Copy, scale=gain[i]), [r] + fd)
            for i in range(2):
                out.append(dve.op(lambda e: e.scalar_tensor_tensor(out=lo[i], in0=src[i], scalar=gain[i],
                                                                   in1=hi[i].bitcast(F32), op0=ALU.mult,
                                                                   op1=ALU.subtract), [rh] + fd))
            b.put(out[-1])
        if src_x is None:
            xnb.put(r)
        return out

    def norm_T(src, ready, g0, dst):
        return norm_turn(norm_rows(src, ready), g0, dst)

    evac_n = [0]

    def evac(dst, src, after, pick=None, gain=None):
        evac_n[0] += 1
        if pick == "act" or (pick is None and evac_n[0] % 2):
            return act.op(lambda e: e.activation(dst, src, ACT.Copy, scale=1.0 if gain is None else gain), after)
        if gain is None:
            return dve.op(lambda e: e.tensor_copy(dst, src), after)
        return dve.op(lambda e: e.tensor_scalar(dst, src, gain, None, ALU.mult), after)

    def add_x(bank, t, n0, scale, tok):
        r = dve.op(lambda e: e.scalar_tensor_tensor(out=x[:, t, n0:n0 + 512], in0=bank.ap[:, :], scalar=scale,
                                                    in1=x[:, t, n0:n0 + 512], op0=ALU.mult, op1=ALU.add), [tok])
        bank.put(r)
        return r

    def both(T, k0=0):
        return lambda kt, t: tuple(a[:, k0 + kt, t * P:(t + 1) * P] for a in T)

    def flat(T, k0, n):
        return [a[:, k0:k0 + n, :].rearrange("p k t -> p (k t)") for a in T]

    def project_x(lhs, KT, W, ready, scale):
        toks = [[None] * 2 for _ in range(2)]
        for c in range(2):
            pair, done = gemm(lhs, KT, W, [(512 * c, 512)], ready)
            for t in range(2):
                toks[t][c] = add_x(pair[t], t, 512 * c, scale, done[t])
        return toks, pe.last()

    hTb = Buf(hT)
    oTb = Buf(oT)

    def ffn(xready, g0, l, names, F, gated, scale, between={}):
        hr, rs, rtok = norm_later(xready, g0, hTb)
        snap = snapshot()
        per = 2 if gated else 4
        nch = F // (P * per)
        acc = banks[0:4]
        pair = (banks[4], banks[5])
        accfree = [b.take() for b in acc]
        aTfree = [oTb.take(), []]
        aTfree[1] = list(aTfree[0])
        tcnt = [0]
        made = {}

        def turn(c, toks, bufs):
            def go():
                out = []
                for g in range(per // 2):
                    b = banks[6 + tcnt[0] % 2]
                    tcnt[0] += 1
                    fb = b.take()
                    for i in range(2):
                        for t in range(2):
                            jj = 2 * g + i
                            r = pe.op(lambda e: e.transpose(
                                b.ap[:, (2 * i + t) * P:(2 * i + t + 1) * P], bufs[t].ap[:, jj * P:(jj + 1) * P], ident),
                                [toks[t]] + fb, inc=(i == 1 and t == 1))
                    hi, lo = flat(oT, 4 * (c % 2) + 2 * g, 2)
                    r2 = halves(hi, lo, b.ap[:, :], [r], aTfree[c % 2])
                    b.put(r2)
                    out.append(r2)
                for t in range(2):
                    bufs[t].put(r)
                made[c] = out
            return go

        def output(c):
            nk = SLOT // 1024
            for k0 in range(0, per, nk):
                hi, lo, tok, j = piece(names[1], l, per * c + k0, nk, [(0, 1024)])
                for kk in range(nk):
                    kt = k0 + kk
                    for n in range(2):
                        for t in range(2):
                            ends = c == nch - 1 and kt == per - 1
                            cs = slice(512 * n, 512 * n + 512)
                            r = products(acc[2 * t + n].ap[:, :], both(oT, 4 * (c % 2))(kt, t),
                                         (hi[:, kk, cs], lo[:, kk, cs]), c == 0 and kt == 0, ends,
                                         tok + made[c] + (accfree[2 * t + n] if c == 0 and kt == 0 else []),
                                         ends or (kk == nk - 1 and t == 1 and n == 1))
                            if ends:
                                fin[2 * t + n] = r
                release(j, r)
            aTfree[c % 2] = [r]
        fin = [None] * 4
        middle = None
        for c in range(nch):
            pcs = [(256 * c, 256), (F + 256 * c, 256)] if gated else [(512 * c, 512)]
            _, done = gemm(both(hT), 8, (names[0], l), pcs, hr, pair, middle)
            toks, bufs = [], []
            for t in range(2):
                s, a = fs_rot.next(), fa_rot.next()
                if gated:
                    r = act.op(lambda e: e.activation(s.ap[:, 0:256], pair[t].ap[:, 0:256], ACT.Silu,
                                                        scale=rs[:, t:t + 1]), [done[t]] + rtok[t] + s.take() + snap)
                    r = dve.op(lambda e: e.scalar_tensor_tensor(
                        out=a.ap[:, 0:256], in0=pair[t].ap[:, 256:512], scalar=rs[:, t:t + 1], in1=s.ap[:, 0:256],
                        op0=ALU.mult, op1=ALU.mult), [r] + a.take() + snap)
                else:
                    r = act.op(lambda e: e.activation(s.ap, pair[t].ap[:, :], ACT.Relu, scale=rs[:, t:t + 1]),
                               [done[t]] + rtok[t] + s.take() + snap)
                    r = dve.op(lambda e: e.tensor_tensor(a.ap, s.ap, s.ap, ALU.mult), [r] + a.take() + snap)
                pair[t].put(r)
                s.put(r)
                toks.append(r)
                bufs.append(a)
            if c:
                output(c - 1)
            middle = turn(c, toks, bufs)
            if c in between:
                tb[:] = banks[6:8]
                between[c]()
                tb[:] = banks[4:7]
        hTb.put(pe.last())
        middle()
        output(nch - 1)
        oTb.put(pe.last())
        toks = [[None] * 2 for _ in range(2)]
        for n in range(2):
            for t in range(2):
                toks[t][n] = add_x(acc[2 * t + n], t, 512 * n, scale, fin[2 * t + n])
        return toks

    fillers = []
    slices = []
    pending = []
    late = []

    def finish_late():
        while late:
            f, into = late.pop(0)
            into.append(f())

    def settle():
        while chains:
            step_chains()
        finish_late()
        while pending:
            pending.pop(0)()

    def flush():
        settle()
        settle()

    def fill():
        settle()
        if slices:
            f = next(slices[0])
            if f:
                slices.pop(0)
                pending.append(f)
        elif fillers:
            pending.append(fillers.pop(0)())

    fill_next = fill

    def drain_fill():
        while fillers or slices or pending:
            fill()
        flush()

    def head_prep(pair, done, nh, hd, dst, k0, gains, into, rope_gain=None, dstfree=(),
                  rowscale=None):
        w = nh * hd
        sq = [sqj_rot.next() for _ in range(2)]
        ss = stat(2 * nh)
        rr = []
        for t in range(2):
            bank = pair[t]
            scale, tscale = (rowscale[0][:, t:t + 1], rowscale[1][t]) if rowscale else (1.0, [])
            r = act.op(lambda e: e.activation(sq[t].ap[:, 0:w], bank.ap[:, 0:w], ACT.Square, scale=scale),
                       [done[t]] + tscale + sq[t].take())
            rr.append(dve.op(lambda e: e.tensor_reduce(ss[:, t * nh:t * nh + nh],
                                                       sq[t].ap[:, 0:w].rearrange("p (h d) -> p h d", h=nh), AX,
                                                       ALU.add), [r]))
        yield
        rs, r0 = rstd(ss, 2 * nh, hd, rr)
        if rowscale:
            r0 = [dve.op(lambda e: e.tensor_scalar(rs[:, t * nh:t * nh + nh], rs[:, t * nh:t * nh + nh],
                                                   rowscale[0][:, t:t + 1], None, ALU.mult), [r0]) for t in range(2)]
        yield
        n3 = [b.ap[:, 0:w].rearrange("p (h d) -> p h d", h=nh) for b in sq]
        fin = [None, None]
        for t in range(2):
            fin[t] = dve.op(lambda e: e.tensor_tensor(
                n3[t], pair[t].ap[:, 0:w].rearrange("p (h d) -> p h d", h=nh),
                rs[:, t * nh:t * nh + nh].unsqueeze(2).to_broadcast([P, nh, hd]), ALU.mult), [r0])
            pair[t].put(fin[t])
        if rope_gain is not None:
            for t in range(2):
                fin[t] = pool.op(lambda e: e.tensor_tensor(n3[t], n3[t], rope_gain.unsqueeze(1).to_broadcast([P, nh, hd]),
                                                           ALU.mult), [fin[t], tsm])
            yield
            for t in range(2):
                tmp = rtmp_rot.next()
                ft = tmp.take()
                q = tmp.ap
                x1, x2 = n3[t][:, :, 0:8], n3[t][:, :, 8:16]
                cb, sb_ = (rope[:, i, t, :].unsqueeze(1).to_broadcast([P, nh, 8]) for i in range(2))
                for i, (a, b) in enumerate(((x1, cb), (x2, sb_), (x2, cb), (x1, sb_))):
                    rr = dve.op(lambda e: e.tensor_tensor(q[:, i, :, :], a, b, ALU.mult), [fin[t], tg["rope"]] + ft)
                dve.op(lambda e: e.tensor_tensor(x1, q[:, 0, :, :], q[:, 1, :, :], ALU.subtract), [rr])
                fin[t] = dve.op(lambda e: e.tensor_tensor(x2, q[:, 2, :, :], q[:, 3, :, :], ALU.add), [rr])
                tmp.put(fin[t])
        nt = w // P

        def finish(t):
            b = nextbank()
            fb = b.take()
            for i in range(nt):
                r = pe.op(lambda e: e.transpose(b.ap[:, i * P:(i + 1) * P], sq[t].ap[:, i * P:(i + 1) * P], ident),
                          [fin[t], tgc] + fb, inc=(i == nt - 1))
            sq[t].put(r)
            n = max(len(gains), 1)
            for i in range(n):
                r2 = evac(dst[:, k0 + i:k0 + nt:n, t * P:(t + 1) * P],
                          b.ap[:, 0:w].rearrange("p (k n) -> p k n", k=nt)[:, i:nt:n, :], [r] + list(dstfree),
                          "act" if t else "dve", gains[i] if gains else None)
            b.put(r2)
            return r2
        late.extend((lambda t=t: finish(t), into) for t in range(2))

    def softmax_group(s, nh, nk, tok, sink=None):
        s3 = s.ap[:, 0:nh * nk].rearrange("p (h k) -> p h k", h=nh)
        nm, sm = stat(nh), stat(nh)
        if sink is None:
            r = dve.op(lambda e: e.tensor_reduce(nm, s3, AX, ALU.max, negate=True), [tok])
        else:
            mx = stat(nh)
            r = dve.op(lambda e: e.tensor_reduce(mx, s3, AX, ALU.max), [tok])
            r = dve.op(lambda e: e.tensor_tensor(mx, mx, sink, ALU.max), [r, tsm])
            r = dve.op(lambda e: e.tensor_scalar(nm, mx, -1.0, None, ALU.mult), [r])
        for i in range(nh):
            r2 = act.op(lambda e, i=i: e.activation(s3[:, i, :], s3[:, i, :], ACT.Exp, bias=nm[:, i:i + 1],
                                                    accum_out=sm[:, i:i + 1]), [r])
        if sink is not None:
            es = stat(nh)
            r = dve.op(lambda e: e.tensor_tensor(es, sink, nm, ALU.add), [r])
            r = act.op(lambda e: e.activation(es, es, ACT.Exp), [r])
            r2 = dve.op(lambda e: e.tensor_tensor(sm, sm, es, ALU.add), [r, r2])
        return r2, sm

    def p_transposed(s, nh, nkt, tok):
        b = nextbank()
        fb = b.take()
        n = nh * nkt
        for i in range(n):
            r = pe.op(lambda e, i=i: e.transpose(b.ap[:, i * P:(i + 1) * P], s.ap[:, i * P:(i + 1) * P], ident),
                      [tok] + fb, inc=(i == n - 1))
        s.put(r)
        pt = pT_rot.next()
        r = evac(pt.ap[:, 0:n * P], b.ap[:, 0:n * P], [r] + pt.take())
        b.put(r)
        return pt, r

    def staged(work, score, finish, heads_at=None, fill=None):
        scored, turned = [], []
        fill = fill or fill_next

        def turn():
            item, (s, r) = scored.pop(0)
            nh = 2 if heads_at is None else len(item[heads_at])
            turned.append((item, p_transposed(s, nh, 2 if heads_at is None else item[0] + 1, r)))

        def close():
            item, (pt, r) = turned.pop(0)
            finish(*item, pt, r)
        for item in work:
            scored.append((item, score(*item)))
            fill()
            if len(scored) == 2:
                turn()
            if len(turned) == 2:
                close()
        turn()
        close()
        fill()
        close()

    def head_attention(q_at, k_at, v_at, ready_qk, ready_v, bias_at, snap, out_cols, sink=None, kfirst=None):
        work = []
        for t in range(2):
            per = 4 if t == 0 else 2
            for a in range(0, 4, per):
                for par in range(2):
                    work.append((t, [2 * (a + i) + par for i in range(per)]))
        state = {}
        otoks = [None, None]
        rsum = [stat(8), stat(8)]
        left = [8, 8]
        sumtok = [[], []]

        def score(t, heads):
            nk = P * (t + 1)
            nh = len(heads)
            b = nextbank()
            fb = b.take()
            for i, h in enumerate(heads):
                r = pe.op(lambda e, i=i, h=h: e.matmul(b.ap[:, i * nk:(i + 1) * nk], q_at(h, t), k_at(h, nk),
                                                       start=True, stop=True), list(ready_qk) + fb, inc=(i == nh - 1))
            s = S_rot.next()
            s3 = s.ap[:, 0:nh * nk].rearrange("p (h k) -> p h k", h=nh)
            bias, tbias = bias_at(heads, t)
            r = dve.op(lambda e: e.scalar_tensor_tensor(
                out=s3, in0=b.ap[:, 0:nh * nk].rearrange("p (h k) -> p h k", h=nh), scalar=0.125, in1=bias,
                op0=ALU.mult, op1=ALU.add), [r] + tbias + s.take() + snap)
            b.put(r)
            sk = None if sink is None else sink[:, heads[0]:heads[-1] + 1:2]
            r, sm = softmax_group(s, nh, nk, r, sk)
            r2 = dve.op(lambda e: e.reciprocal(rsum[t][:, heads[0]:heads[-1] + 1:2], sm), [r])
            sumtok[t].append(r2)
            return s, r

        def finish(t, heads, pt, r):
            nkt = t + 1
            fo = ob.take()
            for i, h in enumerate(heads):
                for kt in range(nkt):
                    r2 = pe.op(lambda e, i=i, h=h, kt=kt: e.matmul(
                        ob.ap[:, 64 * h:64 * h + 64], pt.ap[:, (i * nkt + kt) * P:(i * nkt + kt + 1) * P],
                        v_at(h, kt), start=(kt == 0), stop=(kt == nkt - 1)), [r] + list(ready_v) + fo,
                        inc=(i == len(heads) - 1 and kt == nkt - 1))
            pt.put(r2)
            left[t] -= len(heads)
            if left[t] == 0:
                r3 = dve.op(lambda e: e.tensor_tensor(
                    O[:, t, out_cols:out_cols + 512].rearrange("p (h d) -> p h d", h=8),
                    ob.ap[:, :].rearrange("p (h d) -> p h d", h=8),
                    rsum[t].unsqueeze(2).to_broadcast([P, 8, 64]), ALU.mult), [r2] + sumtok[t] + ofree)
                ob.put(r3)
                otoks[t] = r3

        ofree = xnb.take()
        xnb.put(*ofree)
        staged(work, score, finish, 1)
        return otoks

    def transpose_out(src_cols, k0, toks, oT_free):
        out = []
        for g in range(2):
            b = nextbank()
            fb = b.take()
            for i in range(2):
                for t in range(2):
                    c = src_cols + (2 * g + i) * P
                    r = pe.op(lambda e, i=i, t=t, c=c, b=b: e.transpose(
                        b.ap[:, (2 * i + t) * P:(2 * i + t + 1) * P], O[:, t, c:c + P], ident),
                        [toks[t]] + fb, inc=(i == 1 and t == 1))
            hi, lo = flat(oT, k0 + 2 * g, 2)
            r2 = halves(hi, lo, b.ap[:, :], [r], oT_free)
            b.put(r2)
            out.append(r2)
        xnb.put(r)
        return out

    tg = {}
    made = {}
    b0 = nextbank()
    r = pe.op(lambda e: e.transpose(b0.ap[:, 0:124], rows[:, :], cst[0:124, 0:124]), [tcst, trow])
    tgc = dve.op(lambda e: e.tensor_copy(gcol[:, :], b0.ap[:, 0:124]), [r])
    b0.put(tgc)

    def trig_prep():
        r = dve.op(lambda e: e.tensor_copy(posf[:, :], posr[:, :]), [tsm])
        r0 = dve.op(lambda e: e.tensor_copy(ssr[:, 2, :].rearrange("p (a n) -> p a n", a=2),
                                            lsr[:, :].unsqueeze(2).to_broadcast([16, 2, 64])), [tsm])
        b = nextbank()
        fb = b.take()
        pe.op(lambda e: e.transpose(b.ap[:, 0:2], posf[:, :], cst[0:2, 0:2]), [r, tcst] + fb, inc=False)
        for i in range(3):
            r = pe.op(lambda e, i=i: e.transpose(b.ap[:, 16 + 16 * i:32 + 16 * i], ssr[:, i, :], cst[0:16, 0:16]),
                      [r0], inc=(i == 2))
        ang = stat(32)
        raw = stat(64)
        dve.op(lambda e: e.tensor_copy(raw[:, 0:2], b.ap[:, 0:2]), [r])
        r = dve.op(lambda e: e.tensor_copy(raw[:, 16:64], b.ap[:, 16:64]), [r])
        b.put(r)
        yield
        rdt = act.op(lambda e: e.activation(SM[:, 0, :], raw[:, 48:64], ACT.Exp), [r])
        lr, li = raw[:, 16:32], raw[:, 32:48]
        for t in range(2):
            r = dve.op(lambda e, t=t: e.tensor_scalar(ang[:, 8 * t:8 * t + 8], inv8, raw[:, t:t + 1], None, ALU.mult),
                       [r])
        r = dve.op(lambda e: e.tensor_tensor(ang[:, 16:32], li, SM[:, 0, :], ALU.mult), [r, rdt])
        k, kh, kl, pk = stat(32), stat(32), stat(32), pieces_of_two_pi()
        r = dve.op(lambda e: e.tensor_scalar(k, ang, 1.0 / TWO_PI, MAGIC, ALU.mult, ALU.add), [r])
        r = dve.op(lambda e: e.tensor_scalar(k, k, MAGIC, None, ALU.subtract), [r])
        r = dve.op(lambda e: e.tensor_scalar(kh, k, 1.0 / 2048, MAGIC, ALU.mult, ALU.add), [r])
        r = dve.op(lambda e: e.tensor_scalar(kh, kh, MAGIC, 2048.0, ALU.subtract, ALU.mult), [r])
        r = dve.op(lambda e: e.tensor_tensor(kl, k, kh, ALU.subtract), [r])
        yield
        for kk, pp in ((kh, pk[0]), (kl, pk[0]), (kh, pk[1]), (kl, pk[1]), (kh, pk[2]), (kl, pk[2]), (k, pk[3])):
            r = dve.op(lambda e, kk=kk, pp=pp: e.scalar_tensor_tensor(out=ang, in0=kk, scalar=-pp, in1=ang,
                                                                      op0=ALU.mult, op1=ALU.add), [r])
        lim = 3.1415925
        r = dve.op(lambda e: e.tensor_scalar(ang, ang, lim, -lim, ALU.min, ALU.max), [r])
        yield
        na = stat(32)
        r2 = dve.op(lambda e: e.tensor_scalar(na, ang, -1.0, None, ALU.mult), [r])
        r2 = dve.op(lambda e: e.tensor_tensor(na, na, ang, ALU.min), [r2])
        r2 = dve.op(lambda e: e.tensor_scalar(na, na, math.pi / 2, None, ALU.add), [r2])
        sn, cs = stat(32), stat(32)
        r1 = act.op(lambda e: e.activation(sn, ang, ACT.Sin), [r])
        r2 = act.op(lambda e: e.activation(cs, na, ACT.Sin), [r2])
        r = dve.op(lambda e: e.tensor_copy(rope[:, 0, :, :].rearrange("p a b -> p (a b)"), cs[:, 0:16]), [r2])
        tro = dve.op(lambda e: e.tensor_copy(rope[:, 1, :, :].rearrange("p a b -> p (a b)"), sn[:, 0:16]), [r1])
        tg["rope"] = tro
        yield
        dve.op(lambda e: e.tensor_copy(SM[:, 2, :], cs[:, 16:32]))
        dve.op(lambda e: e.tensor_copy(SM[:, 3, :], sn[:, 16:32]))
        w = [stat(16) for _ in range(6)]
        r = dve.op(lambda e: e.tensor_tensor(w[0], lr, SM[:, 0, :], ALU.mult), [rdt])
        rm = act.op(lambda e: e.activation(SM[:, 1, :], w[0], ACT.Exp), [r])

        def tt(o, a, b_, op, after):
            return dve.op(lambda e: e.tensor_tensor(o, a, b_, op), after)
        r = tt(w[0], SM[:, 1, :], SM[:, 2, :], ALU.mult, [rm, dve.last()])
        r = dve.op(lambda e: e.tensor_scalar(w[0], w[0], -1.0, None, ALU.add), [r])
        tt(w[1], SM[:, 1, :], SM[:, 3, :], ALU.mult, [])
        tt(w[2], lr, lr, ALU.mult, [])
        r = tt(w[3], li, li, ALU.mult, [])
        r = tt(w[2], w[2], w[3], ALU.add, [r])
        rd = dve.op(lambda e: e.reciprocal(w[2], w[2]), [r])
        yield
        r = tt(w[3], w[0], lr, ALU.mult, [rd])
        r = tt(w[4], w[1], li, ALU.mult, [])
        r = tt(w[3], w[3], w[4], ALU.add, [r])
        r = tt(SM[:, 4, :], w[3], w[2], ALU.mult, [r])
        r = tt(w[4], w[1], lr, ALU.mult, [r])
        r = tt(w[5], w[0], li, ALU.mult, [])
        r = tt(w[4], w[4], w[5], ALU.subtract, [r])
        tf = tt(SM[:, 5, :], w[4], w[2], ALU.mult, [r])
        tg["sm"] = tf
        yield
        made["in"] = input_matrices()

    def input_matrices():
        tf = tg["sm"]

        def tt(o, a, b_, op, after):
            return dve.op(lambda e: e.tensor_tensor(o, a, b_, op), after)
        fre = SM[:, 4, :].unsqueeze(2).to_broadcast([P, 16, 32])
        fim = SM[:, 5, :].unsqueeze(2).to_broadcast([P, 16, 32])
        tA, tB, tC, tD = (R2[:, 1024 + 512 * i:1536 + 512 * i].rearrange("p (j h) -> p j h", h=32) for i in range(4))
        tt(tA, BL[:, 0, :, :], fre, ALU.mult, [tf, tbl])
        tt(tB, BL[:, 1, :, :], fim, ALU.mult, [])
        tt(tC, BL[:, 1, :, :], fre, ALU.mult, [])
        r = tt(tD, BL[:, 0, :, :], fim, ALU.mult, [])
        tt(BL[:, 0, :, :], tA, tB, ALU.subtract, [r])
        return tt(BL[:, 1, :, :], tC, tD, ALU.add, [r])

    def input_turn(r):
        for ri in range(2):
            b = nextbank()
            fb = b.take()
            for J in range(4):
                r2 = pe.op(lambda e, b=b, ri=ri, J=J: e.transpose(
                    b.ap[:, J * P:(J + 1) * P], BL[:, ri, 4 * J:4 * J + 4, :].rearrange("p j h -> p (j h)"), ident),
                    [r] + fb, inc=(J == 3))
            tbt = dve.op(lambda e, b=b, ri=ri: e.tensor_copy(BT[:, ri, :, :].rearrange("p J c -> p (J c)"), b.ap[:, :]),
                         [r2])
            b.put(tbt)
        tg["bt"] = tbt
        xkv.put(tbt)

    pqb = [Buf(p) for p in pq]
    ptab = {}
    spilled = {}

    def phase_table(J):
        t = pq0[J % 2]
        r = [pool.op(lambda e: e.tensor_copy(t[:, ri, :, 0:1], SM[:, 2 + ri, 4 * J:4 * J + 4].unsqueeze(2)),
                     [tg["sm"], spilled.get(J - 2)]) for ri in range(2)]
        n = 1
        while n < 256:
            c, s = t[:, 0, :, 0:n], t[:, 1, :, 0:n]
            cw = t[:, 0, :, n - 1:n].to_broadcast([P, 4, n])
            sw = t[:, 1, :, n - 1:n].to_broadcast([P, 4, n])
            u1, u2 = tabs[:, 0, :, 0:n], tabs[:, 1, :, 0:n]
            for out, (a, b_), op in ((0, (cw, sw), ALU.subtract), (1, (sw, cw), ALU.add)):
                ra = pool.op(lambda e: e.tensor_tensor(u1, c, a, ALU.mult), r)
                rb = pool.op(lambda e: e.tensor_tensor(u2, s, b_, ALU.mult), r)
                ro = pool.op(lambda e: e.tensor_tensor(t[:, out, :, n:2 * n], u1, u2, op), [ra, rb])
                r = [ro]
            n *= 2
        spilled[J] = dma(pool, spill[J], early[J % 2].rearrange("p k t -> p (k t)"), f"spill{J}", [ro])

    def load_table(J):
        src = spill[J].rearrange("p (r n) -> p r n", r=2)
        dst = M[:, :, :] if J % 2 == 0 else kT.rearrange("p (r j) n -> p r (j n)", r=2)
        ptab[J] = dma(pool, dst, src, f"tab{J % 2}", pqb[J % 2].take() + [spilled[J]])

    def mem_load():
        fr = xnb.take()
        tm = [dma(pool, M[:, t, :], v("mem").rearrange("b (t p) d -> t p (b d)", p=P)[t], "mem", fr + mfree[:])
              for t in range(2)]
        xnb.put(*fr)
        return [[tm[-1]] * 2] * 2

    mfree = []
    mTb = Buf(mT)
    xkv = Buf(None)

    def cross_kv_fillers(l):
        W = ("x_w_kv", l)
        out = {"k": [], "v": []}
        xkfree = xkv.take()

        def chunk(c):
            def start():
                pair, done = gemm(both(mT), 8, W, [(512 * c, 512)], mready[:])
                if c == 3:
                    mTb.put(pe.last())

                def consume():
                    if c < 2:
                        chains.append(head_prep(pair, done, 2, 256, xkT, 4 * c, xgain(l, 1), out["k"], dstfree=xkfree))
                    else:
                        for t in range(2):
                            r = evac(xv[:, t, 512 * (c - 2):512 * (c - 1)], pair[t].ap[:, :], [done[t]] + xkfree)
                            pair[t].put(r)
                            out["v"].append(r)
                return consume
            return start

        fillers.extend([chunk(c) for c in range(4)])
        return out

    def xgain(l, i):
        return [gcol[:, 112 + 4 * l + 2 * i + n:113 + 4 * l + 2 * i + n] for n in range(2)]

    def cross_attention(xready, l, kvout):
        hr, rstd_x, rtok = norm_later(xready, (5 * l + 2) * 8, hTb)
        snap = snapshot()
        drain_fill()
        qr = [[], []]
        for c in range(2):
            pair, done = gemm(both(hT), 8, ("x_w_q", l), [(512 * c, 512)], hr)
            flush()
            chains.append(head_prep(pair, done, 2, 256, qT, 4 * c, xgain(l, 0), qr[c], dstfree=snap,
                                    rowscale=(rstd_x, rtok)))
        hTb.put(pe.last())
        rs = [stat(4), stat(4)]
        otok = {}
        stoks = {}
        ofree = xnb.take()
        xnb.put(*ofree)

        def score(t, hp):
            if (t, hp) == (0, 1):
                flush()
            ready = qr[hp] + kvout["k"]
            b = nextbank()
            fb = b.take()
            for i in range(2):
                h = 2 * hp + i
                for c in range(2):
                    r = pe.op(lambda e, i=i, h=h, c=c: e.matmul(
                        b.ap[:, 256 * i:256 * i + 256], qT[:, 2 * h + c, t * P:(t + 1) * P], xkT[:, 2 * h + c, :],
                        start=(c == 0), stop=(c == 1)), ready + fb, inc=(i == 1 and c == 1))
            s = S_rot.next()
            r = act.op(lambda e: e.activation(s.ap, b.ap[:, :], ACT.Copy, scale=0.0625), [r] + s.take() + snap)
            b.put(r)
            r, sm = softmax_group(s, 2, 256, r)
            stoks[(t, hp)] = dve.op(lambda e: e.reciprocal(rs[t][:, 2 * hp:2 * hp + 2], sm), [r])
            return s, r

        def finish(t, hp, pt, r):
            fo = ob.take()
            for i in range(2):
                h = 2 * hp + i
                for kt in range(2):
                    r2 = pe.op(lambda e, i=i, h=h, kt=kt: e.matmul(
                        ob.ap[:, 256 * i:256 * i + 256], pt.ap[:, (2 * i + kt) * P:(2 * i + kt + 1) * P],
                        xv[:, kt, 256 * h:256 * h + 256], start=(kt == 0), stop=(kt == 1)), [r] + kvout["v"] + fo,
                        inc=(i == 1 and kt == 1))
            pt.put(r2)
            r3 = dve.op(lambda e: e.tensor_tensor(
                O[:, t, 512 * hp:512 * hp + 512].rearrange("p (h d) -> p h d", h=2),
                ob.ap[:, :].rearrange("p (h d) -> p h d", h=2),
                rs[t][:, 2 * hp:2 * hp + 2].unsqueeze(2).to_broadcast([P, 2, 256]), ALU.mult),
                [r2, stoks[(t, hp)]] + ofree)
            ob.put(r3)
            otok[(t, hp)] = r3

        outr = []
        oTf = oTb.take()
        staged([(t, hp) for hp in range(2) for t in range(2)], score, finish, None, step_chains)
        for hp in range(2):
            outr += transpose_out(512 * hp, 4 * hp, [otok[(0, hp)], otok[(1, hp)]], oTf)
        xkv.put(pe.last())
        toks, pl = project_x(both(oT), 8, ("x_w_o", l), outr, 1.0)
        oTb.put(pl)
        return toks

    def even_mixer(xready):
        hr = norm_T(x, xready, 8, hTb)
        snap = snapshot() + R1free
        W = ("even_w_in", 0)
        lhs = both(hT)
        qr, vr = [], []

        def chunk_qk(c0, gi, dst, rope_on, acc):
            pair, done = gemm(lhs, 8, W, [(c0, 512)], hr)
            return lambda: chains.append(head_prep(
                pair, done, 8, 64, dst, 0, [] if rope_on else [gcol[:, 120 + gi:121 + gi]], acc,
                evg[:, gi, :] if rope_on else None, snap))
        b = nextbank()
        fb = b.take()
        for k0 in range(0, 8, 4):
            hi, lo, tok, j = piece(W[0], W[1], k0, 4, [(1536, 8)])
            for kk in range(4):
                r = products(b.ap[0:8, 0:256], (hi[:, kk, :], lo[:, kk, :]), tuple(a[:, k0 + kk, :] for a in hT),
                             k0 + kk == 0, k0 + kk == 7, tok + fb + [hr[k0 + kk]], kk == 3)
            release(j, r)
        z, na = (M[0:8, 1, 512 + 256 * i:768 + 256 * i] for i in range(2))
        r = dve.op(lambda e: e.tensor_scalar(z, b.ap[0:8, 0:256], fbias[:, :], None, ALU.add), [r, tsm] + mem_read)
        b.put(r)
        r = dve.op(lambda e: e.scalar_tensor_tensor(out=na, in0=z, scalar=-1.0, in1=z, op0=ALU.mult, op1=ALU.min), [r])
        rm = dve.op(lambda e: e.tensor_scalar(z, z, 0.0, None, ALU.min), [r])
        r = act.op(lambda e: e.activation(na, na, ACT.Exp), [r])
        r = act.op(lambda e: e.activation(na, na, ACT.Ln, bias=1.0), [r])
        r = dve.op(lambda e: e.tensor_tensor(z, z, na, ALU.subtract), [r, rm])
        r = dve.op(lambda e: e.tensor_tensor_scan(cumT[:, 0, :], cst[0:8, 256:257].to_broadcast([8, 256]), z, 0.0,
                                                  ALU.mult, ALU.add), [r])
        r1 = dve.op(lambda e: e.tensor_scalar(cumT[:, 1, :], cumT[:, 0, :], -1.0, None, ALU.mult), [r])

        def logf_sums():
            tb_ = []
            for t in range(2):
                nk = P * (t + 1)
                per = 512 // nk
                for h0 in range(0, 8, per):
                    b = nextbank()
                    fb = b.take()
                    for i in range(per):
                        h = h0 + i
                        pe.op(lambda e, b=b, i=i, h=h, nk=nk: e.matmul(
                            b.ap[:, i * nk:(i + 1) * nk], sel(h, P), cumT[:, 1, 0:nk], start=True, stop=False),
                            [r1] + fb, inc=False)
                        r = pe.op(lambda e, b=b, i=i, h=h, nk=nk, t=t: e.matmul(
                            b.ap[:, i * nk:(i + 1) * nk], cumT[:, 0, t * P:(t + 1) * P], sel(h, nk),
                            start=False, stop=True), inc=(i == per - 1))
                    dstb = biasA[:, h0:h0 + per, :] if t else biasB[:, h0:h0 + per, 0:P]
                    r = dve.op(lambda e, b=b, dstb=dstb, nk=nk, per=per: e.tensor_tensor(
                        dstb, b.ap[:, 0:per * nk].rearrange("p (h k) -> p h k", h=per),
                        maskc[:, 256 - nk:256].unsqueeze(1).to_broadcast([P, per, nk]), ALU.add), [r] + snap)
                    b.put(r)
                    tb_.append(r)
            return tb_
        chunk_qk(0, 0, qT, False, qr)()
        add = chunk_qk(512, 1, kT, False, qr)
        flush()
        add()
        pair, done = gemm(lhs, 8, W, [(1024, 512)], hr)
        flush()
        for t in range(2):
            r = evac(vsb[:, t, :], pair[t].ap[:, :], [done[t]] + vfree.take())
            pair[t].put(r)
            vr.append(r)
        tbias = logf_sums()
        R = {}

        def f_qk(c0, gi, dst, name):
            def start():
                R[name] = []
                return chunk_qk(c0, gi, dst, True, R[name])
            return start

        def f_v():
            pair, done = gemm(lhs, 8, W, [(2568, 512)], hr)
            hTb.put(pe.last())

            def consume():
                R["v"] = [evac(M[:, t, 0:512], pair[t].ap[:, :], [done[t]] + mem_read) for t in range(2)]
                for t in range(2):
                    pair[t].put(R["v"][t])
            return consume
        bq = qT[:, 4:8, :]
        bk = kT[:, 4:8, :]
        fillers.extend([f_qk(1544, 2, bq, "q"), f_qk(2056, 3, bk, "k"), f_v])
        kvout = cross_kv_fillers(0)
        q_at = lambda h, t: qT[64 * (h % 2):64 * (h % 2) + 64, h // 2, t * P:(t + 1) * P]
        k_at = lambda h, nk: kT[64 * (h % 2):64 * (h % 2) + 64, h // 2, 0:nk]

        def bias_at(heads, t):
            hs = slice(heads[0], heads[-1] + 1, 2)
            return (biasA[:, hs, :] if t else biasB[:, hs, 0:P]), tbias
        ot = head_attention(q_at, k_at, lambda h, kt: vsb[:, kt, 64 * h:64 * h + 64], qr, vr, bias_at, snap, 0)
        flush()
        rb = R["q"] + R["k"]
        oTf = oTb.take()
        outr = transpose_out(0, 0, ot, oTf)
        lw = stat(128)
        l2 = stat(2)
        r = dve.op(lambda e: e.tensor_tensor(lw.rearrange("p (a n) -> p a n", a=2), lamp[:, 0:4:2, :], lamp[:, 1:4:2, :],
                                             ALU.mult), [tsm])
        r = dve.op(lambda e: e.tensor_reduce(l2, lw.rearrange("p (a n) -> p a n", a=2), AX, ALU.add), [r])
        r = act.op(lambda e: e.activation(l2, l2, ACT.Exp), [r])
        lam_init = 0.8 - 0.6 * math.exp(-0.3 * 0)
        nl = stat(1)
        r = dve.op(lambda e: e.tensor_tensor(nl, l2[:, 1:2], l2[:, 0:1], ALU.subtract), [r])
        tnl = dve.op(lambda e: e.tensor_scalar(nl, nl, -lam_init, None, ALU.add), [r])
        work = [(0, [0, 1, 2, 3]), (1, [0, 1]), (1, [2, 3])]
        fin = []

        def score(t, heads):
            nk, nh = P * (t + 1), len(heads)
            got = []
            for j in range(2):
                b = nextbank()
                fb = b.take()
                for i, h in enumerate(heads):
                    r = pe.op(lambda e, i=i, h=h, j=j, b=b: e.matmul(
                        b.ap[:, i * nk:(i + 1) * nk], bq[64 * j:64 * j + 64, h, t * P:(t + 1) * P],
                        bk[64 * j:64 * j + 64, h, 0:nk], start=True, stop=True), rb + fb, inc=(i == nh - 1))
                s = S_rot.next()
                s3 = s.ap[:, 0:nh * nk].rearrange("p (h k) -> p h k", h=nh)
                r = dve.op(lambda e, b=b, s3=s3: e.scalar_tensor_tensor(
                    out=s3, in0=b.ap[:, 0:nh * nk].rearrange("p (h k) -> p h k", h=nh), scalar=0.125,
                    in1=maskb[:, 256 - nk:256].unsqueeze(1).to_broadcast([P, nh, nk]), op0=ALU.mult, op1=ALU.add),
                    [r] + s.take())
                b.put(r)
                r, sm = softmax_group(s, nh, nk, r)
                got.append((s, s3, r, sm))
            rr = []
            for j in range(2):
                s, s3, r, sm = got[j]
                rc = stat(nh)
                r = dve.op(lambda e, rc=rc, sm=sm: e.reciprocal(rc, sm), [r])
                if j:
                    r = dve.op(lambda e, rc=rc: e.tensor_scalar(rc, rc, nl, None, ALU.mult), [r, tnl])
                r = dve.op(lambda e, s3=s3, rc=rc: e.tensor_tensor(
                    s3, s3, rc.unsqueeze(2).to_broadcast([P, nh, nk]), ALU.mult), [r])
                rr.append(r)
            s = got[0][0]
            r = pool.op(lambda e: e.tensor_tensor(s.ap, s.ap, got[1][0].ap, ALU.add), rr)
            got[1][0].put(r)
            return s, r

        def finish(t, heads, pt, r):
            nkt = t + 1
            fo = ob.take()
            for i, h in enumerate(heads):
                for kt in range(nkt):
                    r2 = pe.op(lambda e, i=i, h=h, kt=kt: e.matmul(
                        ob.ap[:, P * h:P * h + P], pt.ap[:, (i * nkt + kt) * P:(i * nkt + kt + 1) * P],
                        M[:, kt, P * h:P * h + P], start=(kt == 0), stop=(kt == nkt - 1)), [r] + R["v"] + fo,
                        inc=(i == len(heads) - 1 and kt == nkt - 1))
            pt.put(r2)
            if heads[-1] != 3:
                return
            sq = sqj_rot.next()
            r = act.op(lambda e: e.activation(sq.ap[:, 0:512], ob.ap[:, :], ACT.Square), [r2] + sq.take())
            ss = stat(4)
            r = dve.op(lambda e: e.tensor_reduce(ss, sq.ap[:, 0:512].rearrange("p (h d) -> p h d", h=4), AX, ALU.add),
                       [r])
            sq.put(r)
            rs, r = rstd(ss, 4, 128, [r])
            o3 = O[:, t, 512:1024].rearrange("p (h d) -> p h d", h=4)
            r = dve.op(lambda e: e.tensor_tensor(o3, ob.ap[:, :].rearrange("p (h d) -> p h d", h=4),
                                                 rs.unsqueeze(2).to_broadcast([P, 4, P]), ALU.mult), [r])
            ob.put(r)
            r = dve.op(lambda e: e.tensor_tensor(o3, o3, sublng[:, :].unsqueeze(1).to_broadcast([P, 4, P]), ALU.mult),
                       [r, tsm])
            r = dve.op(lambda e: e.tensor_scalar(O[:, t, 512:1024], O[:, t, 512:1024], 1.0 - lam_init, None, ALU.mult),
                       [r])
            fin.append(r)
        staged(work, score, finish, 1)
        outr += transpose_out(512, 4, fin, oTf)
        vfree.put(pe.last())
        drain_fill()
        toks, pl = project_x(both(oT), 8, ("even_w_out", 0), outr, 1.0)
        oTb.put(pl)
        mfree.append(pl)
        return toks, kvout

    vfree = Buf(None)
    mem_read = []

    def odd_mixer(xready):
        hr = norm_T(x, xready, (5 + 1) * 8, hTb)
        snap = snapshot()
        W = ("odd_w_in", 0)
        lhs = both(hT)
        rel = v("rel")
        tb0 = dma(pool, biasB[:, :, :], bass.AP(rel.tensor, rel.offset, [[1, P], [512, 8], [1, 256]]), "rel", snap)
        tbias = []

        def rel_bias():
            for g in range(4):
                b = nextbank()
                r = pe.op(lambda e, b=b, g=g: e.matmul(
                    b.ap[:, :], flip, biasB[:, 2 * g:2 * g + 2, :].rearrange("p h k -> p (h k)"), start=True, stop=True),
                    [tb0] + b.take())
                r = dve.op(lambda e, b=b, g=g: e.tensor_tensor(
                    biasA[:, 2 * g:2 * g + 2, :], b.ap[:, :].rearrange("p (h k) -> p h k", h=2),
                    maskb.unsqueeze(1).to_broadcast([P, 2, 256]), ALU.add), [r] + snap)
                b.put(r)
                tbias.append(r)
        qr, vr = [], []
        for n, (c0, dst) in enumerate(((1536, qT), (2048, kT))):
            pair, done = gemm(lhs, 8, W, [(c0, 512)], hr)
            flush()
            chains.append(head_prep(pair, done, 8, 64, dst, 0, [gcol[:, 122 + n:123 + n]], qr, dstfree=snap))
        pair, done = gemm(lhs, 8, W, [(2560, 512)], hr)
        flush()
        fv = vfree.take()
        for t in range(2):
            r = evac(vsb[:, t, :], pair[t].ap[:, :], [done[t]] + fv)
            pair[t].put(r)
            vr.append(r)
        rel_bias()
        tflip = pe.last()
        R = {}
        uc = biasB

        def f_conv(which, c0):
            def start():
                pair, done = gemm_T(lambda kt: tuple(a[:, kt, :] for a in hT), 8, W, [(c0, 512)], hr)
                if which == "b":
                    hTb.put(pe.last())

                def consume():
                    if which == "c":
                        R["c"] = [evac(uc[:, 2 * m:2 * m + 2, :].rearrange("p a b -> p (a b)"), pair[m].ap[:, :],
                                       [done[m], tflip] + snap) for m in range(2)]
                        for m in range(2):
                            pair[m].put(R["c"][m])
                    elif which == "h":
                        R["u"] = []
                        for m in range(2):
                            o = uc[:, 2 * m:2 * m + 2, :].rearrange("p a b -> p (a b)")
                            r = dve.op(lambda e, o=o, m=m: e.tensor_tensor(o, o, pair[m].ap[:, :], ALU.mult),
                                       [done[m], R["c"][m]])
                            pair[m].put(r)
                            R["u"].append(r)
                        R["y"] = []
                        for k in range(4):
                            u, y = uc[:, k, :], uc[:, 4 + k, :]
                            w = [gcol[:, 96 + 4 * i + k:97 + 4 * i + k] for i in range(3)]
                            r = dve.op(lambda e, u=u, y=y, w=w: e.tensor_scalar(y, u, w[2], None, ALU.mult),
                                       [R["u"][k // 2]] + snap)
                            r = dve.op(lambda e, u=u, y=y, w=w: e.scalar_tensor_tensor(
                                out=y[:, 1:256], in0=u[:, 0:255], scalar=w[1], in1=y[:, 1:256], op0=ALU.mult,
                                op1=ALU.add), [r])
                            r = dve.op(lambda e, u=u, y=y, w=w: e.scalar_tensor_tensor(
                                out=y[:, 2:256], in0=u[:, 0:254], scalar=w[0], in1=y[:, 2:256], op0=ALU.mult,
                                op1=ALU.add), [r])
                            R["y"].append(r)
                    else:
                        R["o"] = []
                        for m in range(2):
                            o = uc[:, 4 + 2 * m:6 + 2 * m, :].rearrange("p a b -> p (a b)")
                            r = dve.op(lambda e: e.tensor_tensor(o, o, pair[m].ap[:, :], ALU.mult),
                                       [done[m], R["y"][2 * m], R["y"][2 * m + 1]])
                            pair[m].put(r)
                            hi, lo = flat(oT, 2 * m, 2)
                            R["o"].append(halves(hi, lo, o, [r], oTf))
                return consume
            return start
        oTf = oTb.take()
        fillers.extend([f_conv("c", 512), f_conv("h", 1024), f_conv("b", 0)])
        kvout = cross_kv_fillers(1)
        q_at = lambda h, t: qT[64 * (h % 2):64 * (h % 2) + 64, h // 2, t * P:(t + 1) * P]
        k_at = lambda h, nk: kT[64 * (h % 2):64 * (h % 2) + 64, h // 2, 0:nk]

        def bias_at(heads, t):
            return biasA[:, heads[0]:heads[-1] + 1:2, 256 - P * (t + 1):256], tbias
        ot = head_attention(q_at, k_at, lambda h, kt: vsb[:, kt, 64 * h:64 * h + 64], qr, vr, bias_at, snap, 512)
        outr = transpose_out(512, 4, ot, oTf)
        vfree.put(pe.last())
        drain_fill()
        outr = R["o"] + outr
        toks, pl = project_x(both(oT), 8, ("odd_w_out", 0), outr, 1.0)
        oTb.put(pl)
        return toks, kvout

    def second_mixer(xready):
        hr = norm_T(x, xready, 80, hTb)
        snap = snapshot()
        W = ("w_in_2", 0)
        lhs = both(hT)
        rhs = lambda kt: tuple(a[:, kt, :] for a in hT)
        tal = [dma(pool, (biasA, biasB)[i][:, :, :], v("alibi")[i], f"al{i}", snap) for i in range(2)]
        tzc = [pool.op(lambda e: e.memset(CL[ri], 0.0), snap) for ri in range(2)][-1]
        for ri, nm in enumerate(("c_re_2", "c_im_2")):
            src = v(nm).rearrange("l (J g) h p -> g h (l J) p", g=8)
            for g in range(8):
                tcl = dma(pool, CL[ri][16 * g:16 * g + 16, :, 64 * (g % 2):64 * (g % 2) + 64], src[g], "cl", [tzc])
        pqb[0].put(*snap)
        load_table(0)

        def queries(c0, dst):
            pair, done = gemm_T(rhs, 8, W, [(c0, 512)], hr)
            out = []
            for m in range(2):
                r = evac(dst[:, 2 * m:2 * m + 2, :].rearrange("p a b -> p (a b)"), pair[m].ap[:, :], [done[m]] + snap)
                pair[m].put(r)
                out.append(r)
            return out

        def keys(c0, dst, vdst, name):
            pair = nextpair()
            first = hr + pair[0].take() + pair[1].take()
            for k0 in range(0, 8, per_piece(256)):
                hi, lo, tok, j = piece(W[0], W[1], k0, per_piece(256), [(c0, 256)])
                for kk in range(per_piece(256)):
                    kt = k0 + kk
                    r0 = products(pair[0].ap[:, 0:256], (hi[:, kk, 0:P], lo[:, kk, 0:P]), rhs(kt), kt == 0, kt == 7,
                                  tok + first, kt == 7)
                    first = []
                    for t in range(2):
                        r1 = products(pair[1].ap[:, P * t:P * t + P], lhs(kt, t), (hi[:, kk, P:256], lo[:, kk, P:256]),
                                      kt == 0 and t == 0, kt == 7, [], t == 1 and (kt == 7 or kk == per_piece(256) - 1),
                                      True)
                release(j, r1)
            ra = evac(dst[:, 0, :], pair[0].ap[:, 0:256], [r0] + snap)
            pair[0].put(ra)
            rb_ = evac(vdst, pair[1].ap[:, 0:256].rearrange("p (t n) -> p t n", t=2), [r1] + snap)
            pair[1].put(rb_)
            rs = [dma(pool, dst[64 * (1 - a):64 * (1 - a) + 64, 1, :], dst[64 * a:64 * a + 64, 0, :], name, [ra] + snap)
                  for a in range(2)]
            return [ra, rs[-1]], rb_
        qa, qm = qT[:, 0:4, :], qT[:, 4:8, :]
        ka, km = kT[:, 0:2, :], kT[:, 2:4, :]
        va, vm = (kT[:, 4 + i, :].rearrange("p (t n) -> p t n", t=2) for i in range(2))
        rqa = queries(0, qa)
        rka, rva = keys(512, ka, va, "ka")
        rqm = queries(1280, qm)
        rkm, rvm = keys(1792, km, vm, "km")
        pair, done = gemm_T(rhs, 8, W, [(768, 512)], hr)
        fv = vfree.take()
        ru = []
        for m in range(2):
            r = evac(uT[:, 2 * m:2 * m + 2, :].rearrange("p a b -> p (a b)"), pair[m].ap[:, :], [done[m]] + fv)
            pair[m].put(r)
            ru.append(r)
        gt = {}

        def f_gate(c):
            for got in gemm_steps(lhs, 8, W, [(2048 + 512 * c, 512)], hr):
                if got:
                    break
                yield None
            pair, done = got
            if c == 5:
                hTb.put(pe.last())

            def consume():
                for t in range(2):
                    gsl = gates[c // 2][:, t, 512 * (c % 2):512 * (c % 2) + 512]
                    gt[(c, t)] = act.op(lambda e: e.activation(gsl, pair[t].ap[:, :], ACT.Copy),
                                        [done[t]] + snap + (xnb.free if c >= 4 else []))
                    pair[t].put(gt[(c, t)])
            yield consume
        slices.extend(f_gate(c) for c in range(4))
        mtok = {}

        def sigmoids(branch):
            for c in range(2 * branch, 2 * branch + 2):
                for t in range(2):
                    gsl = gates[branch][:, t, 512 * (c % 2):512 * (c % 2) + 512]
                    gt[(c, t)] = act.op(lambda e: e.activation(gsl, gsl, ACT.Sigmoid), [gt[(c, t)]])

        def gated(lhs_, Wo, ready, branch, c):
            for got in gemm_steps(lhs_, 4, Wo, [(512 * c, 512)], ready):
                if got:
                    break
                yield None
            pair, done = got

            def consume():
                if c == 0:
                    sigmoids(branch)
                cs = slice(512 * c, 512 * c + 512)
                for t in range(2):
                    gsl = gates[branch][:, t, cs]
                    r = dve.op(lambda e: e.tensor_tensor(gsl, gsl, pair[t].ap[:, :], ALU.mult),
                               [done[t], gt[(2 * branch + c, t)]])
                    pair[t].put(r)
                    if branch == 2:
                        r = pool.op(lambda e: e.tensor_tensor(gsl, gsl, gates[0][:, t, cs], ALU.add), [r, mtok[(0, c, t)]])
                    elif branch == 1:
                        r = dve.op(lambda e: e.tensor_tensor(M[:, t, cs], gsl, gates[2][:, t, cs], ALU.add),
                                   [r, mtok[(2, c, t)]] + pqb[0].free)
                    mtok[(branch, c, t)] = r
            yield consume

        def attend(qd, kd_, vd, rq, rv, bias, tb_, sink):
            q_at = lambda h, t: qd[64 * (h % 2):64 * (h % 2) + 64, h // 2, t * P:(t + 1) * P]
            k_at = lambda h, nk: kd_[64 * (h % 2):64 * (h % 2) + 64, int(h // 4 != h % 2), 0:nk]
            return head_attention(q_at, k_at, lambda h, kt: vd[:, kt, 64 * (h // 4):64 * (h // 4) + 64], rq, [rv],
                                  lambda heads, t: (bias[:, heads[0]:heads[-1] + 1:2, 256 - P * (t + 1):256], [tb_]),
                                  snap, 0, sink)
        ot = attend(qa, ka, va, rqa + rka, rva, biasA, tal[0], sinkb)
        oTf = oTb.take()
        outa = transpose_out(0, 0, ot, oTf)
        tzr = pool.op(lambda e: e.memset(CR, 0.0), [ot, pe.last()])
        ot = attend(qm, km, vm, rqm + rkm, rvm, biasB, tal[1], None)
        outm = transpose_out(0, 4, ot, oTf)
        slices.extend(f_gate(c) for c in (4, 5))
        slices.extend(gated(both(oT), ("w_o_swa_2", 0), outa, 0, c) for c in range(2))
        rz = []
        zin = qT[:, 0:4, :]
        snap2 = snapshot()
        pqb[1].put(*snap2)
        load_table(1)
        T_rot = Rot([R1[:, 1024 * i:1024 * i + 1024].rearrange("p (n a t) -> p n a t", n=2, a=2) for i in range(2)])
        H_rot = Rot([R1[:, 2560 + 512 * i:3072 + 512 * i].rearrange("p (a t) -> p a t", a=2) for i in range(3)])
        G = R1[:, 2048:2560].rearrange("p (a t) -> p a t", a=2)
        gb = Buf(G)
        gb.put(*snap2)
        for rot in (T_rot, H_rot):
            for b in rot.bufs:
                b.put(*snap2)
        crbuf = [Buf(CR[:, i]) for i in range(2)]
        tcr = {}

        def project_of(J):
            buf = crbuf[J % 2]
            fc = buf.take()
            b = banks[6]
            fb = b.take()
            for ri in range(2):
                r = pe.op(lambda e: e.transpose(b.ap[:, P * ri:P * ri + P], CL[ri][:, J, :], ident), [tcl] + fb,
                          inc=(ri == 1))
            for ri in range(2):
                dst = bass.AP(buf.ap.tensor, buf.ap.offset + 512 * ri, [[2048, P], [160, 4], [1, 32]])
                rc = dve.op(lambda e: e.tensor_scalar(dst, b.ap[:, P * ri:P * ri + P].rearrange("p (j c) -> p j c", j=4),
                                                      -1.0 if ri else 1.0, None, ALU.mult), [r, tzr] + fc)
            b.put(rc)
            tcr[J] = rc

        def phases(J, jj):
            tab = pqb[J % 2].ap
            return [tab[:, n, jj, :].unsqueeze(1).to_broadcast([P, 2, 256]) for n in range(2)]

        def drive(J, jj):
            b = banks[4 + jj % 2]
            fb = b.take()
            for ri in range(2):
                r = pe.op(lambda e: e.matmul(
                    b.ap[:, 256 * ri:256 * ri + 256], BT[32 * jj:32 * jj + 32, ri, J, :],
                    uT[32 * jj:32 * jj + 32, J, :], start=True, stop=True), ru + [tg["bt"]] + fb, inc=(ri == 1))
            return b, r

        def turn_back(J, jj, b, r):
            c, s = phases(J, jj)
            b3 = b.ap[:, :].rearrange("p (a t) -> p a t", a=2)
            T, X = T_rot.next(), H_rot.next()
            T1, T2 = T.ap[:, 0], T.ap[:, 1]
            dve.op(lambda e: e.tensor_tensor(T1, b3, c, ALU.mult), [r, ptab[J]] + T.take())
            r = dve.op(lambda e: e.tensor_tensor(T2, b3, s, ALU.mult))
            b.put(r)
            r1 = pool.op(lambda e: e.tensor_tensor(X.ap[:, 0, :], T1[:, 0, :], T2[:, 1, :], ALU.add), [r] + X.take())
            r2 = pool.op(lambda e: e.tensor_tensor(X.ap[:, 1, :], T1[:, 1, :], T2[:, 0, :], ALU.subtract), [r])
            return T, X, (r1, r2)

        def turn_forth(J, jj, T, X, rx):
            mg = SM[:, 1, 4 * J + jj:4 * J + jj + 1].to_broadcast([P, 256])
            fg = gb.take()
            for a in range(2):
                r = dve.op(lambda e: e.tensor_tensor_scan(G[:, a, :], mg, X.ap[:, a, :], 0.0, ALU.mult, ALU.add),
                           [rx[a]] + fg)
            c, s = phases(J, jj)
            T1, T2 = T.ap[:, 0], T.ap[:, 1]
            dve.op(lambda e: e.tensor_tensor(T1, G, c, ALU.mult), [r, rx[1]])
            r = dve.op(lambda e: e.tensor_tensor(T2, G, s, ALU.mult), [r])
            pqb[J % 2].put(r)
            gb.put(r)
            if jj == 3 and J + 2 < 4:
                load_table(J + 2)
            r1 = pool.op(lambda e: e.tensor_tensor(X.ap[:, 0, :], T1[:, 0, :], T2[:, 1, :], ALU.subtract), [r])
            r2 = pool.op(lambda e: e.tensor_tensor(X.ap[:, 1, :], T1[:, 1, :], T2[:, 0, :], ALU.add), [r])
            T.put(r2)
            return X, [r1, r2]

        def project(J, jj, X, rh):
            fy = ob.take() if jj == 0 else []
            for ri in range(2):
                r = pe.op(lambda e: e.matmul(
                    ob.ap[:, 0:256], crbuf[J % 2].ap[:, ri, P * jj:P * jj + P], X.ap[:, ri, :],
                    start=(jj == 0 and ri == 0), stop=(jj == 3 and ri == 1)), rh + [tcr[J]] + fy, inc=(ri == 1))
            X.put(r)
            if jj < 3:
                return
            crbuf[J % 2].put(r)
            r = dve.op(lambda e: e.scalar_tensor_tensor(
                out=zin[:, J, :], in0=uT[:, J, :], scalar=gcol[:, 108 + J:109 + J], in1=ob.ap[:, 0:256], op0=ALU.mult,
                op1=ALU.add), [r] + snap2)
            ob.put(r)
            rz.append(r)
            if J + 2 < 4:
                project_of(J + 2)
        project_of(0)
        project_of(1)
        driven, back, forth = {0: drive(0, 0)}, {}, {}
        for k in range(19):
            if k >= 3:
                project(*divmod(k - 3, 4), *forth.pop(k - 3))
            if k < 16:
                back[k] = turn_back(*divmod(k, 4), *driven.pop(k))
            fill()
            if k + 1 < 16:
                driven[k + 1] = drive(*divmod(k + 1, 4))
            if 1 <= k < 17:
                forth[k - 1] = turn_forth(*divmod(k - 1, 4), *back.pop(k - 1))
        drain_fill()
        slices.extend(gated(both(oT, 4), ("w_o_moba_2", 0), outm, 2, c) for c in range(2))
        fh = hTb.take()
        rz2 = [act.op(lambda e: e.activation(zin[:, J, :], zin[:, J, :], ACT.Gelu_apprx_tanh), [rz[J]])
               for J in range(4)]
        rz2 = [halves(hT[0][:, J, :], hT[1][:, J, :], zin[:, J, :], [rz2[J]], fh) for J in range(4)]
        for _ in range(2):
            fill()
        settle()
        pairs = []
        for half in (1, 0):
            pairs.append(gemm_T(rhs, 4, ("w_glu_2", 0), [(512 * half, 512)], rz2))
        zg = kT[:, 0:4, :]
        yin = qT[:, 4:8, :]
        ry = []
        for m in range(2):
            zs = zg[:, 2 * m:2 * m + 2, :].rearrange("p a b -> p (a b)")
            ys = yin[:, 2 * m:2 * m + 2, :].rearrange("p a b -> p (a b)")
            (p2, d2), (p1, d1) = pairs
            r = act.op(lambda e, zs=zs, m=m, p2=p2: e.activation(zs, p2[m].ap[:, :], ACT.Sigmoid), [d2[m]] + snap2)
            p2[m].put(r)
            r = dve.op(lambda e, zs=zs, ys=ys, m=m, p1=p1: e.tensor_tensor(ys, zs, p1[m].ap[:, :], ALU.mult),
                       [r, d1[m]] + snap2)
            p1[m].put(r)
            hi, lo = flat(hT, 4 + 2 * m, 2)
            ry.append(halves(hi, lo, ys, [r], fh))
        drain_fill()
        slices.extend(gated(both(hT, 4), ("w_o_ssm_2", 0), ry, 1, c) for c in range(2))
        drain_fill()
        oTb.put(pe.last())
        hTb.put(pe.last())
        xnb.put([mtok[(1, c, t)] for c in range(2) for t in range(2)])
        outr = []
        fo = oTb.take()
        for c in range(2):
            for g in range(2):
                b = nextbank()
                fb = b.take()
                for i in range(2):
                    for t in range(2):
                        col = 512 * c + (2 * g + i) * P
                        r = pe.op(lambda e, i=i, t=t, col=col, b=b: e.transpose(
                            b.ap[:, (2 * i + t) * P:(2 * i + t + 1) * P], M[:, t, col:col + P], ident),
                            [mtok[(1, c, t)]] + fb, inc=(i == 1 and t == 1))
                k0 = 4 * c + 2 * g
                hi, lo = flat(oT, k0, 2)
                r2 = halves(hi, lo, b.ap[:, :], [r], fo)
                b.put(r2)
                outr.append(r2)
        toks, pl = project_x(both(oT), 8, ("w_out_2", 0), outr, 1.0)
        oTb.put(pl)
        return toks

    mready = []

    def mem_rows():
        made["rows"] = norm_rows(M, made["mem"])

    def mem_turn(l):
        mready[:] = norm_turn(made["rows"], (5 * l + 3) * 8, mTb)
        mfree.append(pe.last())

    def angles():
        chain = trig_prep()
        next(chain)
        chains.append(chain)
    made["mem"] = mem_load()
    tok = ffn(tx, 0, 0, ("ffn1_w_in", "ffn1_w_out"), 2816, True, 0.5,
              {1: angles, 3: lambda: input_turn(made["in"]), 4: mem_rows, 5: lambda: mem_turn(0)})
    for J in range(4):
        phase_table(J)
    mem_read.extend(made["rows"])
    vfree.put(pool.last())
    R1free = [spilled[2], spilled[3]]
    tok, kvout = even_mixer(tok)
    tok = cross_attention(tok, 0, kvout)
    made["mem"] = mem_load()
    tok = ffn(tok, 4 * 8, 0, ("ffn2_w_in", "ffn2_w_out"), 2816, True, 0.5, {2: mem_rows, 3: lambda: mem_turn(1)})
    tok = ffn(tok, 5 * 8, 1, ("ffn1_w_in", "ffn1_w_out"), 2816, True, 0.5)
    tok, kvout = odd_mixer(tok)
    tok = cross_attention(tok, 1, kvout)
    tok = ffn(tok, (5 + 4) * 8, 1, ("ffn2_w_in", "ffn2_w_out"), 2816, True, 0.5)
    tok = second_mixer(tok)
    tok = ffn(tok, 88, 0, ("w_ff1_2", "w_ff2_2"), 4096, False, 1.0)
    fsn = snapshot()
    tgf = dma(pool, M[:, 0, :], bc_rows(v("norm_final_2"), 1024), "gf", fsn)
    r, tr = row_rstd(x, tok)
    ends = []
    for t in range(2):
        rr = dve.op(lambda e, t=t: e.scalar_tensor_tensor(out=O[:, t, :], in0=x[:, t, :], scalar=r[:, t:t + 1],
                                                          in1=M[:, 0, :], op0=ALU.mult, op1=ALU.mult),
                    [tr[t], tgf] + fsn)
        ends.append(dma(sp, v("out").rearrange("b (t p) d -> t p (b d)", p=P)[t], O[:, t, :], f"out{t}", [rr]))
    sp.wait(ends)
    sp.wait(list(spilled.values()))
    return order


NAMES = ['x', 'mem', 'positions', 'ln_gains', 'ffn1_w_in', 'ffn1_w_out', 'ffn2_w_in', 'ffn2_w_out', 'even_w_in',
         'even_f_bias', 'even_qk_gains', 'even_lambda', 'even_subln_gain', 'even_w_out', 'odd_w_in', 'odd_conv_w',
         'odd_qk_gains', 'odd_rel_bias', 'odd_w_out', 'x_w_q', 'x_w_kv', 'x_qk_gains', 'x_w_o', 'norm_mix_2', 'w_in_2',
         'sinks_2', 'lam_re_2', 'lam_im_2', 'log_step_2', 'b_re_2', 'b_im_2', 'c_re_2', 'c_im_2', 'd_skip_2',
         'w_glu_2', 'w_o_swa_2', 'w_o_ssm_2', 'w_o_moba_2', 'w_out_2', 'norm_ffn_2', 'w_ff1_2', 'w_ff2_2',
         'norm_final_2']


def kernel(**inputs):
    import concourse.bacc as bacc
    from concourse.bass_utils import run_bass_kernel_spmd as run

    arrays = {}

    def give(name, a):
        arrays["in_" + name] = np.ascontiguousarray(a)

    for name in NAMES:
        if name == 'odd_rel_bias':
            tab = np.asarray(inputs[name])[0]
            give("rel", np.concatenate([np.repeat(tab[:, 256:257], 127, 1), tab[:, ::-1],
                                        np.repeat(tab[:, 0:1], 128, 1)], 1))
        else:
            give(name, np.asarray(inputs[name]))
    give("consts", build_consts())
    give("alibi", build_alibi())
    def program(plan):
        nc = bacc.Bacc("TRN2", target_bir_lowering=False, num_devices=1)
        D = {n[3:]: nc.dram_tensor(n, a.shape, mybir.dt.from_np(a.dtype), kind="ExternalInput").ap()
             for n, a in arrays.items()}
        D["out"] = nc.dram_tensor("out", (1, 256, 1024), F32, kind="ExternalOutput").ap()
        return nc, build(nc, D, plan)

    _, plan = program(None)
    nc, _ = program(plan)
    r = run(nc, [arrays], core_ids=[0])
    return np.asarray(r.results[0]["out"])
```
